# Optimizing a Trainium2 kernel written in Bass

```python
import jax, jax.numpy as jnp
from jax import lax
import numpy as np

D_MODEL = 1024
BATCH = 1
SEQ = 512
DEPTH = 1

HEAD_DIM = 64
ATTN_PAIRS = ((128, 1), (512, 4), (2048, 16))
ATTN_GROUPS = 3
ATTN_HEADS_PER_GROUP = 8
ATTN_BLOCK = 64
ROPE_THETA = 10000.0
RET_HEADS = 8
RET_QK_DIM = 64
RET_V_DIM = 128
RET_CHUNK = 128
MOE_GROUPS = 8
MOE_EXPERTS_PER_GROUP = 8
MOE_N_EXPERTS = MOE_GROUPS * MOE_EXPERTS_PER_GROUP
MOE_TOP_K = 2
MOE_HIDDEN = 512
MOE_BLOCK = 128
NORM_EPS = 1e-6

ATTN_W = ATTN_GROUPS * ATTN_HEADS_PER_GROUP * HEAD_DIM
ATTN_OUT_W = ATTN_HEADS_PER_GROUP * HEAD_DIM
RET_QK_W = RET_HEADS * RET_QK_DIM
RET_V_W = RET_HEADS * RET_V_DIM
IN_SPLIT_POINTS = (ATTN_W, 2 * ATTN_W, 3 * ATTN_W,
                   3 * ATTN_W + RET_QK_W, 3 * ATTN_W + 2 * RET_QK_W,
                   3 * ATTN_W + 2 * RET_QK_W + RET_V_W,
                   3 * ATTN_W + 2 * RET_QK_W + 2 * RET_V_W)
IN_W = IN_SPLIT_POINTS[-1] + 2 * D_MODEL


def rms_norm(x, w):
    xf = x.astype(jnp.float32)
    y = xf * lax.rsqrt(jnp.mean(xf * xf, axis=-1, keepdims=True) + NORM_EPS)
    return (y * w.astype(jnp.float32)).astype(x.dtype)

def rotary_tables(seq_len):
    inv_freq = 1.0 / (ROPE_THETA ** (jnp.arange(0, HEAD_DIM, 2, dtype=jnp.float32) / HEAD_DIM))
    ang = jnp.arange(seq_len, dtype=jnp.float32)[:, None] * inv_freq[None, :]
    return jnp.cos(ang), jnp.sin(ang)

def apply_rotary(t, cos, sin):
    t1, t2 = jnp.split(t.astype(jnp.float32), 2, axis=-1)
    c = cos[None, :, None, :]
    s = sin[None, :, None, :]
    return jnp.concatenate([t1 * c - t2 * s, t1 * s + t2 * c], axis=-1)

def dilated_window_attention(q, k, v, dilation, half):
    B, S, H, Dh = q.shape
    L = S // dilation
    nb = -(-L // ATTN_BLOCK)
    Lp = nb * ATTN_BLOCK
    N = B * dilation

    def strided(t):
        t = t.reshape(B, L, dilation, H, Dh).transpose(0, 2, 3, 1, 4)
        return t.reshape(N, H, L, Dh)

    qb = jnp.pad(strided(q), ((0, 0), (0, 0), (0, Lp - L), (0, 0))).reshape(N, H, nb, ATTN_BLOCK, Dh)

    def band(t):
        tp = jnp.pad(strided(t), ((0, 0), (0, 0), (ATTN_BLOCK, Lp - L + ATTN_BLOCK), (0, 0)))
        tb = tp.reshape(N, H, nb + 2, ATTN_BLOCK, Dh)
        return jnp.concatenate([tb[:, :, :-2], tb[:, :, 1:-1], tb[:, :, 2:]], axis=3)

    kw = band(k)
    vw = band(v)
    scores = jnp.einsum('nhbqd,nhbkd->nhbqk', qb, kw) * (Dh ** -0.5)
    blk = jnp.arange(nb)[:, None] * ATTN_BLOCK
    q_pos = blk + jnp.arange(ATTN_BLOCK)[None, :]
    k_pos = blk - ATTN_BLOCK + jnp.arange(3 * ATTN_BLOCK)[None, :]
    rel = k_pos[:, None, :] - q_pos[:, :, None]
    in_range = (k_pos[:, None, :] >= 0) & (k_pos[:, None, :] < L)
    valid = (jnp.abs(rel) <= half) & (in_range | (rel == 0))
    scores = jnp.where(valid[None, None], scores, -jnp.inf)
    m = jnp.max(scores, axis=-1, keepdims=True)
    p = jnp.exp(scores - m)
    denom = jnp.sum(p, axis=-1, keepdims=True)
    out = jnp.einsum('nhbqk,nhbkd->nhbqd', p, vw) / denom
    lse = (m + jnp.log(denom))[..., 0]
    out = out.reshape(N, H, Lp, Dh)[:, :, :L].reshape(B, dilation, H, L, Dh)
    out = out.transpose(0, 3, 1, 2, 4).reshape(B, S, H, Dh)
    lse = lse.reshape(N, H, Lp)[:, :, :L].reshape(B, dilation, H, L)
    lse = lse.transpose(0, 3, 1, 2).reshape(B, S, H)
    return out, lse

def retention_chunkwise(q, k, v, log_g):
    B, H, S, Dk = q.shape
    Dv = v.shape[-1]
    C = RET_CHUNK
    nc = S // C
    qc = q.reshape(B, H, nc, C, Dk)
    kc = k.reshape(B, H, nc, C, Dk)
    vc = v.reshape(B, H, nc, C, Dv)
    idx = jnp.arange(C, dtype=jnp.float32)
    rel = idx[:, None] - idx[None, :]
    decay = jnp.where(rel[None] >= 0, jnp.exp(jnp.maximum(rel[None], 0.0) * log_g[:, None, None]), 0.0)
    scores = jnp.einsum('bhnqd,bhnkd->bhnqk', qc, kc) * decay[None, :, None]
    inner = jnp.einsum('bhnqk,bhnkv->bhnqv', scores, vc)
    zeta = jnp.exp((C - 1 - idx)[None, :] * log_g[:, None])
    kv = jnp.einsum('bhnkd,bhnkv->nbhdv', kc * zeta[None, :, None, :, None], vc)
    chunk_decay = jnp.exp(C * log_g)[None, :, None, None]

    def step(state, kv_chunk):
        return chunk_decay * state + kv_chunk, state

    _, prev_states = lax.scan(step, jnp.zeros((B, H, Dk, Dv), jnp.float32), kv)
    xi = jnp.exp((idx + 1.0)[None, :] * log_g[:, None])
    cross = jnp.einsum('bhnqd,nbhdv->bhnqv', qc * xi[None, :, None, :, None], prev_states)
    return (inner + cross).reshape(B, H, S, Dv)

def hybrid_mixer(xn, w_in, b_branch_gate, ret_decay_fwd, ret_decay_bwd, ret_gn_w,
                 w_attn_branch, w_ret_branch, w_out, cos, sin):
    B, S, _ = xn.shape
    proj = jnp.einsum('bsd,de->bse', xn, w_in)
    q_a, k_a, v_a, q_r, k_r, v_r, g_r, gate_logits = jnp.split(proj, IN_SPLIT_POINTS, axis=-1)

    n_a = ATTN_GROUPS * ATTN_HEADS_PER_GROUP
    q_a = apply_rotary(q_a.reshape(B, S, n_a, HEAD_DIM), cos, sin).reshape(B, S, ATTN_GROUPS, ATTN_HEADS_PER_GROUP, HEAD_DIM)
    k_a = apply_rotary(k_a.reshape(B, S, n_a, HEAD_DIM), cos, sin).reshape(B, S, ATTN_GROUPS, ATTN_HEADS_PER_GROUP, HEAD_DIM)
    v_a = v_a.astype(jnp.float32).reshape(B, S, ATTN_GROUPS, ATTN_HEADS_PER_GROUP, HEAD_DIM)
    outs = []
    lses = []
    for g, (window, dilation) in enumerate(ATTN_PAIRS):
        o, l = dilated_window_attention(q_a[:, :, g], k_a[:, :, g], v_a[:, :, g], dilation, window // (2 * dilation))
        outs.append(o)
        lses.append(l)
    mix_w = jax.nn.softmax(jnp.stack(lses, axis=0), axis=0)
    y_att = jnp.einsum('gbsh,gbshd->bshd', mix_w, jnp.stack(outs, axis=0)).reshape(B, S, ATTN_OUT_W)

    q_r = apply_rotary(q_r.reshape(B, S, RET_HEADS, RET_QK_DIM), cos, sin).transpose(0, 2, 1, 3)
    k_r = (apply_rotary(k_r.reshape(B, S, RET_HEADS, RET_QK_DIM), cos, sin) * (RET_QK_DIM ** -0.5)).transpose(0, 2, 1, 3)
    v_r = v_r.astype(jnp.float32).reshape(B, S, RET_HEADS, RET_V_DIM).transpose(0, 2, 1, 3)
    log_g_fwd = jax.nn.log_sigmoid(ret_decay_fwd.astype(jnp.float32))
    log_g_bwd = jax.nn.log_sigmoid(ret_decay_bwd.astype(jnp.float32))
    ret_f = retention_chunkwise(q_r, k_r, v_r, log_g_fwd)
    ret_b = jnp.flip(retention_chunkwise(jnp.flip(q_r, 2), jnp.flip(k_r, 2), jnp.flip(v_r, 2), log_g_bwd), 2)
    ret = ret_f + ret_b
    mu = jnp.mean(ret, axis=-1, keepdims=True)
    var = jnp.mean(jnp.square(ret - mu), axis=-1, keepdims=True)
    ret = (ret - mu) * lax.rsqrt(var + NORM_EPS)
    ret = ret.transpose(0, 2, 1, 3).reshape(B, S, RET_V_W) * ret_gn_w.astype(jnp.float32)
    y_ret = jax.nn.silu(g_r.astype(jnp.float32)) * ret

    gates = jax.nn.sigmoid((gate_logits + b_branch_gate).astype(jnp.float32))
    g_att, g_ret = jnp.split(gates, 2, axis=-1)
    merged = (g_att * jnp.einsum('bse,ed->bsd', y_att, w_attn_branch.astype(jnp.float32))
              + g_ret * jnp.einsum('bse,ed->bsd', y_ret, w_ret_branch.astype(jnp.float32)))
    return jnp.einsum('bsd,de->bse', merged.astype(xn.dtype), w_out)

def hierarchical_moe(x2, w_group, b_group, w_expert, b_expert, w1, w3, w2):
    T, D = x2.shape
    xf = x2.astype(jnp.float32)
    group_p = jax.nn.softmax(xf @ w_group.astype(jnp.float32) + b_group.astype(jnp.float32), axis=-1)
    g_w, g_idx = lax.top_k(group_p, 1)
    exp_logits = (xf @ w_expert.astype(jnp.float32) + b_expert.astype(jnp.float32)).reshape(T, MOE_GROUPS, MOE_EXPERTS_PER_GROUP)
    sel_logits = jnp.take_along_axis(exp_logits, g_idx[:, :, None], axis=1)[:, 0]
    e_w, e_idx = lax.top_k(jax.nn.softmax(sel_logits, axis=-1), MOE_TOP_K)
    e_w = e_w / jnp.sum(e_w, axis=-1, keepdims=True)
    gate = (g_w * e_w).reshape(-1)
    eid = (g_idx * MOE_EXPERTS_PER_GROUP + e_idx).reshape(-1).astype(jnp.int32)
    tok = jnp.repeat(jnp.arange(T, dtype=jnp.int32), MOE_TOP_K)
    A = T * MOE_TOP_K

    order = jnp.argsort(eid)
    s_eid = eid[order]
    s_tok = tok[order]
    s_gate = gate[order]
    counts = jnp.bincount(eid, length=MOE_N_EXPERTS)
    starts = jnp.cumsum(counts) - counts
    padded = (counts + MOE_BLOCK - 1) // MOE_BLOCK * MOE_BLOCK
    p_ends = jnp.cumsum(padded)
    p_starts = p_ends - padded
    dest = p_starts[s_eid] + (jnp.arange(A, dtype=jnp.int32) - starts[s_eid])
    n_blocks = -(-A // MOE_BLOCK) + MOE_N_EXPERTS
    slot_tok = jnp.full((n_blocks * MOE_BLOCK,), T, jnp.int32).at[dest].set(s_tok)
    blk_eid = jnp.clip(jnp.searchsorted(p_ends, jnp.arange(n_blocks) * MOE_BLOCK, side='right'), 0, MOE_N_EXPERTS - 1)
    x_pad = jnp.concatenate([x2, jnp.zeros((1, D), x2.dtype)], axis=0)
    x_slots = x_pad[slot_tok].reshape(n_blocks, MOE_BLOCK, D)

    def expert_block(args):
        xb, e = args
        hid = jax.nn.silu(xb @ w1[e]) * (xb @ w3[e])
        return hid @ w2[e]

    y_slots = lax.map(expert_block, (x_slots, blk_eid)).reshape(n_blocks * MOE_BLOCK, D)
    y_assign = y_slots[dest].astype(jnp.float32) * s_gate[:, None]
    return jax.ops.segment_sum(y_assign, s_tok, num_segments=T).astype(x2.dtype)

def first_inputs(seed: int = 0) -> dict:
    key = jax.random.key(seed)
    ks = jax.random.split(key, 20)
    L = DEPTH
    f32 = jnp.float32

    def nrm(k, shape, scale):
        return jax.random.normal(k, shape, f32) * scale

    heads = jnp.arange(RET_HEADS, dtype=f32)
    decay_logit = jnp.log(2.0 ** (5.0 + heads) - 1.0)
    return {
        'x': nrm(ks[0], (BATCH, SEQ, D_MODEL), 1.0),
        'norm_mix_w': 1.0 + nrm(ks[1], (L, D_MODEL), 0.02),
        'w_in': nrm(ks[2], (L, D_MODEL, IN_W), D_MODEL ** -0.5),
        'b_branch_gate': nrm(ks[3], (L, 2 * D_MODEL), 0.02),
        'ret_decay_fwd': decay_logit[None] + nrm(ks[4], (L, RET_HEADS), 0.05),
        'ret_decay_bwd': decay_logit[None] + nrm(ks[5], (L, RET_HEADS), 0.05),
        'ret_gn_w': 1.0 + nrm(ks[6], (L, RET_V_W), 0.02),
        'w_attn_branch': nrm(ks[7], (L, ATTN_OUT_W, D_MODEL), ATTN_OUT_W ** -0.5),
        'w_ret_branch': nrm(ks[8], (L, RET_V_W, D_MODEL), RET_V_W ** -0.5),
        'w_out': nrm(ks[9], (L, D_MODEL, D_MODEL), D_MODEL ** -0.5),
        'norm_moe_w': 1.0 + nrm(ks[10], (L, D_MODEL), 0.02),
        'moe_w_group': nrm(ks[11], (L, D_MODEL, MOE_GROUPS), D_MODEL ** -0.5),
        'moe_b_group': nrm(ks[12], (L, MOE_GROUPS), 0.01),
        'moe_w_expert': nrm(ks[13], (L, D_MODEL, MOE_N_EXPERTS), D_MODEL ** -0.5),
        'moe_b_expert': nrm(ks[14], (L, MOE_N_EXPERTS), 0.01),
        'moe_w1': nrm(ks[15], (L, MOE_N_EXPERTS, D_MODEL, MOE_HIDDEN), D_MODEL ** -0.5),
        'moe_w3': nrm(ks[16], (L, MOE_N_EXPERTS, D_MODEL, MOE_HIDDEN), D_MODEL ** -0.5),
        'moe_w2': nrm(ks[17], (L, MOE_N_EXPERTS, MOE_HIDDEN, D_MODEL), MOE_HIDDEN ** -0.5),
        'norm_final_w': 1.0 + nrm(ks[18], (D_MODEL,), 0.02),
    }

def first_block(x, norm_mix_w, w_in, b_branch_gate, ret_decay_fwd, ret_decay_bwd, ret_gn_w,
              w_attn_branch, w_ret_branch, w_out, norm_moe_w, moe_w_group, moe_b_group,
              moe_w_expert, moe_b_expert, moe_w1, moe_w3, moe_w2, norm_final_w):
    B, S, D = x.shape
    cos, sin = rotary_tables(S)
    h = x
    for l in range(DEPTH):
        xn = rms_norm(h, norm_mix_w[l])
        mix = hybrid_mixer(xn, w_in[l], b_branch_gate[l], ret_decay_fwd[l], ret_decay_bwd[l], ret_gn_w[l],
                           w_attn_branch[l], w_ret_branch[l], w_out[l], cos, sin)
        h = h + mix.astype(h.dtype)
        hn = rms_norm(h, norm_moe_w[l])
        ffn = hierarchical_moe(hn.reshape(B * S, D), moe_w_group[l], moe_b_group[l], moe_w_expert[l],
                               moe_b_expert[l], moe_w1[l], moe_w3[l], moe_w2[l])
        h = h + ffn.reshape(B, S, D).astype(h.dtype)
    return rms_norm(h, norm_final_w)


DEPTH_2 = 2

MLSTM_HEADS = 4
MLSTM_QK_DIM = 64
MLSTM_V_DIM = 128
MLSTM_QK_W = MLSTM_HEADS * MLSTM_QK_DIM
MLSTM_W = MLSTM_HEADS * MLSTM_V_DIM
MLSTM_CHUNK = 128
QK_CONV = 4
FORGET_BIAS = 3.0
ATTN_HEADS = 8
ATTN_KV_HEADS = 2
ATTN_HEAD_DIM = 64
ATTN_W_2 = ATTN_HEADS * ATTN_HEAD_DIM
ATTN_KV_W = ATTN_KV_HEADS * ATTN_HEAD_DIM
WINDOW = 128
MIX_W = MLSTM_W + ATTN_W_2
SPLITS = (MLSTM_QK_W, MLSTM_QK_W, MLSTM_W, MLSTM_W, 2 * MLSTM_HEADS, ATTN_W_2, ATTN_KV_W, ATTN_KV_W)
IN_W_2 = sum(SPLITS)
D_FF = 2816
FFN_CONV = 3
EPS = 1e-6


def rmsnorm(x, g):
    xf = x.astype(jnp.float32)
    y = xf * lax.rsqrt(jnp.mean(xf * xf, axis=-1, keepdims=True) + EPS)
    return (y * g.astype(jnp.float32)).astype(x.dtype)

def causal_dwconv(x, w):
    K, C = w.shape
    return lax.conv_general_dilated(
        x, w[:, None, :].astype(x.dtype), window_strides=(1,), padding=[(K - 1, 0)],
        dimension_numbers=('NWC', 'WIO', 'NWC'), feature_group_count=C)

def rope(x):
    S, D = x.shape[1], x.shape[-1]
    inv = 1.0 / (ROPE_THETA ** (jnp.arange(0, D, 2, dtype=jnp.float32) / D))
    ang = jnp.arange(S, dtype=jnp.float32)[:, None] * inv[None, :]
    cos = jnp.cos(ang)[None, :, None, :]
    sin = jnp.sin(ang)[None, :, None, :]
    xf = x.astype(jnp.float32)
    x1, x2 = xf[..., :D // 2], xf[..., D // 2:]
    return jnp.concatenate([x1 * cos - x2 * sin, x2 * cos + x1 * sin], axis=-1)

def mlstm_chunkwise(q, k, v, log_i, log_f):
    B, S, H, DK = q.shape
    DV = v.shape[-1]
    L = MLSTM_CHUNK
    NC = S // L

    def chunks(a):
        a = a.reshape((B, NC, L) + a.shape[2:])
        return jnp.moveaxis(a, (1, 3), (0, 2))

    qc = chunks(q)
    kc = chunks(k * (DK ** -0.5))
    vc = chunks(v)
    lic = chunks(log_i)
    bc = jnp.cumsum(chunks(log_f), axis=-1)
    causal = jnp.tril(jnp.ones((L, L), dtype=bool))

    def step(carry, inp):
        C, n, m = carry
        q_, k_, v_, b_, li_ = inp
        dlog = b_[..., :, None] - b_[..., None, :] + li_[..., None, :]
        dlog = jnp.where(causal, dlog, -jnp.inf)
        inter = b_ + m[..., None]
        m_row = jnp.maximum(inter, jnp.max(dlog, axis=-1))
        w_intra = jnp.exp(dlog - m_row[..., None])
        w_inter = jnp.exp(inter - m_row)
        s = jnp.einsum('bhtd,bhsd->bhts', q_, k_) * w_intra
        num = (w_inter[..., None] * jnp.einsum('bhtd,bhde->bhte', q_, C)
               + jnp.einsum('bhts,bhse->bhte', s, v_))
        den = w_inter * jnp.einsum('bhtd,bhd->bht', q_, n) + jnp.sum(s, axis=-1)
        h = num / jnp.maximum(jnp.abs(den), jnp.exp(-m_row))[..., None]
        b_last = b_[..., -1]
        ls = b_last[..., None] - b_ + li_
        m_new = jnp.maximum(b_last + m, jnp.max(ls, axis=-1))
        decay = jnp.exp(b_last + m - m_new)
        ws = jnp.exp(ls - m_new[..., None])
        C = decay[..., None, None] * C + jnp.einsum('bhs,bhsd,bhse->bhde', ws, k_, v_)
        n = decay[..., None] * n + jnp.einsum('bhs,bhsd->bhd', ws, k_)
        return (C, n, m_new), h

    init = (jnp.zeros((B, H, DK, DV), jnp.float32), jnp.zeros((B, H, DK), jnp.float32),
            jnp.zeros((B, H), jnp.float32))
    _, hs = lax.scan(step, init, (qc, kc, vc, bc, lic))
    return jnp.moveaxis(hs, (0, 2), (1, 3)).reshape(B, S, H, DV)

def sliding_window_attention(q, k, v, sinks):
    B, S, H, D = q.shape
    KV = k.shape[2]
    G = H // KV
    W = WINDOW
    NB = S // W
    qb = q.reshape(B, NB, W, KV, G, D)
    kb = k.reshape(B, NB, W, KV, D)
    vb = v.reshape(B, NB, W, KV, D)
    kk = jnp.concatenate([jnp.concatenate([jnp.zeros_like(kb[:, :1]), kb[:, :-1]], axis=1), kb], axis=2)
    vv = jnp.concatenate([jnp.concatenate([jnp.zeros_like(vb[:, :1]), vb[:, :-1]], axis=1), vb], axis=2)
    s = jnp.einsum('bnqkgd,bnskd->bnkgqs', qb, kk) * (D ** -0.5)
    qpos = jnp.arange(W)[:, None] + W
    kpos = jnp.arange(2 * W)[None, :]
    diff = qpos - kpos
    band = (diff >= 0) & (diff < W)
    first = (jnp.arange(NB) == 0)[:, None, None]
    valid = band[None] & ~(first & (kpos[None] < W))
    s = jnp.where(valid[None, :, None, None], s, -jnp.inf)
    sink = sinks.astype(jnp.float32).reshape(1, 1, KV, G, 1, 1)
    mx = jnp.maximum(jnp.max(s, axis=-1, keepdims=True), sink)
    p = jnp.exp(s - mx)
    denom = jnp.sum(p, axis=-1, keepdims=True) + jnp.exp(sink - mx)
    o = jnp.einsum('bnkgqs,bnskd->bnqkgd', p / denom, vv)
    return o.reshape(B, S, H * D)

def token_mixer(h, w_in, qk_conv_w, qk_conv_b, gate_bias, mh_norm_g, attn_sinks, w_out):
    B, S, _ = h.shape
    z = h @ w_in
    parts = []
    off = 0
    for w in SPLITS:
        parts.append(z[..., off:off + w])
        off += w
    mq, mk, mv, mo, mif, aq, ak, av = parts
    qk = jax.nn.silu(causal_dwconv(jnp.concatenate([mq, mk], axis=-1), qk_conv_w) + qk_conv_b)
    qk = qk.astype(jnp.float32)
    mq_h = qk[..., :MLSTM_QK_W].reshape(B, S, MLSTM_HEADS, MLSTM_QK_DIM)
    mk_h = qk[..., MLSTM_QK_W:].reshape(B, S, MLSTM_HEADS, MLSTM_QK_DIM)
    mv_h = mv.astype(jnp.float32).reshape(B, S, MLSTM_HEADS, MLSTM_V_DIM)
    gates = mif.astype(jnp.float32) + gate_bias.astype(jnp.float32)
    log_i = gates[..., :MLSTM_HEADS]
    log_f = jax.nn.log_sigmoid(gates[..., MLSTM_HEADS:])
    ht = mlstm_chunkwise(mq_h, mk_h, mv_h, log_i, log_f)
    ht = ht * lax.rsqrt(jnp.mean(ht * ht, axis=-1, keepdims=True) + EPS)
    m_out = ht.reshape(B, S, MLSTM_W) * mh_norm_g.astype(jnp.float32) * jax.nn.sigmoid(mo.astype(jnp.float32))
    q = rope(aq.reshape(B, S, ATTN_HEADS, ATTN_HEAD_DIM))
    k = rope(ak.reshape(B, S, ATTN_KV_HEADS, ATTN_HEAD_DIM))
    v = av.astype(jnp.float32).reshape(B, S, ATTN_KV_HEADS, ATTN_HEAD_DIM)
    a_out = sliding_window_attention(q, k, v, attn_sinks)
    y = jnp.concatenate([m_out, a_out], axis=-1).astype(h.dtype)
    return y @ w_out

def conv_ffn(h, w_up, ffn_conv_w, w_down):
    u = causal_dwconv(h @ w_up, ffn_conv_w)
    gate, val = u[..., :D_FF], u[..., D_FF:]
    return (jax.nn.silu(gate) * val) @ w_down

def second_inputs(seed: int = 0) -> dict:
    key = jax.random.key(seed)
    ks = jax.random.split(key, 20)
    f32 = jnp.float32
    nrm = lambda k, shape: jax.random.normal(k, shape, f32)
    return {
        "x": nrm(ks[0], (BATCH, SEQ, D_MODEL)),
        "g_pre_mix": 1.0 + 0.05 * nrm(ks[1], (DEPTH_2, D_MODEL)),
        "w_in": nrm(ks[2], (DEPTH_2, D_MODEL, IN_W_2)) * D_MODEL ** -0.5,
        "qk_conv_w": nrm(ks[3], (DEPTH_2, QK_CONV, 2 * MLSTM_QK_W)) * QK_CONV ** -0.5,
        "qk_conv_b": 0.02 * nrm(ks[4], (DEPTH_2, 2 * MLSTM_QK_W)),
        "gate_bias": jnp.concatenate([0.1 * nrm(ks[5], (DEPTH_2, MLSTM_HEADS)),
                                      FORGET_BIAS + 0.5 * nrm(ks[6], (DEPTH_2, MLSTM_HEADS))], axis=-1),
        "mh_norm_g": 1.0 + 0.05 * nrm(ks[7], (DEPTH_2, MLSTM_W)),
        "attn_sinks": 0.5 * nrm(ks[8], (DEPTH_2, ATTN_HEADS)),
        "w_out": nrm(ks[9], (DEPTH_2, MIX_W, D_MODEL)) * MIX_W ** -0.5,
        "g_post_mix": 1.0 + 0.05 * nrm(ks[10], (DEPTH_2, D_MODEL)),
        "g_pre_ffn": 1.0 + 0.05 * nrm(ks[11], (DEPTH_2, D_MODEL)),
        "w_up": nrm(ks[12], (DEPTH_2, D_MODEL, 2 * D_FF)) * D_MODEL ** -0.5,
        "ffn_conv_w": nrm(ks[13], (DEPTH_2, FFN_CONV, 2 * D_FF)) * FFN_CONV ** -0.5,
        "w_down": nrm(ks[14], (DEPTH_2, D_FF, D_MODEL)) * D_FF ** -0.5,
        "g_post_ffn": 1.0 + 0.05 * nrm(ks[15], (DEPTH_2, D_MODEL)),
    }

def second_block(x, g_pre_mix, w_in, qk_conv_w, qk_conv_b, gate_bias, mh_norm_g, attn_sinks, w_out,
              g_post_mix, g_pre_ffn, w_up, ffn_conv_w, w_down, g_post_ffn):
    for l in range(DEPTH_2):
        h = rmsnorm(x, g_pre_mix[l])
        y = token_mixer(h, w_in[l], qk_conv_w[l], qk_conv_b[l], gate_bias[l], mh_norm_g[l],
                        attn_sinks[l], w_out[l])
        x = x + rmsnorm(y, g_post_mix[l])
        h = rmsnorm(x, g_pre_ffn[l])
        y = conv_ffn(h, w_up[l], ffn_conv_w[l], w_down[l])
        x = x + rmsnorm(y, g_post_ffn[l])
    return x


def setup_inputs(seed=0):
    out = dict(first_inputs(seed))
    for name, value in second_inputs(seed + 1).items():
        if name != "x":
            out[name + "_2"] = value
    return out


def reference(
    x, norm_mix_w, w_in, b_branch_gate, ret_decay_fwd, ret_decay_bwd, ret_gn_w, w_attn_branch,
    w_ret_branch, w_out, norm_moe_w, moe_w_group, moe_b_group, moe_w_expert, moe_b_expert,
    moe_w1, moe_w3, moe_w2, norm_final_w, g_pre_mix_2, w_in_2, qk_conv_w_2, qk_conv_b_2,
    gate_bias_2, mh_norm_g_2, attn_sinks_2, w_out_2, g_post_mix_2, g_pre_ffn_2, w_up_2,
    ffn_conv_w_2, w_down_2, g_post_ffn_2,
):
    x = first_block(
        x, norm_mix_w, w_in, b_branch_gate, ret_decay_fwd, ret_decay_bwd, ret_gn_w,
        w_attn_branch, w_ret_branch, w_out, norm_moe_w, moe_w_group, moe_b_group, moe_w_expert,
        moe_b_expert, moe_w1, moe_w3, moe_w2, norm_final_w,
    )
    return second_block(
        x, g_pre_mix_2, w_in_2, qk_conv_w_2, qk_conv_b_2, gate_bias_2, mh_norm_g_2,
        attn_sinks_2, w_out_2, g_post_mix_2, g_pre_ffn_2, w_up_2, ffn_conv_w_2, w_down_2,
        g_post_ffn_2,
    )


_drawn_inputs = setup_inputs


def setup_inputs(seed=0):
    import zlib

    import numpy as np

    out = dict(_drawn_inputs(seed))
    spreads = {}
    factors = {'b_branch_gate': 2.9, 'moe_b_group': 4.155, 'attn_sinks_2': 4.065}
    for name, (base, spread) in spreads.items():
        noise = np.random.default_rng([zlib.crc32(name.encode()), seed]).standard_normal(out[name].shape)
        drawn = base * np.exp(spread * noise) if base else spread * noise
        out[name] = __import__('jax').numpy.asarray(drawn.astype(out[name].dtype))
    for name, factor in factors.items():
        out[name] = (out[name] * factor).astype(out[name].dtype)
    return out
```

```python
from contextlib import ExitStack

import numpy as np
import concourse.bass as bass
from concourse import mybir

F32 = mybir.dt.float32
F32R = mybir.dt.float32r
I32 = mybir.dt.int32
U32 = mybir.dt.uint32
ACT = mybir.ActivationFunctionType
ALU = mybir.AluOpType
AX = mybir.AxisListType

P = 128
D = 1024
S = 512
NT = S // P
KC = D // P
BANK = 512
UNIT = KC * BANK
RING = 4
EPS = 1e-6
NEG = -1e30

HEADS = 8
DH = 64
GROUPS = 3
HALF = 64
STRIDE = 4
DV = 128
STRIP = (2 * NT - 1) * P
EXPERTS = 64
EGROUPS = 8
PER_GROUP = EXPERTS // EGROUPS
HID = 512
FC = HID // P
ARENA = 17024
CAP = 64
SPILL = 2 * S // CAP - 1
BLOCKS = EXPERTS + SPILL
NO_ROW = 1 << 20
ROUTES = EGROUPS + EXPERTS

LAYERS = 2
MH = 4
CONV = 4
FCONV = 3
W_AK = 2056
W_GATES = 1536
W_AQ = 1544
FF = 2816
FB = FF // P

INPUTS = [
    "x", "norm_mix_w", "w_in", "b_branch_gate", "ret_decay_fwd", "ret_decay_bwd", "ret_gn_w",
    "w_attn_branch", "w_ret_branch", "w_out", "norm_moe_w", "moe_w_group", "moe_b_group",
    "moe_w_expert", "moe_b_expert", "moe_w1", "moe_w3", "moe_w2", "norm_final_w", "g_pre_mix_2",
    "w_in_2", "qk_conv_w_2", "qk_conv_b_2", "gate_bias_2", "mh_norm_g_2", "attn_sinks_2",
    "w_out_2", "g_post_mix_2", "g_pre_ffn_2", "w_up_2", "ffn_conv_w_2", "w_down_2", "g_post_ffn_2",
]

TABLES = {}


def tables():
    p = np.arange(P)[:, None]
    parts = {"ident": np.eye(P)}
    inv = (1.0 / (np.float32(10000.0) ** (np.arange(0, DH, 2, dtype=np.float32) / np.float32(DH)))).astype(np.float32)
    for name, token in (("nat", p + P * np.arange(NT)[None]), ("perm", STRIDE * p + np.arange(NT)[None])):
        ang = (token[:, :, None].astype(np.float32) * inv[None, None]).astype(np.float32)
        c, s = np.cos(ang), np.sin(ang)
        parts["cos_" + name] = np.concatenate([c, c], -1).reshape(P, -1)
        parts["sin_" + name] = np.concatenate([-s, s], -1).reshape(P, -1)
    j = np.arange(2 * P)[None]
    parts["mask_band"] = np.where(abs(j - HALF - p) <= HALF, 0, NEG)
    k = np.arange(P)[None]
    parts["mask_near"] = np.where(abs(k - p) <= HALF, 0, NEG)
    parts["mask_comb"] = np.where((k - p) % STRIDE == 0, 0, NEG)
    diff = p - (j - P)
    parts["mask_window"] = np.where((diff >= 0) & (diff < P), 0, NEG)
    parts["mask_causal_t"] = np.where(k >= p, 0, NEG)
    parts["before"] = (p < k) * 1.0
    parts["ones"] = np.ones((P, P))
    parts["expert_row"] = np.broadcast_to(np.arange(EXPERTS)[None], (P, EXPERTS))
    parts["spill_row"] = np.broadcast_to(np.arange(SPILL + 1)[None], (P, SPILL + 1))
    parts["token"] = p + P * np.arange(NT)[None]
    parts["eps"] = np.full((P, 1), EPS)
    parts["spread"] = np.repeat((p == np.arange(MH)[None]).astype(np.float32), P, axis=1)
    rel = np.arange(STRIP)[None] - (NT - 1) * P - p
    parts["rel"] = rel * np.ones((P, 1))
    at = 0
    for name, a in parts.items():
        TABLES[name] = (at, a.shape[1])
        at += a.shape[1]
    return np.ascontiguousarray(np.concatenate([np.asarray(a, np.float32) for a in parts.values()], 1))


CONST = tables().shape[1]
KEPT = TABLES["rel"][0]


class Arena:

    def __init__(self, whole, at=0):
        self.whole, self.at = whole, at

    def __call__(self, *shape):
        n = int(np.prod(shape))
        view = self.whole[:, self.at:self.at + n]
        self.at += n
        assert self.at <= self.whole.shape[1], self.at
        if len(shape) > 1:
            names = "abcd"[:len(shape)]
            view = view.rearrange(f"p ({' '.join(names)}) -> p {' '.join(names)}",
                                  **{x: m for x, m in zip(names, shape)})
        return view


def build(nc, t, const, out):
    ctx = ExitStack()
    with ctx:
        def sb(name, shape, dt=F32):
            return ctx.enter_context(nc.sbuf_tensor(name, shape, dt))

        stage_sems = {}

        def sem(name):
            return ctx.enter_context(nc.semaphore(name))

        stage_done = {me: sem("stage_done_" + me) for me in ("pe", "dve", "act")}
        stage_entered = {me: sem("stage_entered_" + me) for me in ("pe", "dve", "act", "pool")}
        stage_open = sem("stage_open")
        unit_loaded = [sem(f"unit_loaded{i}") for i in range(RING)]
        unit_used = sem("unit_used")
        consts_loaded = sem("consts_loaded")
        spill_loaded = sem("spill_loaded")
        spill_used = sem("spill_used")
        spill_next = sem("spill_next")
        gates_loaded = sem("gates_loaded")
        out_stored = sem("out_stored")
        table_out = sem("table_out")
        gathered = [sem("gathered0"), sem("gathered1")]
        scattered = [sem("scattered0"), sem("scattered1")]
        spill_gathered = sem("spill_gathered")
        spill_scattered = sem("spill_scattered")

        STAGE = [
            "pe_chain", "dve_chain", "act_chain", "pool_chain",
            "rows_loaded", "more_loaded",
            "sums_ready", "roots_ready", "rows_ready", "turned", "turned_kept",
            "proj_ready", "taken_dve", "taken_act", "roped",
            "scores_ready", "scores_taken", "max_ready", "probs_ready", "probs_turned", "probs_kept",
            "mixed_ready", "mixed_taken", "spilled_out", "spilled_in", "exp_asked", "exp_ready",
            "strip_asked", "strip_ready", "weighted", "moments", "deviation", "gated",
            "biased", "cleared", "logits_ready", "chosen", "ranked", "placed", "table_in",
            "stored", "x_turned",
            "gate_ready", "silu_ready", "up_ready", "hidden_ready",
            "down_ready", "fold_made", "x_high", "x_low", "w_high", "w_low", "gate_kept", "up_kept",
            "gate_turned", "up_turned", "y_act", "y_dve", "index_copied", "waits_passed", "pe_passed",
        ]
        for name in STAGE:
            stage_sems[name] = sem(name)
        nums = [s.num for s in stage_sems.values()]
        assert nums == list(range(nums[0], nums[0] + len(nums)))
        Z = type("Sems", (), stage_sems)

        with ExitStack() as plain:
            ring = plain.enter_context(nc.sbuf_tensor("ring", [P, RING, UNIT], F32))
            xn = plain.enter_context(nc.sbuf_tensor("xn", [P, NT, D], F32))
            xnT = plain.enter_context(nc.sbuf_tensor("xnT", [P, KC, S], F32))
            rows = plain.enter_context(nc.sbuf_tensor("rows", [P, 4, D], F32))
        ring_low = sb("ring_low", [P, RING, UNIT], F32R)
        xn_r = sb("xn_r", [P, NT * D], F32R)
        xnT_r = sb("xnT_r", [P, KC * S], F32R)
        rows_r = sb("rows_r", [P, 4 * D], F32R)
        h = sb("h", [P, NT, D])
        cst = sb("cst", [P, KEPT])
        arena = sb("arena", [P, ARENA])
        small = sb("small", [P, 512])
        ps = ctx.enter_context(nc.psum_tensor("ps", [P, 8, BANK], F32))

        def table(name):
            at, n = TABLES[name]
            return cst[:, at:at + n]

        ident = table("ident")

        class Chain:

            def __init__(self, eng, done):
                self.eng, self.done, self.n = eng, done, 0

            def __call__(self, ins):
                self.n += 1
                ins.then_inc(self.done, 1)
                self.eng.wait_ge(self.done, self.n)

        passed = {}
        layer_base = {}

        def next_stage(eng, me, chain=None):
            n = passed.get(me, 0)
            passed[me] = n + 1
            if me in layer_base:
                n = layer_base[me] + n
            if me == "pool":
                for done in stage_done.values():
                    eng.wait_ge(done, n + 1)
                eng.sem_inc(stage_entered[me], 1)
                eng.sem_clear(range(nums[0], nums[-1] + 1))
                eng.drain().then_inc(stage_open, 1)
            else:
                eng.drain().then_inc(stage_done[me], 1)
                eng.wait_ge(stage_open, n + 1)
                eng.sem_inc(stage_entered[me], 1)
            if chain:
                chain.n = 0

        def slot(u):
            return ring[:, u % RING]

        def unit_low(u, cols=BANK):
            return ring_low[:, u % RING].rearrange("p (c n) -> p c n", n=cols)

        def unit(u, cols=BANK):
            return slot(u)[:, 0:UNIT].rearrange("p (c n) -> p c n", n=cols)

        ring_turns = {"loaded": 0}

        def wait_unit(pe, u):
            pe.wait_ge(unit_loaded[u % RING], ring_turns["loaded"] + 16 * (u // RING + 1))

        def release_unit(pe):
            pe.drain().then_inc(unit_used, 1)

        def norm_dve(v, link, src, row, dst, squares=None):
            ss = small[:, 0:NT]
            rstd = small[:, 8:8 + NT]
            for i in range(NT):
                ins = nc.vector.tensor_tensor_reduce(out=(dst if squares is None else squares)[:, i, :], in0=src[:, i, :], in1=src[:, i, :], scale=1.0,
                                                     scalar=0.0, op0=ALU.mult, op1=ALU.add, accum_out=ss[:, i:i + 1])
            ins.then_inc(Z.sums_ready, 1)
            v.wait_ge(Z.roots_ready, 1)
            link(nc.vector.reciprocal(rstd, small[:, 4:4 + NT]))
            for i in range(NT):
                nc.vector.scalar_tensor_tensor(out=dst[:, i, :], in0=src[:, i, :], scalar=rstd[:, i:i + 1], in1=row,
                                               op0=ALU.mult, op1=ALU.mult).then_inc(Z.rows_ready, 1)

        def norm_act(a):
            a.wait_ge(Z.sums_ready, 1)
            nc.scalar.activation(small[:, 4:4 + NT], small[:, 0:NT], ACT.Sqrt, bias=table("eps"),
                                 scale=1.0 / D).then_inc(Z.roots_ready, 1)

        def turn_pe(pe, src, chunks, ready=None, bank0=0):
            n = 0
            for i in range(NT):
                if ready is not None:
                    pe.wait_ge(ready, i + 1)
                view = src[:, i, :].rearrange("k (p c) -> k c p", c=chunks)
                for c0 in range(0, chunks, 4):
                    if n >= 4:
                        pe.wait_ge(Z.turned_kept, n - 3)
                    for c in range(4):
                        ins = nc.tensor.transpose(ps[:, bank0 + n % 4, c * P:(c + 1) * P], view[:, c0 + c, :], ident)
                    ins.then_inc(Z.turned, 1)
                    n += 1

        def turn_act(a, dst, chunks, bank0=0):
            n = 0
            for i in range(NT):
                for c0 in range(0, chunks, 4):
                    a.wait_ge(Z.turned, n + 1)
                    nc.scalar.activation(dst[:, c0:c0 + 4, i * P:(i + 1) * P],
                                         ps[:, bank0 + n % 4, :].rearrange("p (c k) -> p c k", c=4),
                                         ACT.Copy).then_inc(Z.turned_kept, 1)
                    n += 1

        def tokens(i, permuted):
            return slice(i, S, STRIDE) if permuted else slice(i * P, (i + 1) * P)

        def heads_pe(pe, units, permuted, values):
            jobs = [(units[j], tokens(i, permuted)) for j in range(2) for i in range(NT)] + values

            def turn(n):
                pe.wait_ge(Z.roped, n + 1)
                if n >= 2:
                    pe.wait_ge(Z.turned_kept, n - 1)
                for c in range(4):
                    ins = nc.tensor.transpose(ps[:, 4 + n % 2, c * P:(c + 1) * P], L.rot[:, n % 2, c * P:(c + 1) * P], ident)
                ins.then_inc(Z.turned, 1)

            for n, (u, toks) in enumerate(jobs):
                if n == 0 or jobs[n - 1][0] != u:
                    wait_unit(pe, u)
                if 4 <= n < 12:
                    pe.wait_ge(Z.taken_dve, n - 3)
                elif n >= 12:
                    pe.wait_ge(Z.taken_act, n - 11)
                rows_out = len(range(*toks.indices(S)))
                for c in range(KC):
                    ins = nc.tensor.matmul(ps[0:rows_out, n % 4, :], xnT[:, c, toks], unit(u)[:, c, :],
                                           start=(c == 0), stop=(c == KC - 1))
                ins.then_inc(Z.proj_ready, 1)
                if n + 1 == len(jobs) or jobs[n + 1][0] != u:
                    release_unit(pe)
                if 1 <= n <= 8:
                    turn(n - 1)

        def rope(src, tmp, dst, cos, sin, heads, paired=False):
            half = DH // 2
            to = "p (c g d) -> p g c d" if paired else "p (g c d) -> p g c d"
            s4 = src.rearrange("p (g c d) -> p g c d", g=2, d=DH)
            t4 = tmp.rearrange(to, g=2, d=DH)
            d4 = dst.rearrange(to, g=2, d=DH)

            def over(x):
                return x[:, None, None, :].to_broadcast([P, 2, heads // 2, x.shape[1]])
            nc.vector.tensor_tensor(t4[:, :, :, 0:half], s4[:, :, :, half:DH], over(sin[:, 0:half]), ALU.mult)
            nc.vector.tensor_tensor(t4[:, :, :, half:DH], s4[:, :, :, 0:half], over(sin[:, half:DH]), ALU.mult)
            nc.vector.tensor_tensor(d4, s4, over(cos), ALU.mult).then_inc(Z.taken_dve, 1)

        def heads_dve(v, link, permuted):
            cos = table("cos_perm" if permuted else "cos_nat").rearrange("p (i d) -> p i d", i=NT)
            sin = table("sin_perm" if permuted else "sin_nat").rearrange("p (i d) -> p i d", i=NT)
            for n in range(2 * NT):
                v.wait_ge(Z.proj_ready, n + 1)
                if n >= 2:
                    v.wait_ge(Z.turned, n - 1)
                rope(ps[:, n % 4, :], L.tmp, L.rot[:, n % 2, :], cos[:, n % NT], sin[:, n % NT], HEADS)
                v.wait_ge(Z.taken_dve, n + 1)
                nc.vector.tensor_tensor(L.rot[:, n % 2, :], L.rot[:, n % 2, :], L.tmp, ALU.add).then_inc(Z.roped, 1)
                if n + 1 < 2 * NT:
                    v.wait_ge(Z.roped, n + 1)

        def heads_act(a, scales, values):
            for n in range(2 * NT):
                dst = (L.qT, L.kT)[n // NT]
                a.wait_ge(Z.turned, n + 1)
                nc.scalar.activation(dst[:, :, (n % NT) * P:(n % NT + 1) * P],
                                     ps[:, 4 + n % 2, :].rearrange("p (c k) -> p c k", c=4), ACT.Copy,
                                     scale=scales[n // NT]).then_inc(Z.turned_kept, 1)
            for j, dst in enumerate(values):
                n = 2 * NT + j
                a.wait_ge(Z.proj_ready, n + 1)
                nc.scalar.activation(dst, ps[0:dst.shape[0], n % 4, :], ACT.Copy).then_inc(Z.taken_act, 1)

        class L:
            lay = Arena(arena)
            qT = lay(4, S)
            kT = lay(4, S)
            v = lay(4096)
            va = v[:, 0:5 * BANK].rearrange("p (i n) -> p i n", n=BANK)
            vr = v.rearrange("p (i n) -> p i n", n=D)
            o = lay(NT, BANK + 2 * HEADS)
            again = lay.at
            rot = lay(2, BANK)
            tmp = lay(BANK)
            lay.at = again
            og = lay(NT, BANK + 2 * HEADS)
            masked = lay(2, BANK)
            probs = lay(2, BANK)
            turned = lay(2, BANK)

        SHIFTED = [slice(max(0, i * P - HALF), min(S, i * P + HALF)) for i in range(NT + 1)]

        def chunks_of(g):
            res = []
            for i in range(NT):
                if g == 0:
                    keys = [(SHIFTED[j], j, SHIFTED[j].stop - SHIFTED[j].start) for j in (i, i + 1)]
                    m0 = keys[0][0].start - (i * P - HALF)
                    res += [(i, slice(h0, h0 + 3, 2), keys, m0) for h0 in (0, 1, 4, 5)]
                else:
                    res += [(i, slice(h0, HEADS, 2), [(slice(i * P, (i + 1) * P), i, P)], 0) for h0 in (0, 1)]
            return res

        class Attention:

            def __init__(self, chunks, mask, q, k, val, masked, probs, turned, res, sinks=None):
                self.chunks, self.mask, self.q, self.k, self.val, self.sinks = chunks, mask, q, k, val, sinks
                self.masked, self.probs, self.turned, self.res = masked, probs, turned, res
                self.per_tile = len(chunks) // NT

        def attend_pe(pe, A):
            def scores(n):
                i, heads, keys, _ = A.chunks[n]
                if n >= 2:
                    pe.wait_ge(Z.scores_taken, n - 1)
                k0, k1 = keys[0][0].start, keys[-1][0].stop
                for j, hh in enumerate(range(*heads.indices(HEADS))):
                    ins = nc.tensor.matmul(ps[:, n % 2, j * (k1 - k0):(j + 1) * (k1 - k0)], A.q(hh)[:, i * P:(i + 1) * P],
                                           A.k(hh)[:, k0:k1], start=True, stop=True)
                ins.then_inc(Z.scores_ready, 1)

            scores(0)
            for n, (i, heads, keys, _) in enumerate(A.chunks):
                if n + 1 < len(A.chunks):
                    scores(n + 1)
                pe.wait_ge(Z.probs_ready, n + 1)
                if n >= 2:
                    pe.wait_ge(Z.probs_kept, n - 1)
                wide = keys[-1][0].stop - keys[0][0].start
                hs = range(*heads.indices(HEADS))
                b = 0
                for j in range(len(hs)):
                    at = 0
                    for _, _, m in keys:
                        ins = nc.tensor.transpose(ps[0:m, 2 + n % 2, b * P:(b + 1) * P],
                                                  A.probs[:, n % 2, j * wide + at:j * wide + at + m], ident)
                        at += m
                        b += 1
                ins.then_inc(Z.probs_turned, 1)
                pe.wait_ge(Z.probs_kept, n + 1)
                if n % A.per_tile == 0 and i >= 2:
                    pe.wait_ge(Z.mixed_taken, i - 1)
                b = 0
                for hh in hs:
                    for x, (_, vt, m) in enumerate(keys):
                        ins = nc.tensor.matmul(ps[:, 4 + i % 2, hh * DH:(hh + 1) * DH], A.turned[0:m, n % 2, b * P:(b + 1) * P],
                                               A.val(hh, vt)[0:m], start=(x == 0), stop=(x == len(keys) - 1))
                        b += 1
                ins.then_inc(Z.mixed_ready, 1)

        def attend_dve(v, link, A):
            for n, (i, heads, keys, m0) in enumerate(A.chunks):
                nh = len(range(*heads.indices(HEADS)))
                wide = keys[-1][0].stop - keys[0][0].start
                m = A.res[:, i, BANK:BANK + HEADS][:, heads]
                v.wait_ge(Z.scores_ready, n + 1)
                if n >= 2:
                    v.wait_ge(Z.probs_ready, n - 1)
                s = A.masked[:, n % 2, 0:nh * wide].rearrange("p (h k) -> p h k", h=nh)
                nc.vector.tensor_tensor(s, ps[:, n % 2, 0:nh * wide].rearrange("p (h k) -> p h k", h=nh),
                                        A.mask[:, None, m0:m0 + wide].to_broadcast([P, nh, wide]), ALU.add).then_inc(Z.scores_taken, 1)
                v.wait_ge(Z.scores_taken, n + 1)
                link(nc.vector.tensor_reduce(m, s, AX.X, ALU.max))
                if A.sinks is not None:
                    link(nc.vector.tensor_tensor(m, m, A.sinks[:, heads], ALU.max))
                nc.vector.tensor_scalar(small[:, 16 + 8 * (n % 2):16 + 8 * (n % 2) + nh], m, -1.0, None, ALU.mult).then_inc(Z.max_ready, 1)
                v.wait_ge(Z.probs_turned, n + 1)
                if n >= 2:
                    v.wait_ge(Z.mixed_ready, n - 1)
                into = A.turned[:, n % 2, :].rearrange("p (b k) -> p b k", k=P)
                frm = ps[:, 2 + n % 2, :].rearrange("p (b k) -> p b k", k=P)
                blocks = nh * len(keys)
                if len({mm for _, _, mm in keys}) > 1:
                    for x, (_, _, mm) in enumerate(keys):
                        ins = nc.vector.tensor_copy(into[0:mm, x:blocks:len(keys), :], frm[0:mm, x:blocks:len(keys), :])
                else:
                    ins = nc.vector.tensor_copy(into[:, 0:blocks], frm[:, 0:blocks])
                ins.then_inc(Z.probs_kept, 1)

        def attend_act(a, A):
            for n, (i, heads, keys, _) in enumerate(A.chunks):
                wide = keys[-1][0].stop - keys[0][0].start
                a.wait_ge(Z.max_ready, n + 1)
                if n >= 2:
                    a.wait_ge(Z.probs_turned, n - 1)
                for j, hh in enumerate(range(*heads.indices(HEADS))):
                    ins = nc.scalar.activation(A.probs[:, n % 2, j * wide:(j + 1) * wide], A.masked[:, n % 2, j * wide:(j + 1) * wide],
                                               ACT.Exp, bias=small[:, 16 + 8 * (n % 2) + j:17 + 8 * (n % 2) + j],
                                               accum_out=A.res[:, i, BANK + HEADS + hh:BANK + HEADS + hh + 1])
                ins.then_inc(Z.probs_ready, 1)
                if n % A.per_tile == 0 and n:
                    a.wait_ge(Z.mixed_ready, n)
                    nc.scalar.activation(A.res[:, i - 1, 0:BANK], ps[:, 4 + (i - 1) % 2, :], ACT.Copy).then_inc(Z.mixed_taken, 1)
            a.wait_ge(Z.mixed_ready, len(A.chunks))
            nc.scalar.activation(A.res[:, NT - 1, 0:BANK], ps[:, 4 + (NT - 1) % 2, :], ACT.Copy).then_inc(Z.mixed_taken, 1)

        def half_of(n):
            return slice(DH * (n % 2), DH * (n % 2) + DH)

        def dilated(g):
            return Attention(chunks_of(g), table(("mask_band", "mask_near", "mask_comb")[g]),
                             lambda hh: L.qT[half_of(hh), hh // 2, :], lambda hh: L.kT[half_of(hh), hh // 2, :],
                             lambda hh, vt: L.va[:, vt, hh * DH:(hh + 1) * DH],
                             L.masked, L.probs, L.turned, L.o if g == 0 else L.og)

        spilled = nc.dram_tensor("attn_spill", (2, S, BANK + 2 * HEADS), F32).ap()

        def leave_act(a, g):
            a.wait_ge(Z.mixed_taken, NT)
            a.dma_start(spilled[g - 1].rearrange("(p i) n -> p i n", i=NT), L.og).then_inc(Z.spilled_out, 16)
            a.wait_ge(Z.spilled_out, 16)

        class C:
            lay = Arena(arena)
            o = [None, lay(NT, BANK + 2 * HEADS), lay(NT, BANK + 2 * HEADS)]
            yT = Arena(arena, 13184)(4, S)
            assert lay.at <= 8192
        C.o[0] = L.o

        def combine_act(a):
            for g in (1, 2):
                a.dma_start(C.o[g], spilled[g - 1].rearrange("(i p) n -> p i n", p=P)).then_inc(Z.spilled_in, 16)
            a.wait_ge(Z.exp_asked, 1)
            e = small[:, 64:64 + 3 * NT * HEADS]
            nc.scalar.activation(e, e, ACT.Exp).then_inc(Z.exp_ready, 1)
            turn_act(a, C.yT, 4)

        def combine_dve(v, link):
            n = NT * HEADS
            top = small[:, 32:64]
            e = [small[:, 64 + g * n:64 + (g + 1) * n].rearrange("p (i h) -> p i h", i=NT) for g in range(GROUPS)]
            m = [C.o[g][:, :, BANK:BANK + HEADS] for g in range(GROUPS)]
            d = [C.o[g][:, :, BANK + HEADS:] for g in range(GROUPS)]
            top = top.rearrange("p (i h) -> p i h", i=NT)
            den = small[:, 192:192 + n].rearrange("p (i h) -> p i h", i=NT)
            v.wait_ge(Z.spilled_in, 32)
            link(nc.vector.tensor_tensor(top, m[0], m[1], ALU.max))
            link(nc.vector.tensor_tensor(top, top, m[2], ALU.max))
            for g in range(GROUPS):
                ins = nc.vector.tensor_tensor(e[g], m[g], top, ALU.subtract)
            ins.then_inc(Z.exp_asked, 1)
            v.wait_ge(Z.exp_ready, 1)
            for g in range(GROUPS):
                ins = nc.vector.tensor_tensor(d[g], d[g], e[g], ALU.mult)
            link(ins)
            link(nc.vector.tensor_tensor(den, d[0], d[1], ALU.add))
            link(nc.vector.tensor_tensor(den, den, d[2], ALU.add))
            link(nc.vector.reciprocal(den, den))
            for g in range(GROUPS):
                ins = nc.vector.tensor_tensor(e[g], e[g], den, ALU.mult)
            link(ins)
            for i in range(NT):
                for g in range(GROUPS):
                    o3 = C.o[g][:, i, 0:BANK].rearrange("p (h d) -> p h d", d=DH)
                    ins = nc.vector.tensor_tensor(o3, o3, e[g][:, i, :, None].to_broadcast([P, HEADS, DH]), ALU.mult)
                link(ins)
                link(nc.vector.tensor_tensor(C.o[0][:, i, 0:BANK], C.o[0][:, i, 0:BANK], C.o[1][:, i, 0:BANK], ALU.add))
                nc.vector.tensor_tensor(C.o[0][:, i, 0:BANK], C.o[0][:, i, 0:BANK], C.o[2][:, i, 0:BANK], ALU.add).then_inc(Z.rows_ready, 1)

        def log_sigmoid_dve(v, link, x, w, out, done=None):
            e, z, z2 = w
            link(nc.vector.tensor_scalar(e, x, -1.0, None, ALU.mult))
            nc.vector.tensor_tensor(e, e, x, ALU.min).then_inc(Z.exp_asked, 1)
            v.wait_ge(Z.exp_ready, 1)
            link(nc.vector.tensor_scalar(z, e, 2.0, None, ALU.add))
            link(nc.vector.reciprocal(z, z))
            link(nc.vector.tensor_tensor(z, z, e, ALU.mult))
            link(nc.vector.tensor_tensor(z2, z, z, ALU.mult))
            link(nc.vector.tensor_scalar(e, z2, 1.0 / 17, None, ALU.mult))
            for n in (15, 13, 11, 9, 7, 5, 3):
                link(nc.vector.scalar_tensor_tensor(out=e, in0=e, scalar=1.0 / n, in1=z2, op0=ALU.add, op1=ALU.mult))
            link(nc.vector.scalar_tensor_tensor(out=e, in0=e, scalar=1.0, in1=z, op0=ALU.add, op1=ALU.mult))
            link(nc.vector.tensor_scalar(z, x, 0.0, None, ALU.min))
            ins = nc.vector.scalar_tensor_tensor(out=out, in0=e, scalar=-2.0, in1=z, op0=ALU.mult, op1=ALU.add)
            if done is None:
                link(ins)
            else:
                ins.then_inc(done, 1)

        class R:
            lay = Arena(arena, 8192)
            w = lay(2, NT, S)
            rel = lay(STRIP)
            assert lay.at <= 13184
            lay.at = 15232
            strip = lay(2, STRIP)
            decay = small[:, 240:256]
            neg = small[:, 256:264]
            mid = small[:, 384:512]

        def retain_pool(pool):
            lo, hi = (NT - 1) * P, NT * P
            pool.wait_ge(Z.more_loaded, 16)
            pool.wait_ge(Z.biased, 1)
            chain = Chain(pool, Z.pool_chain)
            for n in range(HEADS):
                if n:
                    pool.wait_ge(Z.strip_ready, n)
                if n >= 2:
                    pool.wait_ge(Z.scores_taken, NT * (n - 1))
                f = R.strip[:, n % 2]
                gf, gb = R.decay[:, n:n + 1], R.neg[:, n:n + 1]
                nc.gpsimd.tensor_scalar(f[:, 0:lo], R.rel[:, 0:lo], gb, None, ALU.mult)
                nc.gpsimd.tensor_scalar(f[:, hi:], R.rel[:, hi:], gf, None, ALU.mult)
                nc.gpsimd.tensor_scalar(f[:, lo:hi], R.rel[:, lo:hi], 0.0, gf, ALU.max, ALU.mult)
                chain(nc.gpsimd.tensor_scalar(R.mid, R.rel[:, lo:hi], 0.0, gb, ALU.min, ALU.mult))
                nc.gpsimd.tensor_tensor(f[:, lo:hi], f[:, lo:hi], R.mid, ALU.add).then_inc(Z.strip_asked, 1)
                pool.wait_ge(Z.exp_ready, n + 2)
                chain(nc.gpsimd.tensor_tensor(R.mid, ident, f[:, lo:hi], ALU.mult))
                nc.gpsimd.tensor_tensor(f[:, lo:hi], f[:, lo:hi], R.mid, ALU.add).then_inc(Z.strip_ready, 1)

        def retain_pe(pe):
            def scores(n):
                r = slice(DH * (n % 2), DH * (n % 2) + DH)
                for kt in range(NT):
                    if kt >= 2:
                        pe.wait_ge(Z.scores_taken, NT * n + kt - 1)
                    elif n >= 2:
                        pe.wait_ge(Z.scores_taken, NT * (n - 2) + kt + 3)
                    nc.tensor.matmul(ps[:, 2 * (n % 2) + kt % 2, :], L.kT[r, n // 2, kt * P:(kt + 1) * P], L.qT[r, n // 2, :],
                                     start=True, stop=True).then_inc(Z.scores_ready, 1)

            scores(0)
            for n in range(HEADS):
                if n + 1 < HEADS:
                    scores(n + 1)
                pe.wait_ge(Z.scores_taken, NT * n + NT)
                if n >= 2:
                    pe.wait_ge(Z.mixed_taken, n - 1)
                for i in range(NT):
                    for kt in range(NT):
                        ins = nc.tensor.matmul(ps[:, 4 + n % 2, i * P:(i + 1) * P], R.w[:, n % 2, kt, i * P:(i + 1) * P],
                                               L.vr[:, kt, n * DV:(n + 1) * DV], start=(kt == 0), stop=(kt == NT - 1))
                ins.then_inc(Z.mixed_ready, 1)

        def retain_dve(v, link):
            v.wait_ge(Z.rows_loaded, 32)
            w = [small[:, 264 + 16 * j:280 + 16 * j] for j in range(3)]
            log_sigmoid_dve(v, link, R.decay, w, R.decay)
            nc.vector.tensor_scalar(R.neg, R.decay[:, HEADS:], -1.0, None, ALU.mult).then_inc(Z.biased, 1)
            lo = (NT - 1) * P

            def normed(n):
                v.wait_ge(Z.mixed_ready, n + 1)
                stats = small[:, 320:344].rearrange("p (i s) -> p i s", i=NT)
                mv = small[:, 344:352].rearrange("p (i s) -> p i s", i=NT)
                std = small[:, 352:356]
                for i in range(NT):
                    ins = nc.vector.bn_stats(stats[:, i, :], ps[:, 4 + n % 2, i * P:(i + 1) * P])
                link(ins)
                for i in range(NT):
                    ins = nc.vector.bn_aggr(mv[:, i, :], stats[:, i, :])
                ins.then_inc(Z.moments, 1)
                v.wait_ge(Z.deviation, n + 1)
                link(nc.vector.reciprocal(small[:, 356:360], std))
                for i in range(NT):
                    ins = nc.vector.tensor_scalar(xn[:, i, n * DV:(n + 1) * DV], ps[:, 4 + n % 2, i * P:(i + 1) * P],
                                                  mv[:, i, 0:1], small[:, 356 + i:357 + i], ALU.subtract, ALU.mult)
                ins.then_inc(Z.mixed_taken, 1)

            for n in range(HEADS):
                v.wait_ge(Z.strip_ready, n + 1)
                if n >= 2:
                    v.wait_ge(Z.mixed_ready, n - 1)
                for kt in range(NT):
                    v.wait_ge(Z.scores_ready, NT * n + kt + 1)
                    nc.vector.tensor_tensor(R.w[:, n % 2, kt, :], ps[:, 2 * (n % 2) + kt % 2, :],
                                            R.strip[:, n % 2, lo - kt * P:lo - kt * P + S], ALU.mult).then_inc(Z.scores_taken, 1)
                if n:
                    normed(n - 1)
            normed(HEADS - 1)

        def retain_act(a):
            a.dma_start(R.decay[:, 0:HEADS], t["ret_decay_fwd"].partition_broadcast(P)).then_inc(Z.rows_loaded, 16)
            a.dma_start(R.decay[:, HEADS:], t["ret_decay_bwd"].partition_broadcast(P)).then_inc(Z.rows_loaded, 16)
            at, n_rel = TABLES["rel"]
            a.dma_start(R.rel, const[:, at:at + n_rel]).then_inc(Z.more_loaded, 16)
            a.wait_ge(Z.exp_asked, 1)
            nc.scalar.activation(small[:, 264:280], small[:, 264:280], ACT.Exp).then_inc(Z.exp_ready, 1)

            def strip(n):
                a.wait_ge(Z.strip_asked, n + 1)
                nc.scalar.activation(R.strip[:, n % 2], R.strip[:, n % 2], ACT.Exp).then_inc(Z.exp_ready, 1)

            strip(0)
            for n in range(HEADS):
                if n + 1 < HEADS:
                    strip(n + 1)
                a.wait_ge(Z.moments, n + 1)
                nc.scalar.activation(small[:, 352:356], small[:, 345:352:2], ACT.Sqrt, bias=table("eps")).then_inc(Z.deviation, 1)

        def jobs_pe(pe, jobs):
            for n, (u, pairs, _) in enumerate(jobs):
                if n == 0 or jobs[n - 1][0] != u:
                    wait_unit(pe, u)
                if n >= 4:
                    who = jobs[n - 4][2]
                    count = sum(j[2] == who for j in jobs[:n - 3])
                    pe.wait_ge(Z.taken_dve if who == "dve" else Z.taken_act, count)
                for c, (left, right) in enumerate(pairs):
                    ins = nc.tensor.matmul(ps[:, n % 4, 0:right.shape[1]], left, right, start=(c == 0), stop=(c == len(pairs) - 1))
                ins.then_inc(Z.proj_ready, 1)
                if n + 1 == len(jobs) or jobs[n + 1][0] != u:
                    release_unit(pe)

        def tiles_jobs(u, src, taker, chunks=KC, halves=(0,), cols=BANK):
            return [(u, [(src[:, c, i * P:(i + 1) * P], unit(u, cols)[:, c, n * BANK:min((n + 1) * BANK, cols)]) for c in range(chunks)], taker)
                    for n in halves for i in range(NT)]

        class M:
            lay = Arena(arena)
            yT = lay(KC, S)
            mT = lay(KC, S)
            part = lay(NT, BANK)
            gate = lay(2, BANK)
            assert lay.at <= 13184

        def gate_dve(v, n_units):
            for n in range(2 * NT):
                half, i = divmod(n, NT)
                x = xn[:, i, half * BANK:(half + 1) * BANK]
                nc.vector.tensor_tensor(x, x, rows[:, 1, half * BANK:(half + 1) * BANK], ALU.mult).then_inc(Z.weighted, 1)
                v.wait_ge(Z.weighted, n + 1)
                v.wait_ge(Z.taken_act, n + 1)
                ins = nc.vector.tensor_tensor(x, x, M.gate[:, n % 2], ALU.mult)
                ins.then_inc(Z.gated if half == 0 else Z.rows_ready, 1)

        def gate_act(a):
            for n in range(2 * NT):
                a.wait_ge(Z.proj_ready, n + 1)
                if n >= 2:
                    m = n - 1
                    a.wait_ge(Z.gated, min(m, NT))
                    if m > NT:
                        a.wait_ge(Z.rows_ready, m - NT)
                nc.scalar.activation(M.gate[:, n % 2], ps[:, n % 4, :], ACT.Silu).then_inc(Z.taken_act, 1)

        U_MERGE = 15
        ATT_HALVES, GATE_A = 0, 8

        def merge_jobs():
            u = U_MERGE
            jobs = tiles_jobs(u, C.yT, "act", chunks=4, halves=(0, 1), cols=D)
            for n in range(2):
                jobs += tiles_jobs(u + 1 + n, xnT, "dve")
            for n in range(2):
                jobs += tiles_jobs(u + 3 + 2 * n, M.yT, "act")
                jobs += tiles_jobs(u + 4 + 2 * n, xnT, "dve")
            return jobs

        def merge_dve(v):
            gates = [n for n, j in enumerate(merge_jobs()) if j[2] == "dve"]
            for k, n in enumerate(gates):
                ret = n >= 16
                half, i = (k // NT) % 2, k % NT
                col = (BANK * half) + (D if ret else 0)
                brow = rows[:, 2:4].rearrange("p a n -> p (a n)")[:, col:col + BANK]
                x = xn[:, i, half * BANK:(half + 1) * BANK]
                v.wait_ge(Z.proj_ready, n + 1)
                nc.vector.tensor_tensor(M.gate[:, k % 2], ps[:, n % 4, :], brow, ALU.add).then_inc(Z.taken_dve, 1)
                v.wait_ge(Z.gated, k + 1)
                if not ret:
                    if k == 0:
                        v.wait_ge(Z.taken_act, 2 * NT)
                    nc.vector.tensor_tensor(x, x, M.gate[:, k % 2], ALU.mult).then_inc(Z.weighted, 1)
                else:
                    if i == 0:
                        v.wait_ge(Z.taken_act, 2 * NT + NT * (half + 1))
                    nc.vector.tensor_tensor(M.gate[:, k % 2], M.gate[:, k % 2], M.part[:, i], ALU.mult).then_inc(Z.rows_ready, 1)
                    v.wait_ge(Z.rows_ready, k - 2 * NT + 1)
                    nc.vector.tensor_tensor(x, x, M.gate[:, k % 2], ALU.add).then_inc(Z.weighted, 1)
                v.wait_ge(Z.weighted, k + 1)

        def merge_act(a):
            k = 0
            copies = 0
            for n, job in enumerate(merge_jobs()):
                if job[2] == "act":
                    a.wait_ge(Z.proj_ready, n + 1)
                    if n < 2 * NT:
                        half, i = divmod(n, NT)
                        dst = xn[:, i, half * BANK:(half + 1) * BANK]
                    else:
                        i = copies % NT
                        dst = M.part[:, i]
                        if copies >= 3 * NT:
                            a.wait_ge(Z.rows_ready, i + 1)
                    nc.scalar.activation(dst, ps[:, n % 4, :], ACT.Copy).then_inc(Z.taken_act, 1)
                    copies += 1
                else:
                    a.wait_ge(Z.taken_dve, k + 1)
                    nc.scalar.activation(M.gate[:, k % 2], M.gate[:, k % 2], ACT.Sigmoid).then_inc(Z.gated, 1)
                    k += 1

        def add_results_dve(v, dst):
            for n in range(2 * NT):
                half, i = divmod(n, NT)
                x = dst[:, i, half * BANK:(half + 1) * BANK]
                v.wait_ge(Z.proj_ready, n + 1)
                nc.vector.tensor_tensor(x, x, ps[:, n % 4, :], ALU.add).then_inc(Z.taken_dve, 1)

        normed_rows = nc.dram_tensor("normed_rows", (S, D), F32).ap()
        slot_table = nc.dram_tensor("slot_table", (CAP * BLOCKS, 2), I32).ap()
        expert_rows = nc.dram_tensor("expert_rows", (2 * S, D), F32).ap()
        gates = small[:, 400:400 + 2 * NT].rearrange("p (i k) -> p i k", k=2)
        spill_info = small[:, 408:408 + SPILL + 1].bitcast(I32)

        class G:
            lay = Arena(arena)
            w = lay(KC, ROUTES)
            bias = lay(ROUTES)
            logits = lay(NT, ROUTES)
            by_group = lay(NT, EXPERTS)
            group_is = lay(NT, EGROUPS)
            in_group = lay(NT, PER_GROUP)
            best = lay(NT, 8)
            best_at = lay(NT, 8).bitcast(U32)
            group = lay(NT)
            e_at = lay(NT, 2)
            num = lay(NT, EGROUPS)
            one = lay(NT)
            is_expert = [lay(NT, EXPERTS), lay(NT, EXPERTS)]
            either = lay(NT, EXPERTS)
            rank = lay(NT, EXPERTS)
            part = lay(NT, EXPERTS)
            place = lay(NT, EXPERTS)
            count = lay(EXPERTS)
            further = lay(EXPERTS)
            cum = lay(EXPERTS)
            first = lay(EXPERTS)
            tmp = lay(EXPERTS)
            le = lay(SPILL + 1, EXPERTS)
            spill = lay(SPILL + 1)
            slot = lay(NT, 2)
            slot_i = lay(NT, 2).bitcast(I32)
            pair = lay(NT, 2, 2)
            pair_i = lay(NT, 2, 2).bitcast(I32)
            empty = lay(2 * BLOCKS).bitcast(I32)

        def load_routes(a):
            a.dma_start(G.w[:, :, 0:EGROUPS], t["moe_w_group"][0].rearrange("(p c) n -> p c n", c=KC)).then_inc(Z.more_loaded, 16)
            a.dma_start(G.w[:, :, EGROUPS:], t["moe_w_expert"][0].rearrange("(p c) n -> p c n", c=KC)).then_inc(Z.more_loaded, 16)
            a.dma_start(G.bias[:, 0:EGROUPS], t["moe_b_group"].partition_broadcast(P)).then_inc(Z.more_loaded, 16)
            a.dma_start(G.bias[:, EGROUPS:], t["moe_b_expert"].partition_broadcast(P)).then_inc(Z.more_loaded, 16)
            a.wait_ge(Z.more_loaded, 64)

        def route_pe(pe):
            for i in range(NT):
                for c in range(KC):
                    ins = nc.tensor.matmul(ps[:, i, 0:ROUTES], xnT[:, c, i * P:(i + 1) * P], G.w[:, c, :], start=(c == 0), stop=(c == KC - 1))
            ins.then_inc(Z.logits_ready, 1)
            pe.wait_ge(Z.chosen, 1)
            for i in range(NT):
                nc.tensor.matmul(ps[:, 4 + i % 2, (i // 2) * EXPERTS:(i // 2 + 1) * EXPERTS], table("before"), G.either[:, i, :], start=True, stop=(i == 0))
                for j in range(i):
                    nc.tensor.matmul(ps[:, 4 + i % 2, (i // 2) * EXPERTS:(i // 2 + 1) * EXPERTS], table("ones"), G.either[:, j, :], start=False, stop=(j == i - 1))
            for j in range(NT):
                ins = nc.tensor.matmul(ps[:, 6, 0:EXPERTS], table("ones"), G.either[:, j, :], start=(j == 0), stop=(j == NT - 1))
            ins.then_inc(Z.ranked, 1)

        def route_act(a):
            a.wait_ge(Z.exp_asked, 1)
            nc.scalar.activation(G.num, G.num, ACT.Exp).then_inc(Z.exp_ready, 1)
            a.wait_ge(Z.exp_asked, 2)
            nc.scalar.activation(G.one, G.one, ACT.Exp).then_inc(Z.exp_ready, 1)
            a.wait_ge(table_out, 16 * (2 * NT + 1))
            a.dma_start(E.table[0:CAP], slot_table.rearrange("(p b) k -> p (b k)", p=CAP)).then_inc(Z.table_in, 16)
            a.wait_ge(Z.table_in, 16)

        def route_dve(v, link):
            def over(x, n, w):
                return x.to_broadcast([P, n, w])
            v.wait_ge(Z.logits_ready, 1)
            link(nc.vector.tensor_tensor(G.logits, ps[:, 0:NT, 0:ROUTES], G.bias[:, None, :].to_broadcast([P, NT, ROUTES]), ALU.add))
            lg = G.logits[:, :, 0:EGROUPS]
            for i in range(NT):
                ins = nc.vector.max(G.best[:, i, :], lg[:, i, :])
            link(ins)
            for i in range(NT):
                nc.vector.max_index(G.best_at[:, i, :], G.best[:, i, :], lg[:, i, :])
            ins = nc.vector.tensor_tensor(G.num, lg, G.best[:, :, 0:1].to_broadcast([P, NT, EGROUPS]), ALU.subtract)
            ins.then_inc(Z.exp_asked, 1)
            v.wait_ge(Z.exp_asked, 1)
            link(nc.vector.tensor_copy(G.group[:, :, None], G.best_at[:, :, 0:1]))
            erow = table("expert_row")
            link(nc.vector.tensor_tensor(G.group_is, erow[:, None, 0:EGROUPS].to_broadcast([P, NT, EGROUPS]),
                                         G.group[:, :, None].to_broadcast([P, NT, EGROUPS]), ALU.is_equal))
            for i in range(NT):
                ins = nc.vector.tensor_tensor(G.by_group[:, i, :].rearrange("p (g e) -> p g e", g=EGROUPS),
                                              G.logits[:, i, EGROUPS:].rearrange("p (g e) -> p g e", g=EGROUPS),
                                              G.group_is[:, i, :, None].to_broadcast([P, EGROUPS, PER_GROUP]), ALU.mult)
            link(ins)
            for i in range(NT):
                ins = nc.vector.tensor_reduce(G.in_group[:, i, :], G.by_group[:, i, :].rearrange("p (g e) -> p e g", g=EGROUPS), AX.X, ALU.add)
            link(ins)
            for i in range(NT):
                ins = nc.vector.max(G.best[:, i, :], G.in_group[:, i, :])
            link(ins)
            for i in range(NT):
                ins = nc.vector.max_index(G.best_at[:, i, :], G.best[:, i, :], G.in_group[:, i, :])
            link(ins)
            nc.vector.tensor_tensor(G.one[:, :, None], G.best[:, :, 1:2], G.best[:, :, 0:1], ALU.subtract).then_inc(Z.exp_asked, 1)
            v.wait_ge(Z.exp_ready, 2)
            link(nc.vector.tensor_reduce(gates[:, :, 0], G.num, AX.X, ALU.add))
            link(nc.vector.scalar_tensor_tensor(out=gates[:, :, 0], in0=G.one, scalar=1.0, in1=gates[:, :, 0], op0=ALU.add, op1=ALU.mult))
            link(nc.vector.reciprocal(gates[:, :, 0], gates[:, :, 0]))
            nc.vector.tensor_tensor(gates[:, :, 1], gates[:, :, 0], G.one, ALU.mult)
            link(nc.vector.tensor_copy(G.e_at, G.best_at[:, :, 0:2]))
            link(nc.vector.scalar_tensor_tensor(out=G.e_at, in0=G.group[:, :, None].to_broadcast([P, NT, 2]), scalar=float(PER_GROUP),
                                                in1=G.e_at, op0=ALU.mult, op1=ALU.add))
            for k in range(2):
                ins = nc.vector.tensor_tensor(G.is_expert[k], erow[:, None, :].to_broadcast([P, NT, EXPERTS]),
                                              G.e_at[:, :, k:k + 1].to_broadcast([P, NT, EXPERTS]), ALU.is_equal)
            link(ins)
            nc.vector.tensor_tensor(G.either, G.is_expert[0], G.is_expert[1], ALU.add).then_inc(Z.chosen, 1)
            v.wait_ge(Z.ranked, 1)
            link(nc.vector.tensor_copy(G.count, ps[:, 6, 0:EXPERTS]))
            for i in range(NT):
                ins = nc.vector.tensor_copy(G.rank[:, i, :], ps[:, 4 + i % 2, (i // 2) * EXPERTS:(i // 2 + 1) * EXPERTS])
            link(nc.vector.tensor_scalar(G.further, G.count, float(CAP), None, ALU.is_gt))
            for m in range(2, S // CAP):
                link(nc.vector.scalar_tensor_tensor(out=G.further, in0=G.count, scalar=float(m * CAP), in1=G.further, op0=ALU.is_gt, op1=ALU.add))
            link(nc.vector.memset(G.tmp, 0.0))
            link(nc.vector.tensor_tensor_scan(G.cum, G.further, G.tmp, 0.0, ALU.add, ALU.add))
            link(nc.vector.tensor_tensor(G.first, G.cum, G.further, ALU.subtract))
            link(nc.vector.tensor_tensor(G.le, G.cum[:, None, :].to_broadcast([P, SPILL + 1, EXPERTS]),
                                         table("spill_row")[:, :, None].to_broadcast([P, SPILL + 1, EXPERTS]), ALU.is_le))
            link(nc.vector.tensor_reduce(G.spill, G.le, AX.X, ALU.add))
            link(nc.vector.tensor_scalar(G.spill, G.spill, float(EXPERTS - 1), None, ALU.min))
            link(nc.vector.tensor_copy(G.spill[:, SPILL:], G.cum[:, EXPERTS - 1:]))
            link(nc.vector.tensor_copy(spill_info, G.spill))
            m = G.part
            link(nc.vector.tensor_scalar(m, G.rank, float(CAP), None, ALU.is_ge))
            for x in range(2, S // CAP):
                link(nc.vector.scalar_tensor_tensor(out=m, in0=G.rank, scalar=float(x * CAP), in1=m, op0=ALU.is_ge, op1=ALU.add))
            link(nc.vector.scalar_tensor_tensor(out=G.place, in0=m, scalar=-float(CAP), in1=G.rank, op0=ALU.mult, op1=ALU.add))
            link(nc.vector.tensor_scalar(G.place, G.place, float(BLOCKS), None, ALU.mult))
            link(nc.vector.scalar_tensor_tensor(out=G.place, in0=erow[:, None, :].to_broadcast([P, NT, EXPERTS]), scalar=1.0, in1=G.place,
                                                op0=ALU.mult, op1=ALU.add))
            link(nc.vector.scalar_tensor_tensor(out=G.first, in0=G.first, scalar=float(EXPERTS - 1), in1=erow, op0=ALU.add, op1=ALU.subtract))
            link(nc.vector.tensor_tensor(G.by_group, m, G.first[:, None, :].to_broadcast([P, NT, EXPERTS]), ALU.add))
            link(nc.vector.scalar_tensor_tensor(out=G.by_group, in0=m, scalar=0.0, in1=G.by_group, op0=ALU.is_gt, op1=ALU.mult))
            link(nc.vector.tensor_tensor(G.place, G.place, G.by_group, ALU.add))
            for k in range(2):
                link(nc.vector.tensor_tensor(G.is_expert[k], G.is_expert[k], G.place, ALU.mult))
                link(nc.vector.tensor_reduce(G.slot[:, :, k], G.is_expert[k], AX.X, ALU.add))
                tok = table("token")
                link(nc.vector.tensor_copy(G.pair[:, :, k, 0], tok))
                link(nc.vector.tensor_scalar(G.pair[:, :, k, 1], tok, 2.0, float(k), ALU.mult, ALU.add))
            link(nc.vector.tensor_copy(G.pair_i, G.pair))
            nc.vector.tensor_copy(G.slot_i, G.slot).then_inc(Z.placed, 1)

        def route_pool(pool):
            nc.gpsimd.memset(G.empty[0:CAP], NO_ROW).then_inc(Z.cleared, 1)
            pool.wait_ge(Z.cleared, 1)
            pool.dma_start(slot_table.rearrange("(p b) k -> p (b k)", p=CAP), G.empty[0:CAP]).then_inc(table_out, 16)
            pool.wait_ge(table_out, 16)
            pool.wait_ge(Z.placed, 1)
            for i in range(NT):
                for k in range(2):
                    nc.gpsimd.indirect_dma_start(out=slot_table, out_offset=bass.IndirectOffsetOnAxis(ap=G.slot_i[:, i, k:k + 1], axis=0),
                                                 in_=G.pair_i[:, i, k, :], in_offset=None).then_inc(table_out, 16)

        U_EXPERTS = 24
        PAR = 4
        assert 3 * PAR % RING == 0 and U_EXPERTS % RING == 0 and EXPERTS % PAR == 0

        class E:
            lay = Arena(arena)
            lay.at = G.lay.at
            table = lay(2 * BLOCKS).bitcast(I32)
            index = lay(4, 2).bitcast(I32)
            fold = lay(CAP)
            x = lay(2, D)
            gate = lay(HID)
            up = lay(HID)
            silu = lay(FC, CAP)
            hT = lay(FC, CAP)
            y = lay(2, D)
            xs = rows_r[:, 0:KC * 2 * CAP].rearrange("p (c k) -> p c k", c=KC)
            high = [xnT_r, xn_r]

        def expert_weights(e):
            w1, w3, w2 = (t[n][0][bass.ds(e, 1)] for n in ("moe_w1", "moe_w3", "moe_w2"))
            return [w1.rearrange("e (p c) n -> p (e c) n", c=KC), w3.rearrange("e (p c) n -> p (e c) n", c=KC),
                    w2.rearrange("e (p c) n -> p (e c) n", c=FC)]

        def wait_past(eng, sem_, value):
            if not isinstance(value, int) or value > 0:
                eng.wait_ge(sem_, value)

        def turns(eng, body):
            for b in range(PAR):
                body(0, b)
            with eng.Fori(1, EXPERTS // PAR) as it:
                for b in range(PAR):
                    body(it, b)

        def experts_sp(sp):
            with sp.Fori(0, EXPERTS // PAR) as it:
                for b in range(PAR):
                    for j, src in enumerate(expert_weights(it * PAR + b)):
                        q = 3 * b + j
                        sp.wait_ge(unit_used, U_EXPERTS + it * (3 * PAR) + (q - RING + 1))
                        sp.dma_start(unit(q, src.shape[2]), src).then_inc(unit_loaded[q % RING], 16)

        def wait_expert_unit(eng, it, q):
            eng.wait_ge(unit_loaded[q % RING], it * (16 * 3 * PAR // RING) + 16 * (U_EXPERTS // RING + q // RING + 1))

        def gather(into, index):
            return nc.gpsimd.indirect_dma_start(out=E.x[0:CAP, into], out_offset=None, in_=normed_rows,
                                                in_offset=bass.IndirectOffsetOnAxis(ap=index[0:CAP, 0:1], axis=0),
                                                bounds_check=S - 1, oob_is_err=False)

        def scatter(frm, index):
            return nc.gpsimd.indirect_dma_start(out=expert_rows, out_offset=bass.IndirectOffsetOnAxis(ap=index[0:CAP, 1:2], axis=0),
                                                in_=E.y[0:CAP, frm], in_offset=None, bounds_check=2 * S - 1, oob_is_err=False)

        def experts_pool(pool):
            nc.gpsimd.memset(E.x[0:CAP], 0.0).then_inc(Z.cleared, 1)
            nc.gpsimd.tensor_copy(E.index[0:CAP, 0:2], E.table[0:CAP, 0:4].rearrange("p (e k) -> p e k", k=2)).then_inc(Z.index_copied, 1)
            pool.wait_ge(Z.cleared, 1)
            pool.wait_ge(Z.index_copied, 1)
            for b in range(2):
                gather(b, E.index[:, b]).then_inc(gathered[b], 16)

            def body(it, b):
                e = it * PAR + b
                wait_past(pool, scattered[b % 2], it * 32 + 16 * (b // 2))
                nc.gpsimd.tensor_copy(E.index[0:CAP, (b + 2) % 4], E.table[0:CAP, bass.ds(it * (2 * PAR) + 2 * (b + 2), 2)]).then_inc(Z.index_copied, 1)
                pool.wait_ge(Z.index_copied, e + 2)
                pool.wait_ge(Z.x_turned, e + 1)
                pool.sem_inc(Z.waits_passed, 1)
                gather(b % 2, E.index[:, (b + 2) % 4]).then_inc(gathered[b % 2], 16)
                pool.wait_ge(Z.y_act, e + 1)
                pool.wait_ge(Z.y_dve, e + 1)
                pool.sem_inc(Z.waits_passed, 1)
                scatter(b % 2, E.index[:, b % 4]).then_inc(scattered[b % 2], 16)
            turns(pool, body)
            for s_ in scattered:
                pool.wait_ge(s_, 16 * EXPERTS // 2)
            for s_ in gathered:
                pool.wait_ge(s_, 16 * (EXPERTS // 2 + 1))

        def turn_x(src):
            view = src[0:CAP].rearrange("k (p c) -> k c p", c=KC)
            for c in range(KC):
                ins = nc.tensor.transpose(ps[:, 0, c * CAP:(c + 1) * CAP], view[:, c, :], ident[0:CAP, 0:CAP])
            return ins

        def part_up(u, j, half, bank):
            high = E.high[j].rearrange("p (c n) -> p c n", c=KC)
            low = unit_low(u)
            res = []
            for c in range(4 * half, 4 * half + 4):
                for k, w in enumerate((high, low)):
                    res.append(nc.tensor.matmul(ps[:, bank, :], E.xs[:, c, :], w[:, c, :],
                                                start=(c == 0 and k == 0), stop=(c == KC - 1 and k == 1)))
            return res

        def fold(src, bank, chunks):
            view = src.rearrange("k (p c) -> k c p", c=FC)
            return [nc.tensor.matmul(ps[:, bank, c * CAP:(c + 1) * CAP], view[:, c, :], E.fold, start=True, stop=True) for c in chunks]

        def down_product(u, chunks):
            res = []
            for half in range(2):
                for c in chunks:
                    ins = nc.tensor.matmul(ps[0:CAP, 5 + half, :], E.hT[:, c, :], unit(u, D)[:, c, half * BANK:(half + 1) * BANK],
                                           start=(c == 0), stop=(c == FC - 1))
                res.append(ins)
            return res

        def quarter(q):
            return slice(q * (UNIT // 4), (q + 1) * (UNIT // 4))

        def split_high(u, j, q):
            nc.scalar.activation(E.high[j][:, quarter(q)], slot(u)[:, quarter(q)], ACT.Copy).then_inc(Z.w_high, 1)

        def split_low(u, j, q):
            nc.vector.tensor_tensor(ring_low[:, u % RING, quarter(q)], slot(u)[:, quarter(q)], E.high[j][:, quarter(q)].bitcast(F32),
                                    ALU.subtract).then_inc(Z.w_low, 1)

        def tokens_high():
            view = ps[:, 0, :].rearrange("p (c k) -> p c k", c=KC)
            return nc.scalar.activation(E.xs[:, :, 0:CAP], view, ACT.Copy)

        def tokens_low():
            view = ps[:, 0, :].rearrange("p (c k) -> p c k", c=KC)
            return nc.vector.tensor_tensor(E.xs[:, :, CAP:], view, E.xs[:, :, 0:CAP].bitcast(F32), ALU.subtract)

        def turned_bank(bank, half):
            return ps[:, bank, 0:HID // 2].rearrange("p (c k) -> p c k", c=FC)[:, 2 * half:2 * half + 2, :]

        UP_BANKS = (1, 7)

        def experts_pe(pe):
            pe.wait_ge(gathered[0], 16)
            turn_x(E.x[:, 0]).then_inc(Z.x_turned, 1)
            pe.wait_ge(Z.fold_made, 1)

            def body(it, b):
                e = it * PAR + b
                pe.wait_ge(Z.x_low, e + 1)
                for half in range(2):
                    pe.wait_ge(Z.w_low, e * 8 + 2 * half + 2)
                    gate = part_up(3 * b, 0, half, 2)
                gate[-1].then_inc(Z.gate_ready, 1)
                wait_past(pe, Z.up_kept, e * 2)
                for half in range(2):
                    pe.wait_ge(Z.w_low, e * 8 + 2 * half + 6)
                    up = part_up(3 * b + 1, 1, half, 3)
                    if half == 0:
                        up[0].then_inc(unit_used, 1)
                up[-1].then_inc(Z.up_ready, 1)
                pe.wait_ge(Z.gate_kept, e + 1)
                folded = fold(E.gate, 4, range(FC))
                folded[0].then_inc(unit_used, 1)
                folded[-1].then_inc(Z.gate_turned, 1)
                for half in range(2):
                    if half:
                        pe.wait_ge(gathered[(b + 1) % 2], it * 32 + 16 * ((b + 1) // 2 + 1))
                        pe.sem_inc(Z.pe_passed, 1)
                        turn_x(E.x[:, (b + 1) % 2]).then_inc(Z.x_turned, 1)
                    else:
                        pe.wait_ge(Z.up_kept, e * 2 + 2)
                    fold(E.up, UP_BANKS[half], range(2 * half, 2 * half + 2))[-1].then_inc(Z.up_turned, 1)
                wait_expert_unit(pe, it, 3 * b + 2)
                wait_past(pe, Z.y_act, e)
                wait_past(pe, Z.y_dve, e)
                for half in range(2):
                    pe.wait_ge(Z.hidden_ready, e * 2 + half + 1)
                    down = down_product(3 * b + 2, range(2 * half, 2 * half + 2))
                for ins in down:
                    ins.then_inc(Z.down_ready, 1)
                release_unit(pe)
            turns(pe, body)

        def experts_dve(v):
            nc.vector.tensor_tensor(E.fold, ident[:, 0:CAP], ident[:, CAP:], ALU.add).then_inc(Z.fold_made, 1)
            v.wait_ge(Z.x_high, 1)
            tokens_low().then_inc(Z.x_low, 1)

            def keep_y(it, b, e):
                v.wait_ge(Z.down_ready, e * 2)
                s_ = (b + 1) % 2
                wait_past(v, scattered[s_], it * 32 + 16 * ((b - 1) // 2))
                nc.vector.tensor_copy(E.y[0:CAP, s_, BANK:], ps[0:CAP, 6, :]).then_inc(Z.y_dve, 1)

            def body(it, b):
                e = it * PAR + b
                for j in range(2):
                    for q in range(4):
                        v.wait_ge(Z.w_high, e * 8 + 4 * j + q + 1)
                        split_low(3 * b + j, j, q)
                if not (isinstance(it, int) and e == 0):
                    keep_y(it, b, e)
                v.wait_ge(Z.up_ready, e + 1)
                wait_past(v, Z.up_turned, e * 2)
                for half in range(2):
                    cols = slice(half * HID // 2, (half + 1) * HID // 2)
                    nc.vector.tensor_copy(E.up[:, cols], ps[:, 3, cols]).then_inc(Z.up_kept, 1)
                wait_past(v, Z.down_ready, e * 2)
                for half in range(2):
                    if half:
                        v.wait_ge(Z.x_high, e + 2)
                        tokens_low().then_inc(Z.x_low, 1)
                    v.wait_ge(Z.up_turned, e * 2 + half + 1)
                    v.wait_ge(Z.silu_ready, e * 2 + half + 1)
                    nc.vector.tensor_tensor(E.hT[:, 2 * half:2 * half + 2, :], E.silu[:, 2 * half:2 * half + 2, :], turned_bank(UP_BANKS[half], half),
                                            ALU.mult).then_inc(Z.hidden_ready, 1)

            turns(v, body)
            keep_y(EXPERTS // PAR, 0, EXPERTS)

        def experts_act(a):
            a.wait_ge(Z.x_turned, 1)
            tokens_high().then_inc(Z.x_high, 1)

            def keep_y(it, b, e):
                a.wait_ge(Z.down_ready, e * 2 - 1)
                s_ = (b + 1) % 2
                wait_past(a, scattered[s_], it * 32 + 16 * ((b - 1) // 2))
                nc.scalar.activation(E.y[0:CAP, s_, 0:BANK], ps[0:CAP, 5, :], ACT.Copy).then_inc(Z.y_act, 1)

            def body(it, b):
                e = it * PAR + b
                for j in range(2):
                    wait_expert_unit(a, it, 3 * b + j)
                    for q in range(4):
                        split_high(3 * b + j, j, q)
                if not (isinstance(it, int) and e == 0):
                    keep_y(it, b, e)
                a.wait_ge(Z.gate_ready, e + 1)
                nc.scalar.activation(E.gate, ps[:, 2, :], ACT.Copy).then_inc(Z.gate_kept, 1)
                a.wait_ge(Z.gate_turned, e + 1)
                wait_past(a, Z.hidden_ready, e * 2)
                for half in range(2):
                    nc.scalar.activation(E.silu[:, 2 * half:2 * half + 2, :], turned_bank(4, half), ACT.Silu).then_inc(Z.silu_ready, 1)
                a.wait_ge(Z.x_turned, e + 2)
                tokens_high().then_inc(Z.x_high, 1)
            turns(a, body)
            keep_y(EXPERTS // PAR, 0, EXPERTS)

        def spills(eng, body):
            n = eng.value_load(spill_info[0:1, SPILL:SPILL + 1], min_val=0, max_val=SPILL)
            with eng.Fori(0, SPILL) as j:
                with eng.If(n > j):
                    body(j)
            return n

        def spill_sp(sp):
            sp.wait_ge(stage_open, STAGES_BEFORE_SPILL)

            def body(j):
                e = sp.value_load(spill_info[0:1, bass.ds(j, 1)], min_val=0, max_val=EXPERTS - 1)
                for q, src in enumerate(expert_weights(e)):
                    sp.dma_start(unit(q, src.shape[2]), src).then_inc(spill_loaded, 16)
                sp.wait_ge(spill_used, j + 1)
                sp.sem_inc(spill_next, 1)
            spills(sp, body)
            sp.wait_ge(stage_open, STAGES_BEFORE_SPILL + 1)

        def spill_pool(pool):
            def body(j):
                at = pool.snap(j * 2 + 2 * EXPERTS, min_val=2 * EXPERTS, max_val=2 * BLOCKS - 2)
                nc.gpsimd.tensor_copy(E.index[0:CAP, 0], E.table[0:CAP, bass.ds(at, 2)]).then_inc(Z.index_copied, 1)
                pool.wait_ge(Z.index_copied, j + 1)
                pool.sem_inc(Z.waits_passed, 1)
                gather(0, E.index[:, 0]).then_inc(spill_gathered, 16)
                pool.wait_ge(Z.y_act, j * 2 + 2)
                pool.sem_inc(Z.waits_passed, 1)
                scatter(0, E.index[:, 0]).then_inc(spill_scattered, 16)
                pool.wait_ge(spill_scattered, j * 16 + 16)
                pool.sem_inc(Z.waits_passed, 1)
            spills(pool, body)

        def spill_pe(pe):
            def body(j):
                pe.wait_ge(spill_gathered, j * 16 + 16)
                pe.sem_inc(Z.pe_passed, 1)
                turn_x(E.x[:, 0]).then_inc(Z.x_turned, 1)
                pe.wait_ge(Z.x_low, j + 1)
                pe.wait_ge(Z.w_low, j * 8 + 8)
                for half in range(2):
                    gate = part_up(0, 0, half, 2)
                gate[-1].then_inc(Z.gate_ready, 1)
                for half in range(2):
                    up = part_up(1, 1, half, 3)
                up[-1].then_inc(Z.up_ready, 1)
                pe.wait_ge(Z.gate_kept, j + 1)
                fold(E.gate, 4, range(FC))[-1].then_inc(Z.gate_turned, 1)
                pe.wait_ge(Z.up_kept, j + 1)
                fold(E.up, 1, range(FC))[-1].then_inc(Z.up_turned, 1)
                pe.wait_ge(Z.hidden_ready, j + 1)
                pe.wait_ge(spill_loaded, j * 48 + 48)
                for ins in down_product(2, range(FC)):
                    ins.then_inc(Z.down_ready, 1)
                pe.drain().then_inc(spill_used, 1)
            spills(pe, body)

        def spill_dve(v):
            def body(j):
                for k in range(2):
                    for q in range(4):
                        v.wait_ge(Z.w_high, j * 8 + 4 * k + q + 1)
                        split_low(k, k, q)
                v.wait_ge(Z.x_high, j + 1)
                tokens_low().then_inc(Z.x_low, 1)
                v.wait_ge(Z.up_ready, j + 1)
                nc.vector.tensor_copy(E.up, ps[:, 3, :]).then_inc(Z.up_kept, 1)
                v.wait_ge(Z.up_turned, j + 1)
                v.wait_ge(Z.silu_ready, j + 1)
                nc.vector.tensor_tensor(E.hT, E.silu, ps[:, 1, 0:FC * CAP].rearrange("p (c k) -> p c k", c=FC), ALU.mult).then_inc(Z.hidden_ready, 1)
            spills(v, body)

        def spill_act(a):
            def body(j):
                a.wait_ge(spill_loaded, j * 48 + 48)
                for k in range(2):
                    for q in range(4):
                        split_high(k, k, q)
                a.wait_ge(Z.x_turned, j + 1)
                tokens_high().then_inc(Z.x_high, 1)
                a.wait_ge(Z.gate_ready, j + 1)
                nc.scalar.activation(E.gate, ps[:, 2, :], ACT.Copy).then_inc(Z.gate_kept, 1)
                a.wait_ge(Z.gate_turned, j + 1)
                nc.scalar.activation(E.silu, ps[:, 4, 0:FC * CAP].rearrange("p (c k) -> p c k", c=FC), ACT.Silu).then_inc(Z.silu_ready, 1)
                for half in range(2):
                    a.wait_ge(Z.down_ready, j * 2 + half + 1)
                    nc.scalar.activation(E.y[0:CAP, 0, half * BANK:(half + 1) * BANK], ps[0:CAP, 5 + half, :], ACT.Copy).then_inc(Z.y_act, 1)
            spills(a, body)

        chosen_rows = Arena(arena)(NT, 2, D)

        def unite_dve(v, link):
            v.wait_ge(Z.more_loaded, 16)
            for k in range(2):
                for i in range(NT):
                    ins = nc.vector.scalar_tensor_tensor(out=h[:, i, :], in0=chosen_rows[:, i, k, :], scalar=gates[:, i, k:k + 1], in1=h[:, i, :],
                                                         op0=ALU.mult, op1=ALU.add)
                link(ins)
            norm_dve(v, link, h, rows[:, 1], h, squares=xn)

        U_LAYERS = U_EXPERTS + 3 * EXPERTS
        LAYER_UNITS = 24
        UP_PAIRS = 2
        DOWN_BLOCKS = KC
        assert U_LAYERS % RING == 0 and LAYER_UNITS % RING == 0

        class Y:
            lay = Arena(arena)
            qk = lay(4, S)
            mv = lay(NT, MH, DV + 1)
            mo = lay(NT, MH * DV)
            aqT = lay(4, S)
            akT = lay(S)
            av = lay(NT, 2 * DH)
            gates = lay(NT, 2 * MH)
            phase = lay.at
            conv = lay(2, S)
            rot = lay(2, BANK)
            rotk = lay(2, 2 * DH)
            tmp = lay(BANK)
            lay.at = phase
            w = lay(2, NT, S)
            li = lay(S)
            lf = lay(S)
            b = lay(S)
            top = lay(S)
            diag = lay(NT, P)
            assert lay.at <= 16340
            lay.at = phase
            masked = lay(2, BANK)
            probs = lay(2, BANK)
            turned = lay(2, BANK)
            res = lay(NT, BANK + 2 * HEADS)
            ff = Arena(arena)
            act = ff(FB, S)
            acc = ff(2, 2, S)
            assert ff.at <= 16340
            squares = Arena(arena)(NT, D)
            par = Arena(arena, 16340)
            fconv = par(2 * FB, FCONV)
            qconv = par(4, CONV)
            qbias = par(4)
            gbias = par(2 * MH)
            sinks = par(HEADS)
            mnorm = par(MH * DV)

        def layer_row(name, l):
            return t[name][bass.ds(l, 1)]

        def layer_units(l):
            def of(name):
                return t[name][bass.ds(l, 1)]
            w = of("w_in_2").rearrange("l (p c) n -> p (l c) n", c=KC)
            us = [(None, w[:, :, n * BANK:(n + 1) * BANK]) for n in range(3)]
            us += [(None, w[:, :, W_AQ:W_AQ + BANK]), (None, w[:, :, W_AK:W_AK + 4 * DH])]
            wo = of("w_out_2").rearrange("l (p c) n -> p (l c) n", c=KC)
            us += [(None, wo[:, :, n * BANK:(n + 1) * BANK]) for n in range(2)]
            wu = of("w_up_2").rearrange("l (p c) (s n) -> p (l c) s n", c=KC, s=2)
            cols = UP_PAIRS * P
            us += [("up", wu[:, :, :, n * cols:(n + 1) * cols]) for n in range(FB // UP_PAIRS)]
            wd = of("w_down_2").rearrange("l (b p) n -> p (l b) n", p=P)
            us += [(None, wd[:, b0:min(b0 + DOWN_BLOCKS, FB), half * BANK:(half + 1) * BANK])
                   for half in range(2) for b0 in range(0, FB, DOWN_BLOCKS)]
            assert len(us) == LAYER_UNITS
            return us

        Q_QK, Q_MV, Q_MO, Q_AQ, Q_AKV, Q_OUT, Q_UP, Q_DOWN = 0, 1, 2, 3, 4, 5, 7, 18

        def akv_unit():
            return slot(Q_AKV)[:, 0:KC * 4 * DH].rearrange("p (c n) -> p c n", c=KC)

        gate_w = slot(Q_AKV)[:, KC * 4 * DH:KC * (4 * DH + 2 * MH)].rearrange("p (c n) -> p c n", c=KC)

        def layers_sp(sp):
            with sp.Fori(0, LAYERS) as l:
                for q, (kind, src) in enumerate(layer_units(l)):
                    sp.wait_ge(unit_used, l * LAYER_UNITS + (U_LAYERS + q - RING + 1))
                    if kind == "up":
                        dst = slot(q).rearrange("p (c s n) -> p c s n", c=KC, s=2)
                    else:
                        n = src.shape[1] * src.shape[2]
                        dst = slot(q)[:, 0:n].rearrange("p (c n) -> p c n", c=src.shape[1])
                    if q == Q_AKV:
                        w = t["w_in_2"][bass.ds(l, 1)].rearrange("l (p c) n -> p (l c) n", c=KC)
                        sp.dma_start(gate_w, w[:, :, W_GATES:W_GATES + 2 * MH]).then_inc(gates_loaded, 16)
                        sp.dma_start(dst, src).then_inc(unit_loaded[q % RING], 16)
                    else:
                        sp.dma_start(dst, src).then_inc(unit_loaded[q % RING], 16)

        def load_layer(a, l):
            for n, name in enumerate(("g_pre_mix_2", "g_post_mix_2", "g_pre_ffn_2", "g_post_ffn_2")):
                a.dma_start(rows[:, n], layer_row(name, l).partition_broadcast(P)).then_inc(Z.rows_loaded, 16)
            for dst, name in ((Y.gbias, "gate_bias_2"), (Y.sinks, "attn_sinks_2"), (Y.mnorm, "mh_norm_g_2")):
                a.dma_start(dst, layer_row(name, l).partition_broadcast(P)).then_inc(Z.more_loaded, 16)
            for dst, name in ((Y.fconv, "ffn_conv_t"), (Y.qconv, "qk_conv_t")):
                a.dma_start(dst, layer_row(name, l).rearrange("l p b k -> (l p) b k")).then_inc(Z.more_loaded, 16)
            a.dma_start(Y.qbias, layer_row("qk_bias_t", l).rearrange("l p b -> (l p) b")).then_inc(Z.more_loaded, 16)

        def project_pe(pe, l):
            def taken(n):
                return (Z.taken_dve, n + 1) if n < 4 else (Z.taken_act, n - 3) if n < 12 else (Z.taken_dve, n - 7)

            def turn(n):
                m = n - 3 * NT
                pe.wait_ge(Z.roped, m + 1)
                if m >= 2:
                    pe.wait_ge(Z.turned_kept, m - 1)
                if n < 4 * NT:
                    for c in range(4):
                        ins = nc.tensor.transpose(ps[:, 4 + m % 2, c * P:(c + 1) * P], Y.rot[:, m % 2, c * P:(c + 1) * P], ident)
                else:
                    ins = nc.tensor.transpose(ps[:, 4 + m % 2, 0:P], Y.rotk[:, m % 2, :], ident)
                ins.then_inc(Z.turned, 1)

            for n in range(5 * NT):
                q, i = divmod(n, NT)
                if i == 0:
                    wait_unit(pe, q)
                if n >= 4:
                    pe.wait_ge(*taken(n - 4))
                if n == 4 * NT:
                    pe.wait_ge(gates_loaded, l * 16 + 16)
                for c in range(KC):
                    flags = dict(start=(c == 0), stop=(c == KC - 1))
                    if q == Q_QK:
                        ins = nc.tensor.matmul(ps[:, n % 4, :], unit(q)[:, c, i * P:(i + 1) * P], xnT[:, c, :], **flags)
                    elif q == Q_AKV:
                        ins = nc.tensor.matmul(ps[:, n % 4, 0:4 * DH], xnT[:, c, i * P:(i + 1) * P], akv_unit()[:, c, :], **flags)
                    else:
                        ins = nc.tensor.matmul(ps[:, n % 4, :], xnT[:, c, i * P:(i + 1) * P], unit(q)[:, c, :], **flags)
                if q == Q_AKV:
                    for c in range(KC):
                        ins = nc.tensor.matmul(ps[:, n % 4, 4 * DH:4 * DH + 2 * MH], xnT[:, c, i * P:(i + 1) * P], gate_w[:, c, :],
                                               start=(c == 0), stop=(c == KC - 1))
                ins.then_inc(Z.proj_ready, 1)
                if i == NT - 1:
                    release_unit(pe)
                if n - 1 >= 3 * NT:
                    turn(n - 1)
            turn(5 * NT - 1)

        def project_dve(v, link):
            for n in range(4):
                v.wait_ge(Z.weighted, n + 1)
                acc = Y.conv[:, n % 2]
                for back in range(1, CONV):
                    ins = nc.vector.scalar_tensor_tensor(out=acc[:, back:], in0=ps[:, n % 4, 0:S - back], scalar=Y.qconv[:, n, CONV - 1 - back:CONV - back],
                                                         in1=acc[:, back:], op0=ALU.mult, op1=ALU.add)
                    if back < CONV - 1:
                        link(ins)
                    else:
                        ins.then_inc(Z.taken_dve, 1)
            cos = table("cos_nat").rearrange("p (i d) -> p i d", i=NT)
            sin = table("sin_nat").rearrange("p (i d) -> p i d", i=NT)
            for m in range(2 * NT):
                n = 3 * NT + m
                i = m % NT
                v.wait_ge(Z.proj_ready, n + 1)
                if m >= 2:
                    v.wait_ge(Z.turned, m - 1)
                res = ps[:, n % 4, :]
                if m < NT:
                    dst, tmp, src, heads = Y.rot[:, m % 2], Y.tmp, res, HEADS
                else:
                    dst, tmp, src, heads = Y.rotk[:, m % 2], Y.tmp[:, 0:2 * DH], res[:, 0:2 * DH], 2
                    nc.vector.tensor_copy(Y.av[:, i], res[:, 2 * DH:4 * DH])
                    nc.vector.tensor_tensor(Y.gates[:, i], res[:, 4 * DH:4 * DH + 2 * MH], Y.gbias, ALU.add)
                rope(src, tmp, dst, cos[:, i], sin[:, i], heads, paired=True)
                v.wait_ge(Z.taken_dve, m + 5)
                nc.vector.tensor_tensor(dst, dst, tmp, ALU.add).then_inc(Z.roped, 1)
                v.wait_ge(Z.roped, m + 1)

        def project_act(a):
            def newest(n):
                a.wait_ge(Z.proj_ready, n + 1)
                nc.scalar.activation(Y.conv[:, n % 2], ps[:, n % 4, :], ACT.Identity, bias=Y.qbias[:, n:n + 1],
                                     scale=Y.qconv[:, n, CONV - 1:CONV]).then_inc(Z.weighted, 1)

            newest(0)
            for n in range(4):
                if n + 1 < 4:
                    if n >= 1:
                        a.wait_ge(Z.gated, n)
                    newest(n + 1)
                a.wait_ge(Z.taken_dve, n + 1)
                nc.scalar.activation(Y.qk[:, n], Y.conv[:, n % 2], ACT.Silu).then_inc(Z.gated, 1)
            for n in range(4, 12):
                i = n % 4
                a.wait_ge(Z.proj_ready, n + 1)
                if n < 8:
                    nc.scalar.activation(Y.mv[:, i, :, 0:DV], ps[:, i, :].rearrange("p (h d) -> p h d", h=MH), ACT.Copy).then_inc(Z.taken_act, 1)
                else:
                    nc.scalar.activation(Y.mo[:, i], ps[:, i, :], ACT.Sigmoid).then_inc(Z.taken_act, 1)
            for m in range(2 * NT):
                i = m % NT
                a.wait_ge(Z.turned, m + 1)
                bank = ps[:, 4 + m % 2, :]
                if m < NT:
                    nc.scalar.activation(Y.aqT[:, :, i * P:(i + 1) * P], bank.rearrange("p (c k) -> p c k", c=4), ACT.Copy,
                                         scale=DH ** -0.5).then_inc(Z.turned_kept, 1)
                else:
                    nc.scalar.activation(Y.akT[:, i * P:(i + 1) * P], bank[:, 0:P], ACT.Copy).then_inc(Z.turned_kept, 1)

        acol = small[:, 64:64 + NT * MH].rearrange("p (i h) -> p i h", i=NT)
        floor = small[:, 80:80 + NT * MH].rearrange("p (i h) -> p i h", i=NT)

        def mlstm_pe(pe):
            pe.wait_ge(Z.biased, 1)
            for x in range(2):
                for i in range(NT):
                    ins = nc.tensor.transpose(ps[0:MH, x, i * P:(i + 1) * P], Y.gates[:, i, x * MH:(x + 1) * MH], ident)
            ins.then_inc(Z.turned, 1)
            pe.wait_ge(Z.ranked, 1)
            for x, src in enumerate((Y.li, Y.lf)):
                for i in range(NT):
                    ins = nc.tensor.transpose(ps[:, 2 + x, i * MH:(i + 1) * MH], src[0:MH, i * P:(i + 1) * P], ident[0:MH, 0:MH])
            ins.then_inc(Z.turned, 1)
            pe.wait_ge(Z.placed, 1)
            pe.wait_ge(Z.exp_ready, 2)
            spread = table("spread").rearrange("p (h k) -> p h k", h=MH)

            def scores(n):
                r = half_of(n)
                if n:
                    pe.wait_ge(Z.strip_ready, n)
                nc.tensor.matmul(ps[:, 4, :], spread[0:MH, n, :], Y.top[0:MH, :], start=True, stop=True).then_inc(Z.strip_asked, 1)
                for kt in range(NT):
                    if kt >= 2:
                        pe.wait_ge(Z.scores_taken, NT * n + kt - 1)
                    elif n >= 2:
                        pe.wait_ge(Z.scores_taken, NT * (n - 2) + kt + 3)
                    nc.tensor.matmul(ps[:, 2 * (n % 2) + kt % 2, kt * P:], Y.qk[r, 2 + n // 2, kt * P:(kt + 1) * P], Y.qk[r, n // 2, kt * P:],
                                     start=True, stop=True).then_inc(Z.scores_ready, 1)

            scores(0)
            for n in range(MH):
                if n + 1 < MH:
                    scores(n + 1)
                pe.wait_ge(Z.scores_taken, NT * n + NT)
                if n:
                    pe.wait_ge(Z.mixed_taken, n)
                for i in range(NT):
                    for kt in range(i + 1):
                        ins = nc.tensor.matmul(ps[:, 5 + i // 2, (i % 2) * (DV + 1):(i % 2 + 1) * (DV + 1)], Y.w[:, n % 2, kt, i * P:(i + 1) * P],
                                               Y.mv[:, kt, n, :], start=(kt == 0), stop=(kt == i))
                ins.then_inc(Z.mixed_ready, 1)

        def mlstm_dve(v, link):
            work = [small[:, 96 + 16 * j:112 + 16 * j].rearrange("p (i h) -> p i h", i=NT) for j in range(3)]
            nc.vector.memset(Y.mv[:, :, :, DV:DV + 1], 1.0)
            nc.vector.memset(Y.top[0:MH], 0.0)
            lf = Y.gates[:, :, MH:]
            log_sigmoid_dve(v, link, lf, work, lf, done=Z.biased)
            v.wait_ge(Z.turned, 1)
            link(nc.vector.tensor_copy(Y.li[0:MH], ps[0:MH, 0, :]))
            link(nc.vector.tensor_copy(Y.lf[0:MH], ps[0:MH, 1, :]))
            link(nc.vector.tensor_tensor_scan(Y.b[0:MH], Y.lf[0:MH], Y.top[0:MH], 0.0, ALU.add, ALU.add))
            link(nc.vector.tensor_tensor(Y.li[0:MH], Y.li[0:MH], Y.b[0:MH], ALU.subtract))
            link(nc.vector.tensor_tensor_scan(Y.top[0:MH], Y.li[0:MH], Y.li[0:MH], 0.0, ALU.max, ALU.max))
            link(nc.vector.scalar_tensor_tensor(out=Y.lf[0:MH], in0=Y.b[0:MH], scalar=-1.0, in1=Y.top[0:MH], op0=ALU.mult, op1=ALU.subtract))
            nc.vector.tensor_scalar(Y.top[0:MH], Y.top[0:MH], -1.0, None, ALU.mult).then_inc(Z.ranked, 1)
            v.wait_ge(Z.turned, 2)
            nc.vector.tensor_copy(acol, ps[:, 2, 0:NT * MH].rearrange("p (i h) -> p i h", i=NT)).then_inc(Z.placed, 1)

            def mixed(n):
                v.wait_ge(Z.mixed_ready, n + 1)
                both = ps[:, 5:7, 0:2 * (DV + 1)].rearrange("p b (i d) -> p b i d", i=2)
                d = small[:, 144:148].rearrange("p (b i) -> p b i", b=2)
                fl = floor[:, :, n].rearrange("p (b i) -> p b i", b=2)
                den = both[:, :, :, DV]
                link(nc.vector.tensor_scalar(d, den, -1.0, None, ALU.mult))
                link(nc.vector.tensor_tensor(d, d, den, ALU.max))
                link(nc.vector.tensor_tensor(d, d, fl, ALU.max))
                link(nc.vector.reciprocal(d, d))
                y = [xn[:, i, n * DV:(n + 1) * DV] for i in range(NT)]
                for i in range(NT):
                    ins = nc.vector.tensor_scalar(y[i], both[:, i // 2, i % 2, 0:DV], small[:, 144 + i:145 + i], None, ALU.mult)
                ins.then_inc(Z.mixed_taken, 1)
                v.wait_ge(Z.mixed_taken, n + 1)
                for i in range(NT):
                    ins = nc.vector.tensor_tensor_reduce(out=Y.diag[:, i], in0=y[i], in1=y[i], scale=1.0, scalar=0.0, op0=ALU.mult, op1=ALU.add,
                                                         accum_out=small[:, 148 + i:149 + i])
                ins.then_inc(Z.moments, 1)
                v.wait_ge(Z.deviation, n + 1)
                link(nc.vector.reciprocal(small[:, 156:160], small[:, 152:156]))
                for i in range(NT):
                    ins = nc.vector.scalar_tensor_tensor(out=y[i], in0=y[i], scalar=small[:, 156 + i:157 + i], in1=Y.mnorm[:, n * DV:(n + 1) * DV],
                                                         op0=ALU.mult, op1=ALU.mult)
                link(ins)
                for i in range(NT):
                    ins = nc.vector.tensor_tensor(y[i], y[i], Y.mo[:, i, n * DV:(n + 1) * DV], ALU.mult)
                link(ins)

            for n in range(MH):
                v.wait_ge(Z.strip_asked, n + 1)
                nc.vector.tensor_tensor(Y.diag, ps[:, 4, :].rearrange("p (i k) -> p i k", i=NT),
                                        table("mask_causal_t")[:, None, :].to_broadcast([P, NT, P]), ALU.add).then_inc(Z.weighted, 1)
                v.wait_ge(Z.strip_ready, n + 1)
                for kt in range(NT):
                    v.wait_ge(Z.scores_ready, NT * n + kt + 1)
                    w = Y.w[:, n % 2, kt, kt * P:]
                    nc.vector.scalar_tensor_tensor(out=w, in0=ps[:, 2 * (n % 2) + kt % 2, kt * P:], scalar=DH ** -0.5, in1=w,
                                                   op0=ALU.mult, op1=ALU.mult).then_inc(Z.scores_taken, 1)
                if n:
                    mixed(n - 1)
            mixed(MH - 1)

        def mlstm_act(a):
            def deviation(n):
                a.wait_ge(Z.moments, n + 1)
                nc.scalar.activation(small[:, 152:156], small[:, 148:152], ACT.Sqrt, bias=table("eps"), scale=1.0 / DV).then_inc(Z.deviation, 1)

            work = small[:, 96:112]
            a.wait_ge(Z.exp_asked, 1)
            nc.scalar.activation(work, work, ACT.Exp).then_inc(Z.exp_ready, 1)
            a.wait_ge(Z.turned, 2)
            nc.scalar.activation(floor, ps[:, 3, 0:NT * MH].rearrange("p (i h) -> p i h", i=NT), ACT.Exp).then_inc(Z.exp_ready, 1)
            a.wait_ge(Z.placed, 1)
            for n in range(MH):
                a.wait_ge(Z.weighted, n + 1)
                if n >= 2:
                    a.wait_ge(Z.mixed_ready, n - 1)
                for kt in range(NT):
                    bias = acol[:, kt, n:n + 1]
                    ins = nc.scalar.activation(Y.w[:, n % 2, kt, kt * P:(kt + 1) * P], Y.diag[:, kt], ACT.Exp, bias=bias)
                    if kt < NT - 1:
                        ins = nc.scalar.activation(Y.w[:, n % 2, kt, (kt + 1) * P:], ps[:, 4, (kt + 1) * P:], ACT.Exp, bias=bias)
                ins.then_inc(Z.strip_ready, 1)
                if n:
                    deviation(n - 1)
            deviation(MH - 1)

        def window_chunks():
            res = []
            for i in range(NT):
                keys = [(slice(j * P, (j + 1) * P), j, P) for j in (i - 1, i) if j >= 0]
                res += [(i, slice(4 * g + j0, 4 * g + j0 + 2), keys, P if i == 0 else 0) for j0 in (0, 2) for g in range(2)]
            return res

        window = Attention(window_chunks(), table("mask_window"), lambda hh: Y.aqT[half_of(hh // 4), hh % 4, :],
                           lambda hh: Y.akT[half_of(hh // 4), :], lambda hh, vt: Y.av[:, vt, (hh // 4) * DH:(hh // 4 + 1) * DH],
                           Y.masked, Y.probs, Y.turned, Y.res, Y.sinks)

        def window_end_dve(v, link):
            m, d = Y.res[:, :, BANK:BANK + HEADS], Y.res[:, :, BANK + HEADS:]
            e = small[:, 64:96].rearrange("p (i h) -> p i h", i=NT)
            nc.vector.tensor_tensor(e, Y.sinks[:, None, :].to_broadcast([P, NT, HEADS]), m, ALU.subtract).then_inc(Z.exp_asked, 1)
            v.wait_ge(Z.exp_ready, 1)
            link(nc.vector.tensor_tensor(d, d, e, ALU.add))
            link(nc.vector.reciprocal(e, d))
            v.wait_ge(Z.mixed_taken, NT)
            for i in range(NT):
                nc.vector.tensor_tensor(xn[:, i, BANK:].rearrange("p (h d) -> p h d", d=DH), Y.res[:, i, 0:BANK].rearrange("p (h d) -> p h d", d=DH),
                                        e[:, i, :, None].to_broadcast([P, HEADS, DH]), ALU.mult)

        def window_end_act(a):
            a.wait_ge(Z.exp_asked, 1)
            nc.scalar.activation(small[:, 64:96], small[:, 64:96], ACT.Exp).then_inc(Z.exp_ready, 1)

        def branch_norm_dve(v, link, row, results):
            v.wait_ge(Z.taken_act, results)
            norm_dve(v, link, xn, row, xn, squares=Y.squares)
            for i in range(NT):
                v.wait_ge(Z.rows_ready, i + 1)
                nc.vector.tensor_tensor(h[:, i, :], h[:, i, :], xn[:, i, :], ALU.add)

        def up_pe(pe):
            for j in range(FB):
                q = Q_UP + j // UP_PAIRS
                w = slot(q).rearrange("p (c s b n) -> p c s b n", c=KC, s=2, b=UP_PAIRS)
                if j % UP_PAIRS == 0:
                    wait_unit(pe, q)
                for s_ in range(2):
                    n = 2 * j + s_
                    if n >= 8:
                        pe.wait_ge(Z.taken_dve, n - 7)
                    for c in range(KC):
                        ins = nc.tensor.matmul(ps[:, n % 8, :], w[:, c, s_, j % UP_PAIRS, :], xnT[:, c, :], start=(c == 0), stop=(c == KC - 1))
                    ins.then_inc(Z.proj_ready, 1)
                if j % UP_PAIRS == UP_PAIRS - 1:
                    release_unit(pe)

        def up_dve(v, link):
            for j in range(FB):
                for s_ in range(2):
                    n = 2 * j + s_
                    acc = Y.acc[:, j % 2, s_]
                    taps = Y.fconv[:, s_ * FB + j]
                    v.wait_ge(Z.weighted, n + 1)
                    link(nc.vector.scalar_tensor_tensor(out=acc[:, 1:], in0=ps[:, n % 8, 0:S - 1], scalar=taps[:, 1:2], in1=acc[:, 1:],
                                                        op0=ALU.mult, op1=ALU.add))
                    nc.vector.scalar_tensor_tensor(out=acc[:, 2:], in0=ps[:, n % 8, 0:S - 2], scalar=taps[:, 0:1], in1=acc[:, 2:],
                                                   op0=ALU.mult, op1=ALU.add).then_inc(Z.taken_dve, 1)
                v.wait_ge(Z.taken_dve, 2 * j + 2)
                v.wait_ge(Z.gated, j + 1)
                nc.vector.tensor_tensor(Y.act[:, j], Y.act[:, j], Y.acc[:, j % 2, 1], ALU.mult).then_inc(Z.rows_ready, 1)

        def up_act(a):
            def newest(n):
                j, s_ = divmod(n, 2)
                a.wait_ge(Z.proj_ready, n + 1)
                if j >= 2:
                    a.wait_ge(Z.rows_ready, j - 1)
                nc.scalar.activation(Y.acc[:, j % 2, s_], ps[:, n % 8, :], ACT.Copy, scale=Y.fconv[:, s_ * FB + j, FCONV - 1:FCONV]).then_inc(Z.weighted, 1)

            for j in range(FB):
                newest(2 * j)
                newest(2 * j + 1)
                a.wait_ge(Z.taken_dve, 2 * j + 1)
                nc.scalar.activation(Y.act[:, j], Y.acc[:, j % 2, 0], ACT.Silu).then_inc(Z.gated, 1)

        def down_pe(pe):
            for half in range(2):
                for b0 in range(0, FB, DOWN_BLOCKS):
                    q = Q_DOWN + 3 * half + b0 // DOWN_BLOCKS
                    wait_unit(pe, q)
                    for i in range(NT):
                        for b in range(b0, min(b0 + DOWN_BLOCKS, FB)):
                            ins = nc.tensor.matmul(ps[:, 4 * half + i, :], Y.act[:, b, i * P:(i + 1) * P], unit(q)[:, b - b0, :],
                                                   start=(b == 0), stop=(b == FB - 1))
                        if b == FB - 1:
                            ins.then_inc(Z.proj_ready, 1)
                    release_unit(pe)

        def keep_results_act(a, banks):
            for n in range(2 * NT):
                half, i = divmod(n, NT)
                a.wait_ge(Z.proj_ready, n + 1)
                nc.scalar.activation(xn[:, i, half * BANK:(half + 1) * BANK], ps[:, n % banks, :], ACT.Copy).then_inc(Z.taken_act, 1)

        STAGES_PER_LAYER = 8

        def layer_loop(eng, me, body):
            before = passed[me]
            with eng.Fori(0, LAYERS) as l:
                layer_base[me] = l * STAGES_PER_LAYER
                if me == "pe":
                    ring_turns["loaded"] = l * (16 * LAYER_UNITS // RING) + 16 * U_LAYERS // RING
                body(l)
            assert passed[me] == before + STAGES_PER_LAYER
            del layer_base[me]
            passed[me] += (LAYERS - 1) * STAGES_PER_LAYER

        U_ATT, U_REST = 0, 9

        STAGES_BEFORE_SPILL = 16

        def first_units():
            w = t["w_in"][0].rearrange("(p c) n -> p c n", c=KC)

            def w_in(j):
                return w[:, :, j * BANK:(j + 1) * BANK]

            wr = t["w_ret_branch"][0].rearrange("(p c) n -> p c n", c=KC)
            wo = t["w_out"][0].rearrange("(p c) n -> p c n", c=KC)
            us = [w_in(j * GROUPS + g) for g in range(GROUPS) for j in range(3)]
            us += [w_in(j) for j in (9, 10, 11, 12, 13, 14)]
            us += [t["w_attn_branch"][0].rearrange("(p c) n -> p c n", c=4), w_in(15), w_in(16)]
            for n in range(2):
                us += [wr[:, :, n * BANK:(n + 1) * BANK], w_in(17 + n)]
            us += [wo[:, :, n * BANK:(n + 1) * BANK] for n in range(2)]
            return us

        block = ctx.enter_context(nc.Block())

        @block.sync
        def _(sp):
            for u, src in enumerate(first_units()):
                if u >= RING:
                    sp.wait_ge(unit_used, u - RING + 1)
                sp.dma_start(unit(u, src.shape[2]), src).then_inc(unit_loaded[u % RING], 16)
            experts_sp(sp)
            spill_sp(sp)
            layers_sp(sp)

        @block.tensor
        def _(pe):
            def nxt():
                next_stage(pe, "pe")
            pe.wait_ge(consts_loaded, 80)
            turn_pe(pe, xn, KC, Z.rows_ready)
            nxt()
            for g in range(GROUPS):
                base = U_ATT + 3 * g
                vals = [(base + 2, SHIFTED[i]) for i in range(5)] if g == 0 else [(base + 2, tokens(i, True)) for i in range(NT)]
                heads_pe(pe, [base, base + 1], g > 0, vals)
                nxt()
                attend_pe(pe, dilated(g))
                nxt()
            view = C.o[0][:, :, 0:BANK]
            turn_pe(pe, view, 4, Z.rows_ready)
            nxt()
            heads_pe(pe, [9, 10], False, [(11 + n, tokens(i, False)) for n in range(2) for i in range(NT)])
            nxt()
            retain_pe(pe)
            nxt()
            jobs_pe(pe, tiles_jobs(13, xnT, "act") + tiles_jobs(14, xnT, "act"))
            turn_pe(pe, xn, KC, Z.rows_ready, bank0=4)
            nxt()
            jobs_pe(pe, merge_jobs())
            nxt()
            turn_pe(pe, xn, KC)
            pe.wait_ge(Z.turned_kept, 2 * NT)
            jobs_pe(pe, tiles_jobs(22, M.mT, "dve") + tiles_jobs(23, M.mT, "dve"))
            nxt()
            turn_pe(pe, xn, KC, Z.rows_ready)
            nxt()
            route_pe(pe)
            nxt()
            experts_pe(pe)
            nxt()
            spill_pe(pe)
            nxt()
            nxt()

            def layer(l):
                turn_pe(pe, xn, KC, Z.rows_ready)
                nxt()
                project_pe(pe, l)
                nxt()
                mlstm_pe(pe)
                nxt()
                attend_pe(pe, window)
                nxt()
                turn_pe(pe, xn, KC)
                pe.wait_ge(Z.turned_kept, 2 * NT)
                jobs_pe(pe, tiles_jobs(Q_OUT, xnT, "act") + tiles_jobs(Q_OUT + 1, xnT, "act"))
                nxt()
                turn_pe(pe, xn, KC, Z.rows_ready)
                nxt()
                up_pe(pe)
                nxt()
                down_pe(pe)
                nxt()
            layer_loop(pe, "pe", layer)

        @block.vector
        def _(v):
            link = Chain(v, Z.dve_chain)

            def nxt():
                next_stage(v, "dve", link)
            v.wait_ge(consts_loaded, 80)
            norm_dve(v, link, h, rows[:, 0], xn)
            nxt()
            for g in range(GROUPS):
                heads_dve(v, link, g > 0)
                nxt()
                attend_dve(v, link, dilated(g))
                nxt()
            combine_dve(v, link)
            nxt()
            heads_dve(v, link, False)
            nxt()
            retain_dve(v, link)
            nxt()
            gate_dve(v, 2)
            nxt()
            merge_dve(v)
            nxt()
            add_results_dve(v, h)
            nxt()
            v.wait_ge(Z.rows_loaded, 32)
            norm_dve(v, link, h, rows[:, 0], xn)
            nxt()
            route_dve(v, link)
            nxt()
            experts_dve(v)
            nxt()
            spill_dve(v)
            nxt()
            unite_dve(v, link)
            nxt()

            def layer(l):
                v.wait_ge(Z.rows_loaded, 64)
                norm_dve(v, link, h, rows[:, 0], xn)
                nxt()
                project_dve(v, link)
                nxt()
                mlstm_dve(v, link)
                nxt()
                attend_dve(v, link, window)
                window_end_dve(v, link)
                nxt()
                branch_norm_dve(v, link, rows[:, 1], 2 * NT)
                nxt()
                norm_dve(v, link, h, rows[:, 2], xn)
                nxt()
                up_dve(v, link)
                nxt()
                branch_norm_dve(v, link, rows[:, 3], 2 * NT)
                nxt()
            layer_loop(v, "dve", layer)

        @block.gpsimd
        def _(pool):
            def nxt():
                next_stage(pool, "pool")
            for _ in range(9):
                nxt()
            retain_pool(pool)
            nxt()
            for _ in range(4):
                nxt()
            route_pool(pool)
            nxt()
            experts_pool(pool)
            nxt()
            spill_pool(pool)
            nxt()
            nxt()

            def layer(l):
                for _ in range(STAGES_PER_LAYER):
                    nxt()
            layer_loop(pool, "pool", layer)

        @block.scalar
        def _(a):
            link = Chain(a, Z.act_chain)

            def nxt():
                next_stage(a, "act", link)
            a.dma_start(h[:, :, :], t["x"][0].rearrange("(i p) d -> p i d", p=P)).then_inc(consts_loaded, 16)
            a.dma_start(cst[:, :], const[:, 0:KEPT]).then_inc(consts_loaded, 16)
            a.dma_start(rows[:, 0], t["norm_mix_w"].partition_broadcast(P)).then_inc(consts_loaded, 16)
            a.dma_start(rows[:, 1], t["ret_gn_w"].partition_broadcast(P)).then_inc(consts_loaded, 16)
            a.dma_start(rows[:, 2:4].rearrange("p a n -> p (a n)"), t["b_branch_gate"].partition_broadcast(P)).then_inc(consts_loaded, 16)
            a.wait_ge(consts_loaded, 80)
            norm_act(a)
            turn_act(a, xnT, KC)
            nxt()
            for g in range(GROUPS):
                if g == 0:
                    dsts = [L.va[0:SHIFTED[i].stop - SHIFTED[i].start, i, :] for i in range(5)]
                else:
                    dsts = [L.va[:, i, :] for i in range(NT)]
                heads_act(a, (DH ** -0.5, 1.0), dsts)
                nxt()
                attend_act(a, dilated(g))
                if g:
                    leave_act(a, g)
                nxt()
            combine_act(a)
            nxt()
            heads_act(a, (1.0, DH ** -0.5), [L.vr[:, i, n * BANK:(n + 1) * BANK] for n in range(2) for i in range(NT)])
            nxt()
            retain_act(a)
            nxt()
            gate_act(a)
            turn_act(a, M.yT, KC, bank0=4)
            nxt()
            merge_act(a)
            nxt()
            turn_act(a, M.mT, KC)
            nxt()
            a.dma_start(rows[:, 0], t["norm_moe_w"].partition_broadcast(P)).then_inc(Z.rows_loaded, 16)
            a.dma_start(rows[:, 1], t["norm_final_w"].rearrange("(a n) -> a n", a=1).partition_broadcast(P)).then_inc(Z.rows_loaded, 16)
            norm_act(a)
            a.wait_ge(Z.rows_ready, NT)
            a.dma_start(normed_rows.rearrange("(i p) d -> p i d", p=P), xn[:, :, :]).then_inc(Z.stored, 16)
            turn_act(a, xnT, KC)
            load_routes(a)
            a.wait_ge(Z.stored, 16)
            nxt()
            route_act(a)
            nxt()
            experts_act(a)
            nxt()
            spill_act(a)
            nxt()
            a.dma_start(chosen_rows, expert_rows.rearrange("(i p k) d -> p i k d", p=P, k=2)).then_inc(Z.more_loaded, 16)
            norm_act(a)
            nxt()

            def layer(l):
                load_layer(a, l)
                norm_act(a)
                turn_act(a, xnT, KC)
                a.wait_ge(Z.more_loaded, 96)
                nxt()
                project_act(a)
                nxt()
                mlstm_act(a)
                nxt()
                attend_act(a, window)
                window_end_act(a)
                nxt()
                turn_act(a, xnT, KC)
                keep_results_act(a, 4)
                norm_act(a)
                nxt()
                norm_act(a)
                turn_act(a, xnT, KC)
                nxt()
                up_act(a)
                nxt()
                keep_results_act(a, 8)
                norm_act(a)
                nxt()
            layer_loop(a, "act", layer)
            a.dma_start(out[0].rearrange("(i p) d -> p i d", p=P), h[:, :, :]).then_inc(out_stored, 16)
            a.wait_ge(out_stored, 16)


def kernel(**inputs):
    import numpy as _np
    import concourse.bacc as _bacc
    from concourse import mybir as _mybir
    from concourse.bass_utils import run_bass_kernel_spmd as _run

    nc, arrays, out = launch_parts(inputs, _bacc, _mybir, _np)
    r = _run(nc, [arrays], core_ids=[0])
    return r.results[0]["out_dram"]


def launch_parts(inputs, _bacc, _mybir, _np):
    nc = _bacc.Bacc("TRN2", target_bir_lowering=False, num_devices=1)
    arrays, t = {}, {}
    for name in INPUTS:
        a = _np.ascontiguousarray(inputs[name])
        arrays[f"in_{name}"] = a
        t[name] = nc.dram_tensor(f"in_{name}", a.shape, _mybir.dt.from_np(a.dtype), kind="ExternalInput").ap()
    for name, frm in (("qk_conv_t", "qk_conv_w_2"), ("ffn_conv_t", "ffn_conv_w_2"), ("qk_bias_t", "qk_conv_b_2")):
        a = _np.asarray(inputs[frm])
        a = a.reshape(a.shape[:-1] + (-1, P))
        a = _np.ascontiguousarray(a.transpose(0, 3, 2, 1) if a.ndim == 4 else a.transpose(0, 2, 1))
        arrays[name] = a
        t[name] = nc.dram_tensor(name, a.shape, _mybir.dt.from_np(a.dtype), kind="ExternalInput").ap()
    arrays["tables"] = tables()
    const = nc.dram_tensor("tables", arrays["tables"].shape, F32, kind="ExternalInput").ap()
    out = nc.dram_tensor("out_dram", (1, S, D), F32, kind="ExternalOutput").ap()
    build(nc, t, const, out)
    return nc, arrays, out
```

```python
from contextlib import ExitStack

import numpy as np
import concourse.bass as bass
from concourse import mybir

F32 = mybir.dt.float32
F32R = mybir.dt.float32r
I32 = mybir.dt.int32
U32 = mybir.dt.uint32
ACT = mybir.ActivationFunctionType
ALU = mybir.AluOpType
AX = mybir.AxisListType

P = 128
D = 1024
S = 512
NT = S // P
KC = D // P
BANK = 512
UNIT = KC * BANK
RING = 4
EPS = 1e-6
NEG = -1e30

HEADS = 8
DH = 64
GROUPS = 3
HALF = 64
STRIDE = 4
DV = 128
STRIP = (2 * NT - 1) * P
EXPERTS = 64
EGROUPS = 8
PER_GROUP = EXPERTS // EGROUPS
HID = 512
FC = HID // P
ARENA = 17024
CAP = 32
SPILL = 2 * S // CAP - 1
BLOCKS = EXPERTS + SPILL
NO_ROW = 1 << 20
ROUTES = EGROUPS + EXPERTS

LAYERS = 2
MH = 4
CONV = 4
FCONV = 3
W_AK = 2056
W_GATES = 1536
W_AQ = 1544
FF = 2816
FB = FF // P

INPUTS = [
    "x", "norm_mix_w", "w_in", "b_branch_gate", "ret_decay_fwd", "ret_decay_bwd", "ret_gn_w",
    "w_attn_branch", "w_ret_branch", "w_out", "norm_moe_w", "moe_w_group", "moe_b_group",
    "moe_w_expert", "moe_b_expert", "moe_w1", "moe_w3", "moe_w2", "norm_final_w", "g_pre_mix_2",
    "w_in_2", "qk_conv_w_2", "qk_conv_b_2", "gate_bias_2", "mh_norm_g_2", "attn_sinks_2",
    "w_out_2", "g_post_mix_2", "g_pre_ffn_2", "w_up_2", "ffn_conv_w_2", "w_down_2", "g_post_ffn_2",
]

TABLES = {}


def tables():
    p = np.arange(P)[:, None]
    parts = {"ident": np.eye(P)}
    inv = (1.0 / (np.float32(10000.0) ** (np.arange(0, DH, 2, dtype=np.float32) / np.float32(DH)))).astype(np.float32)
    for name, token in (("nat", p + P * np.arange(NT)[None]), ("perm", STRIDE * p + np.arange(NT)[None])):
        ang = (token[:, :, None].astype(np.float32) * inv[None, None]).astype(np.float32)
        c, s = np.cos(ang), np.sin(ang)
        parts["cos_" + name] = np.concatenate([c, c], -1).reshape(P, -1)
        parts["sin_" + name] = np.concatenate([-s, s], -1).reshape(P, -1)
    j = np.arange(2 * P)[None]
    parts["mask_band"] = np.where(abs(j - HALF - p) <= HALF, 0, NEG)
    k = np.arange(P)[None]
    parts["mask_near"] = np.where(abs(k - p) <= HALF, 0, NEG)
    parts["mask_comb"] = np.where((k - p) % STRIDE == 0, 0, NEG)
    diff = p - (j - P)
    parts["mask_window"] = np.where((diff >= 0) & (diff < P), 0, NEG)
    parts["mask_causal_t"] = np.where(k >= p, 0, NEG)
    parts["before"] = (p < k) * 1.0
    parts["ones"] = np.ones((P, P))
    parts["expert_row"] = np.broadcast_to(np.arange(EXPERTS)[None], (P, EXPERTS))
    parts["token"] = p + P * np.arange(NT)[None]
    parts["eps"] = np.full((P, 1), EPS)
    parts["spread"] = np.repeat((p == np.arange(MH)[None]).astype(np.float32), P, axis=1)
    rel = np.arange(STRIP)[None] - (NT - 1) * P - p
    parts["rel"] = rel * np.ones((P, 1))
    at = 0
    for name, a in parts.items():
        TABLES[name] = (at, a.shape[1])
        at += a.shape[1]
    return np.ascontiguousarray(np.concatenate([np.asarray(a, np.float32) for a in parts.values()], 1))


CONST = tables().shape[1]
KEPT = TABLES["rel"][0]


class Arena:

    def __init__(self, whole, at=0):
        self.whole, self.at = whole, at

    def __call__(self, *shape):
        n = int(np.prod(shape))
        view = self.whole[:, self.at:self.at + n]
        self.at += n
        assert self.at <= self.whole.shape[1], self.at
        if len(shape) > 1:
            names = "abcd"[:len(shape)]
            view = view.rearrange(f"p ({' '.join(names)}) -> p {' '.join(names)}",
                                  **{x: m for x, m in zip(names, shape)})
        return view


def build(nc, t, const, out):
    ctx = ExitStack()
    with ctx:
        def sb(name, shape, dt=F32):
            return ctx.enter_context(nc.sbuf_tensor(name, shape, dt))

        stage_sems = {}

        def sem(name):
            return ctx.enter_context(nc.semaphore(name))

        stage_done = {me: sem("stage_done_" + me) for me in ("pe", "dve", "act")}
        stage_entered = {me: sem("stage_entered_" + me) for me in ("pe", "dve", "act", "pool")}
        stage_open = sem("stage_open")
        unit_loaded = [sem(f"unit_loaded{i}") for i in range(RING)]
        unit_used = sem("unit_used")
        consts_loaded = sem("consts_loaded")
        x_loaded = [sem(f"x_loaded{i}") for i in range(NT)]
        first_row_loaded = sem("first_row_loaded")
        mixer_rows_loaded = sem("mixer_rows_loaded")
        moe_rows_loaded = sem("moe_rows_loaded")
        normed_stored = sem("normed_stored")
        layer_loaded = sem("layer_loaded")
        chosen_loaded = [sem(f"chosen_loaded{i}") for i in range(NT)]
        sp_passed = sem("sp_passed")
        rows_sent = sem("rows_sent")
        half_high = sem("half_high")
        half_low = sem("half_low")
        spill_loaded = sem("spill_loaded")
        spill_used = sem("spill_used")
        spill_next = sem("spill_next")
        gates_loaded = sem("gates_loaded")
        out_stored = sem("out_stored")
        table_out = sem("table_out")
        gathered = [sem("gathered0"), sem("gathered1")]
        scattered = [sem("scattered0"), sem("scattered1")]
        spill_gathered = sem("spill_gathered")
        spill_scattered = sem("spill_scattered")

        STAGE = [
            "pe_chain", "dve_chain", "act_chain", "pool_chain",
            "rows_loaded", "row0_loaded", "more_loaded",
            "sums_ready", "roots_ready", "rows_ready", "turned", "turned_kept", "turned_low", "tile_added",
            "proj_ready", "taken_dve", "taken_act", "roped",
            "scores_ready", "scores_taken", "max_ready", "probs_ready", "probs_turned", "probs_kept",
            "mixed_ready", "mixed_taken", "spilled_out", "spilled_in", "exp_asked", "exp_ready",
            "strip_asked", "strip_ready", "weighted", "moments", "deviation", "gated",
            "biased", "cleared", "logits_ready", "chosen", "ranked", "placed", "table_in",
            "x_turned",
            "gate_ready", "silu_ready", "up_ready", "hidden_ready",
            "down_ready", "fold_made", "x_high", "x_low", "w_high", "w_low", "gate_kept", "up_kept",
            "gate_turned", "up_turned", "y_act", "y_dve", "index_copied", "waits_passed", "pe_passed",
        ]
        for name in STAGE:
            stage_sems[name] = sem(name)
        nums = [s.num for s in stage_sems.values()]
        assert nums == list(range(nums[0], nums[0] + len(nums)))
        Z = type("Sems", (), stage_sems)

        with ExitStack() as plain:
            ring = plain.enter_context(nc.sbuf_tensor("ring", [P, RING, UNIT], F32))
            xn = plain.enter_context(nc.sbuf_tensor("xn", [P, NT, D], F32))
            xnT = plain.enter_context(nc.sbuf_tensor("xnT", [P, KC, S], F32))
            rows = plain.enter_context(nc.sbuf_tensor("rows", [P, 4, D], F32))
            h = plain.enter_context(nc.sbuf_tensor("h", [P, NT, D], F32))
            arena = plain.enter_context(nc.sbuf_tensor("arena", [P, ARENA], F32))
        ring_r = sb("ring_r", [P, RING, UNIT], F32R)
        xn_r = sb("xn_r", [P, NT * D], F32R)
        xnT_r = sb("xnT_r", [P, KC * S], F32R)
        rows_r = sb("rows_r", [P, 4 * D], F32R)
        h_r = sb("h_r", [P, NT * D], F32R)
        arena_r = sb("arena_r", [P, ARENA], F32R)
        cst = sb("cst", [P, KEPT])
        small = sb("small", [P, 512])
        ps = ctx.enter_context(nc.psum_tensor("ps", [P, 8, BANK], F32))

        def table(name):
            at, n = TABLES[name]
            return cst[:, at:at + n]

        ident = table("ident")

        class Chain:

            def __init__(self, eng, done):
                self.eng, self.done, self.n = eng, done, 0

            def __call__(self, ins):
                self.n += 1
                ins.then_inc(self.done, 1)
                self.eng.wait_ge(self.done, self.n)

        passed = {}
        layer_base = {}

        def next_stage(eng, me, chain=None):
            n = passed.get(me, 0)
            passed[me] = n + 1
            if me in layer_base:
                n = layer_base[me] + n
            if me == "pool":
                for done in stage_done.values():
                    eng.wait_ge(done, n + 1)
                eng.sem_inc(stage_entered[me], 1)
                eng.sem_clear(range(nums[0], nums[-1] + 1))
                eng.drain().then_inc(stage_open, 1)
            else:
                eng.drain().then_inc(stage_done[me], 1)
                eng.wait_ge(stage_open, n + 1)
                eng.sem_inc(stage_entered[me], 1)
            if chain:
                chain.n = 0

        def slot(u):
            return ring[:, u % RING]

        def unit_low(u, cols=BANK):
            return ring_r[:, u % RING].rearrange("p (c n) -> p c n", n=cols)

        def unit(u, cols=BANK):
            return slot(u)[:, 0:UNIT].rearrange("p (c n) -> p c n", n=cols)

        current = {"l": None}
        FIRST_LOADS = (12, 12, 0, 0)

        def unit_size(q):
            return KC * (4 * DH + 2 * MH) if current["l"] is not None and q == Q_AKV else UNIT

        def unit_quarter(q, part):
            n = unit_size(q) // 4
            return slice(part * n, (part + 1) * n)

        def quarter_count(q, part):
            n = 4 * q + part + 1
            return n if current["l"] is None else current["l"] * (4 * SPLIT) + (4 * FIRST_UNITS + n)

        def high_act(a, q):
            if current["l"] is None:
                a.wait_ge(unit_loaded[q % 2], 16 * (q // 2 + 1))
                if q >= 2:
                    a.wait_ge(unit_used, q - 1)
            else:
                wait_layer_unit(a, q)
                if q == Q_AKV:
                    a.wait_ge(gates_loaded, current["l"] * 16 + 16)
                a.wait_ge(unit_used, current["l"] * LAYER_UNITS + (U_LAYERS + q - 1))
            for part in range(4):
                cols = unit_quarter(q, part)
                nc.scalar.activation(ring_r[:, 2 + q % 2, cols], ring[:, q % 2, cols], ACT.Copy).then_inc(half_high, 1)

        def low_pool(pool, q):
            for part in range(4):
                cols = unit_quarter(q, part)
                pool.wait_ge(half_high, quarter_count(q, part))
                nc.gpsimd.tensor_tensor(ring_r[:, q % 2, cols], ring[:, q % 2, cols], ring_r[:, 2 + q % 2, cols].bitcast(F32),
                                        ALU.subtract).then_inc(half_low, 1)

        def wait_halves(pe, q, part):
            pe.wait_ge(half_low, quarter_count(q, part))

        def halves(q):
            return ring_r[:, 2 + q % 2], ring_r[:, q % 2]

        def chunks_of_unit(q, cols=BANK):
            return [w.rearrange("p (c n) -> p c n", n=cols) for w in halves(q)]

        def passes(xs, ws, weights_left=False):
            pairs = [(xs[0], ws[0]), (xs[1], ws[0]), (xs[0], ws[1])]
            return [(w, x) if weights_left else (x, w) for x, w in pairs]

        def products(bank, xs, ws, weights_left=False, start=True, stop=True):
            for k, (left, right) in enumerate(passes(xs, ws, weights_left)):
                ins = nc.tensor.matmul(bank, left, right, start=(start and k == 0), stop=(stop and k == 2))
            return ins

        def release_unit(pe):
            pe.drain().then_inc(unit_used, 1)

        def norm_dve(v, link, src, row, dst, squares=None, loaded=None, row_loaded=None):
            ss = small[:, 0:NT]
            rstd = small[:, 8:8 + NT]
            for i in range(NT):
                if loaded:
                    v.wait_ge(loaded[i], 16)
                ins = nc.vector.tensor_tensor_reduce(out=(dst if squares is None else squares)[:, i, :], in0=src[:, i, :], in1=src[:, i, :], scale=1.0,
                                                     scalar=0.0, op0=ALU.mult, op1=ALU.add, accum_out=ss[:, i:i + 1])
            ins.then_inc(Z.sums_ready, 1)
            v.wait_ge(Z.roots_ready, 1)
            if row_loaded:
                v.wait_ge(row_loaded, 16)
            link(nc.vector.reciprocal(rstd, small[:, 4:4 + NT]))
            for i in range(NT):
                nc.vector.scalar_tensor_tensor(out=dst[:, i, :], in0=src[:, i, :], scalar=rstd[:, i:i + 1], in1=row,
                                               op0=ALU.mult, op1=ALU.mult).then_inc(Z.rows_ready, 1)

        def norm_act(a):
            a.wait_ge(Z.sums_ready, 1)
            nc.scalar.activation(small[:, 4:4 + NT], small[:, 0:NT], ACT.Sqrt, bias=table("eps"),
                                 scale=1.0 / D).then_inc(Z.roots_ready, 1)

        def tile_norm_dve(link, src, row, dst, i, base):
            rstd = small[:, base + 8 + i:base + 9 + i]
            link(nc.vector.reciprocal(rstd, small[:, base + 4 + i:base + 5 + i]))
            return nc.vector.scalar_tensor_tensor(out=dst[:, i, :], in0=src[:, i, :], scalar=rstd, in1=row, op0=ALU.mult, op1=ALU.mult)

        BRANCH, NEXT = 0, 12

        def tile_roots_act(a, src, scratch, ready=None):
            for i in range(NT):
                if ready is not None:
                    a.wait_ge(ready, i + 1)
                nc.scalar.activation(scratch[:, i, :], src[:, i, :], ACT.Square, accum_out=small[:, i:i + 1]).then_inc(Z.sums_ready, 1)
                a.wait_ge(Z.sums_ready, i + 1)
                nc.scalar.activation(small[:, 4 + i:5 + i], small[:, i:i + 1], ACT.Sqrt, bias=table("eps"), scale=1.0 / D).then_inc(Z.roots_ready, 1)

        def tile_norms_dve(v, link, src, row, dst, row_loaded=None):
            if row_loaded:
                v.wait_ge(row_loaded, 16)
            for i in range(NT):
                v.wait_ge(Z.roots_ready, i + 1)
                tile_norm_dve(link, src, row, dst, i, 0).then_inc(Z.rows_ready, 1)

        def finish_act(a, src, banks, has_next, then=None):
            count = 0

            def root(x, i, base):
                nonlocal count
                nc.scalar.activation(Y.squares[:, count % 2], x[:, i, :], ACT.Square, accum_out=small[:, base + i:base + i + 1]).then_inc(Z.sums_ready, 1)
                count += 1
                a.wait_ge(Z.sums_ready, count)
                nc.scalar.activation(small[:, base + 4 + i:base + 5 + i], small[:, base + i:base + i + 1], ACT.Sqrt, bias=table("eps"),
                                     scale=1.0 / D).then_inc(Z.roots_ready, 1)

            def next_root(i):
                a.wait_ge(Z.tile_added, i + 1)
                root(h, i, NEXT)
            for n in range(2 * NT):
                half, i = divmod(n, NT)
                a.wait_ge(Z.proj_ready, n + 1)
                nc.scalar.activation(src[:, i, half * BANK:(half + 1) * BANK], ps[:, n % banks, :], ACT.Copy).then_inc(Z.taken_act, 1)
                if then:
                    then(n)
                if half:
                    a.wait_ge(Z.taken_act, n + 1)
                    root(src, i, BRANCH)
                    if has_next and i:
                        next_root(i - 1)
            if has_next:
                next_root(NT - 1)

        def finish_dve(v, link, src, row, next_row, dst):
            roots = 0

            def next_norm(i):
                v.wait_ge(Z.roots_ready, roots)
                tile_norm_dve(link, h, next_row, dst, i, NEXT)
            for i in range(NT):
                roots += 1
                v.wait_ge(Z.roots_ready, roots)
                link(tile_norm_dve(link, src, row, src, i, BRANCH))
                nc.vector.tensor_tensor(h[:, i, :], h[:, i, :], src[:, i, :], ALU.add).then_inc(Z.tile_added, 1)
                if next_row is not None and i:
                    roots += 1
                    next_norm(i - 1)
            if next_row is not None:
                roots += 1
                next_norm(NT - 1)

        def turn_pe(pe, src, chunks, ready=None, bank0=0, emptied=None, before=0):
            n = 0
            for i in range(NT):
                if ready is not None:
                    pe.wait_ge(ready, i + 1)
                view = src[:, i, :].rearrange("k (p c) -> k c p", c=chunks)
                for c0 in range(0, chunks, 4):
                    if n >= 4:
                        pe.wait_ge(emptied or Z.turned_kept, before + n - 3)
                    for c in range(4):
                        ins = nc.tensor.transpose(ps[:, bank0 + n % 4, c * P:(c + 1) * P], view[:, c0 + c, :], ident)
                    ins.then_inc(Z.turned, 1)
                    n += 1

        def turn_act(a, dst, chunks, bank0=0, before=0):
            n = 0
            for i in range(NT):
                for c0 in range(0, chunks, 4):
                    a.wait_ge(Z.turned, before + n + 1)
                    nc.scalar.activation(dst[:, c0:c0 + 4, i * P:(i + 1) * P],
                                         ps[:, bank0 + n % 4, :].rearrange("p (c k) -> p c k", c=4),
                                         ACT.Copy).then_inc(Z.turned_kept, 1)
                    n += 1

        def turn_low_dve(v, dst, low, bank0=0, in_place=True):
            n = 0
            for i in range(NT):
                for c0 in range(0, dst.shape[1], 4):
                    v.wait_ge(Z.turned_kept, n + 1)
                    if in_place:
                        v.wait_ge(Z.turned, 2 * i + 2)
                    nc.vector.tensor_tensor(low(slice(c0, c0 + 4), i), ps[:, bank0 + n % 4, :].rearrange("p (c k) -> p c k", c=4),
                                            dst[:, c0:c0 + 4, i * P:(i + 1) * P].bitcast(F32), ALU.subtract).then_inc(Z.turned_low, 1)
                    n += 1

        def xn_low_of(chunks, i):
            return xn_low[:, i, chunks, :]

        h_low = h_r.rearrange("p (c t) -> p c t", c=KC)

        def h_low_of(chunks, i):
            return h_low[:, chunks, i * P:(i + 1) * P]

        xn_low = xn_r.rearrange("p (i c k) -> p i c k", i=NT, c=KC)
        xnT_high = xnT_r.rearrange("p (c t) -> p c t", c=KC)

        def tokens(i, permuted):
            return slice(i, S, STRIDE) if permuted else slice(i * P, (i + 1) * P)

        def heads_pe(pe, units, permuted, values):
            jobs = [(units[j], tokens(i, permuted)) for j in range(2) for i in range(NT)] + values

            def turn(n):
                pe.wait_ge(Z.roped, n + 1)
                if n >= 2:
                    pe.wait_ge(Z.turned_kept, n - 1)
                for c in range(4):
                    ins = nc.tensor.transpose(ps[:, 4 + n % 2, c * P:(c + 1) * P], L.rot[:, n % 2, c * P:(c + 1) * P], ident)
                ins.then_inc(Z.turned, 1)

            for n, (u, toks) in enumerate(jobs):
                first = n == 0 or jobs[n - 1][0] != u
                if 4 <= n < 12:
                    pe.wait_ge(Z.taken_dve, n - 3)
                elif n >= 12:
                    pe.wait_ge(Z.taken_act, n - 11)
                rows_out = len(range(*toks.indices(S)))
                for c in range(KC):
                    if first and c % 2 == 0:
                        wait_halves(pe, u, c // 2)
                    ins = products(ps[0:rows_out, n % 4, :], (xnT_high[:, c, toks], h_low[:, c, toks]), [w[:, c, :] for w in chunks_of_unit(u)],
                                   start=(c == 0), stop=(c == KC - 1))
                ins.then_inc(Z.proj_ready, 1)
                if n + 1 == len(jobs) or jobs[n + 1][0] != u:
                    release_unit(pe)
                if 1 <= n <= 8:
                    turn(n - 1)

        def rope(src, tmp, dst, cos, sin, heads, paired=False):
            half = DH // 2
            to = "p (c g d) -> p g c d" if paired else "p (g c d) -> p g c d"
            s4 = src.rearrange("p (g c d) -> p g c d", g=2, d=DH)
            t4 = tmp.rearrange(to, g=2, d=DH)
            d4 = dst.rearrange(to, g=2, d=DH)

            def over(x):
                return x[:, None, None, :].to_broadcast([P, 2, heads // 2, x.shape[1]])
            nc.vector.tensor_tensor(t4[:, :, :, 0:half], s4[:, :, :, half:DH], over(sin[:, 0:half]), ALU.mult)
            nc.vector.tensor_tensor(t4[:, :, :, half:DH], s4[:, :, :, 0:half], over(sin[:, half:DH]), ALU.mult)
            nc.vector.tensor_tensor(d4, s4, over(cos), ALU.mult).then_inc(Z.taken_dve, 1)

        def heads_dve(v, permuted):
            cos = table("cos_perm" if permuted else "cos_nat").rearrange("p (i d) -> p i d", i=NT)
            sin = table("sin_perm" if permuted else "sin_nat").rearrange("p (i d) -> p i d", i=NT)
            for n in range(2 * NT):
                v.wait_ge(Z.proj_ready, n + 1)
                if n >= 2:
                    v.wait_ge(Z.turned, n - 1)
                rope(ps[:, n % 4, :], L.tmp, L.rot[:, n % 2, :], cos[:, n % NT], sin[:, n % NT], HEADS)
                v.wait_ge(Z.taken_dve, n + 1)
                nc.vector.tensor_tensor(L.rot[:, n % 2, :], L.rot[:, n % 2, :], L.tmp, ALU.add).then_inc(Z.roped, 1)
                if n + 1 < 2 * NT:
                    v.wait_ge(Z.roped, n + 1)

        def heads_act(a, scales, values, split):
            def between(n):
                if n in split and split[n] is None:
                    combine_act(a)
                elif n in split:
                    high_act(a, split[n])

            between(-1)
            for n in range(2 * NT):
                dst = (L.qT, L.kT)[n // NT]
                a.wait_ge(Z.turned, n + 1)
                nc.scalar.activation(dst[:, :, (n % NT) * P:(n % NT + 1) * P],
                                     ps[:, 4 + n % 2, :].rearrange("p (c k) -> p c k", c=4), ACT.Copy,
                                     scale=scales[n // NT]).then_inc(Z.turned_kept, 1)
                between(n)
            for j, dst in enumerate(values):
                n = 2 * NT + j
                a.wait_ge(Z.proj_ready, n + 1)
                nc.scalar.activation(dst, ps[0:dst.shape[0], n % 4, :], ACT.Copy).then_inc(Z.taken_act, 1)
                between(n)

        class L:
            lay = Arena(arena)
            qT = lay(4, S)
            kT = lay(4, S)
            v = lay(4096)
            va = v[:, 0:5 * BANK].rearrange("p (i n) -> p i n", n=BANK)
            vr = v.rearrange("p (i n) -> p i n", n=D)
            o = lay(NT, BANK + 2 * HEADS)
            again = lay.at
            rot = lay(2, BANK)
            tmp = lay(BANK)
            rotated = lay.at
            lay.at = again
            og = lay(NT, BANK + 2 * HEADS)
            masked = lay(2, BANK)
            probs = lay(2, BANK)
            turned = lay(2, BANK)

        SHIFTED = [slice(max(0, i * P - HALF), min(S, i * P + HALF)) for i in range(NT + 1)]

        def chunks_of(g):
            res = []
            for i in range(NT):
                if g == 0:
                    keys = [(SHIFTED[j], j, SHIFTED[j].stop - SHIFTED[j].start) for j in (i, i + 1)]
                    m0 = keys[0][0].start - (i * P - HALF)
                    res += [(i, slice(h0, h0 + 3, 2), keys, m0) for h0 in (0, 1, 4, 5)]
                else:
                    res += [(i, slice(h0, HEADS, 2), [(slice(i * P, (i + 1) * P), i, P)], 0) for h0 in (0, 1)]
            return res

        class Attention:

            def __init__(self, chunks, mask, q, k, val, masked, probs, turned, res, sinks=None):
                self.chunks, self.mask, self.q, self.k, self.val, self.sinks = chunks, mask, q, k, val, sinks
                self.masked, self.probs, self.turned, self.res = masked, probs, turned, res
                self.per_tile = len(chunks) // NT

        def attend_pe(pe, A):
            def scores(n):
                i, heads, keys, _ = A.chunks[n]
                if n >= 2:
                    pe.wait_ge(Z.scores_taken, n - 1)
                k0, k1 = keys[0][0].start, keys[-1][0].stop
                for j, hh in enumerate(range(*heads.indices(HEADS))):
                    ins = nc.tensor.matmul(ps[:, n % 2, j * (k1 - k0):(j + 1) * (k1 - k0)], A.q(hh)[:, i * P:(i + 1) * P],
                                           A.k(hh)[:, k0:k1], start=True, stop=True)
                ins.then_inc(Z.scores_ready, 1)

            def turn(n):
                i, heads, keys, _ = A.chunks[n]
                pe.wait_ge(Z.probs_ready, n + 1)
                if n >= 2:
                    pe.wait_ge(Z.probs_kept, n - 1)
                wide = keys[-1][0].stop - keys[0][0].start
                b = 0
                for j in range(len(range(*heads.indices(HEADS)))):
                    at = 0
                    for _, _, m in keys:
                        ins = nc.tensor.transpose(ps[0:m, 2 + n % 2, b * P:(b + 1) * P],
                                                  A.probs[:, n % 2, j * wide + at:j * wide + at + m], ident)
                        at += m
                        b += 1
                ins.then_inc(Z.probs_turned, 1)

            def values(n):
                i, heads, keys, _ = A.chunks[n]
                pe.wait_ge(Z.probs_kept, n + 1)
                if n % A.per_tile == 0 and i >= 2:
                    pe.wait_ge(Z.mixed_taken, i - 1)
                b = 0
                for hh in range(*heads.indices(HEADS)):
                    for x, (_, vt, m) in enumerate(keys):
                        ins = nc.tensor.matmul(ps[:, 4 + i % 2, hh * DH:(hh + 1) * DH], A.turned[0:m, n % 2, b * P:(b + 1) * P],
                                               A.val(hh, vt)[0:m], start=(x == 0), stop=(x == len(keys) - 1))
                        b += 1
                ins.then_inc(Z.mixed_ready, 1)

            scores(0)
            for n in range(len(A.chunks)):
                if n + 1 < len(A.chunks):
                    scores(n + 1)
                turn(n)
                if n:
                    values(n - 1)
            values(len(A.chunks) - 1)

        def attend_dve(v, link, A):
            def keep_turned(n):
                i, heads, keys, _ = A.chunks[n]
                nh = len(range(*heads.indices(HEADS)))
                v.wait_ge(Z.probs_turned, n + 1)
                if n >= 2:
                    v.wait_ge(Z.mixed_ready, n - 1)
                into = A.turned[:, n % 2, :].rearrange("p (b k) -> p b k", k=P)
                frm = ps[:, 2 + n % 2, :].rearrange("p (b k) -> p b k", k=P)
                blocks = nh * len(keys)
                if len({mm for _, _, mm in keys}) > 1:
                    for x, (_, _, mm) in enumerate(keys):
                        ins = nc.vector.tensor_copy(into[0:mm, x:blocks:len(keys), :], frm[0:mm, x:blocks:len(keys), :])
                else:
                    ins = nc.vector.tensor_copy(into[:, 0:blocks], frm[:, 0:blocks])
                ins.then_inc(Z.probs_kept, 1)

            for n, (i, heads, keys, m0) in enumerate(A.chunks):
                nh = len(range(*heads.indices(HEADS)))
                wide = keys[-1][0].stop - keys[0][0].start
                m = A.res[:, i, BANK:BANK + HEADS][:, heads]
                v.wait_ge(Z.scores_ready, n + 1)
                if n >= 2:
                    v.wait_ge(Z.probs_ready, n - 1)
                s = A.masked[:, n % 2, 0:nh * wide].rearrange("p (h k) -> p h k", h=nh)
                nc.vector.tensor_tensor(s, ps[:, n % 2, 0:nh * wide].rearrange("p (h k) -> p h k", h=nh),
                                        A.mask[:, None, m0:m0 + wide].to_broadcast([P, nh, wide]), ALU.add).then_inc(Z.scores_taken, 1)
                v.wait_ge(Z.scores_taken, n + 1)
                link(nc.vector.tensor_reduce(m, s, AX.X, ALU.max))
                if A.sinks is not None:
                    link(nc.vector.tensor_tensor(m, m, A.sinks[:, heads], ALU.max))
                nc.vector.tensor_scalar(small[:, 16 + 8 * (n % 2):16 + 8 * (n % 2) + nh], m, -1.0, None, ALU.mult).then_inc(Z.max_ready, 1)
                if n:
                    keep_turned(n - 1)
            keep_turned(len(A.chunks) - 1)

        def attend_act(a, A):
            for n, (i, heads, keys, _) in enumerate(A.chunks):
                wide = keys[-1][0].stop - keys[0][0].start
                a.wait_ge(Z.max_ready, n + 1)
                if n >= 2:
                    a.wait_ge(Z.probs_turned, n - 1)
                for j, hh in enumerate(range(*heads.indices(HEADS))):
                    ins = nc.scalar.activation(A.probs[:, n % 2, j * wide:(j + 1) * wide], A.masked[:, n % 2, j * wide:(j + 1) * wide],
                                               ACT.Exp, bias=small[:, 16 + 8 * (n % 2) + j:17 + 8 * (n % 2) + j],
                                               accum_out=A.res[:, i, BANK + HEADS + hh:BANK + HEADS + hh + 1])
                ins.then_inc(Z.probs_ready, 1)
                if n % A.per_tile == 1 and i:
                    a.wait_ge(Z.mixed_ready, n - 1)
                    nc.scalar.activation(A.res[:, i - 1, 0:BANK], ps[:, 4 + (i - 1) % 2, :], ACT.Copy).then_inc(Z.mixed_taken, 1)
            a.wait_ge(Z.mixed_ready, len(A.chunks))
            nc.scalar.activation(A.res[:, NT - 1, 0:BANK], ps[:, 4 + (NT - 1) % 2, :], ACT.Copy).then_inc(Z.mixed_taken, 1)

        def half_of(n):
            return slice(DH * (n % 2), DH * (n % 2) + DH)

        def dilated(g):
            return Attention(chunks_of(g), table(("mask_band", "mask_near", "mask_comb")[g]),
                             lambda hh: L.qT[half_of(hh), hh // 2, :], lambda hh: L.kT[half_of(hh), hh // 2, :],
                             lambda hh, vt: L.va[:, vt, hh * DH:(hh + 1) * DH],
                             L.masked, L.probs, L.turned, L.o if g == 0 else L.og)

        spilled = nc.dram_tensor("attn_spill", (2, S, BANK + 2 * HEADS), F32).ap()

        def leave_act(a, g):
            a.wait_ge(Z.mixed_taken, NT)
            a.dma_start(spilled[g - 1].rearrange("(p i) n -> p i n", i=NT), L.og).then_inc(Z.spilled_out, 16)
            a.wait_ge(Z.spilled_out, 16)

        class C:
            lay = Arena(arena)
            lay.at = L.rotated
            o = [None, lay(NT, BANK + 2 * HEADS), lay(NT, BANK + 2 * HEADS)]
            yT = Arena(arena, 13184)(4, S)
        C.o[0] = L.o

        def combine_load_act(a):
            for g in (1, 2):
                a.dma_start(C.o[g], spilled[g - 1].rearrange("(i p) n -> p i n", p=P)).then_inc(Z.spilled_in, 16)

        def combine_act(a):
            a.wait_ge(Z.exp_asked, 1)
            e = small[:, 64:64 + 3 * NT * HEADS]
            nc.scalar.activation(e, e, ACT.Exp).then_inc(Z.exp_ready, 1)

        def combine_dve(v, link):
            n = NT * HEADS
            top = small[:, 32:64]
            e = [small[:, 64 + g * n:64 + (g + 1) * n].rearrange("p (i h) -> p i h", i=NT) for g in range(GROUPS)]
            m = [C.o[g][:, :, BANK:BANK + HEADS] for g in range(GROUPS)]
            d = [C.o[g][:, :, BANK + HEADS:] for g in range(GROUPS)]
            top = top.rearrange("p (i h) -> p i h", i=NT)
            den = small[:, 192:192 + n].rearrange("p (i h) -> p i h", i=NT)
            v.wait_ge(Z.spilled_in, 32)
            link(nc.vector.tensor_tensor(top, m[0], m[1], ALU.max))
            link(nc.vector.tensor_tensor(top, top, m[2], ALU.max))
            for g in range(GROUPS):
                ins = nc.vector.tensor_tensor(e[g], m[g], top, ALU.subtract)
            ins.then_inc(Z.exp_asked, 1)
            v.wait_ge(Z.exp_ready, 1)
            for g in range(GROUPS):
                ins = nc.vector.tensor_tensor(d[g], d[g], e[g], ALU.mult)
            link(ins)
            link(nc.vector.tensor_tensor(den, d[0], d[1], ALU.add))
            link(nc.vector.tensor_tensor(den, den, d[2], ALU.add))
            link(nc.vector.reciprocal(den, den))
            for g in range(GROUPS):
                ins = nc.vector.tensor_tensor(e[g], e[g], den, ALU.mult)
            link(ins)
            for i in range(NT):
                for g in range(GROUPS):
                    o3 = C.o[g][:, i, 0:BANK].rearrange("p (h d) -> p h d", d=DH)
                    ins = nc.vector.tensor_tensor(o3, o3, e[g][:, i, :, None].to_broadcast([P, HEADS, DH]), ALU.mult)
                link(ins)
                link(nc.vector.tensor_tensor(C.o[0][:, i, 0:BANK], C.o[0][:, i, 0:BANK], C.o[1][:, i, 0:BANK], ALU.add))
                nc.vector.tensor_tensor(C.o[0][:, i, 0:BANK], C.o[0][:, i, 0:BANK], C.o[2][:, i, 0:BANK], ALU.add).then_inc(Z.rows_ready, 1)

        def log_sigmoid_dve(v, link, x, w, out, done=None):
            e, z, z2 = w
            link(nc.vector.tensor_scalar(e, x, -1.0, None, ALU.mult))
            nc.vector.tensor_tensor(e, e, x, ALU.min).then_inc(Z.exp_asked, 1)
            v.wait_ge(Z.exp_ready, 1)
            link(nc.vector.tensor_scalar(z, e, 2.0, None, ALU.add))
            link(nc.vector.reciprocal(z, z))
            link(nc.vector.tensor_tensor(z, z, e, ALU.mult))
            link(nc.vector.tensor_tensor(z2, z, z, ALU.mult))
            link(nc.vector.tensor_scalar(e, z2, 1.0 / 17, None, ALU.mult))
            for n in (15, 13, 11, 9, 7, 5, 3):
                link(nc.vector.scalar_tensor_tensor(out=e, in0=e, scalar=1.0 / n, in1=z2, op0=ALU.add, op1=ALU.mult))
            link(nc.vector.scalar_tensor_tensor(out=e, in0=e, scalar=1.0, in1=z, op0=ALU.add, op1=ALU.mult))
            link(nc.vector.tensor_scalar(z, x, 0.0, None, ALU.min))
            ins = nc.vector.scalar_tensor_tensor(out=out, in0=e, scalar=-2.0, in1=z, op0=ALU.mult, op1=ALU.add)
            if done is None:
                link(ins)
            else:
                ins.then_inc(done, 1)

        class R:
            lay = Arena(arena, 8192)
            w = lay(2, NT, S)
            rel = lay(STRIP)
            assert lay.at <= 13184
            lay.at = 15232
            strip = lay(2, STRIP)
            decay = small[:, 240:256]
            neg = small[:, 256:264]
            mid = small[:, 384:512]

        def retain_pool(pool):
            lo, hi = (NT - 1) * P, NT * P
            pool.wait_ge(Z.more_loaded, 16)
            pool.wait_ge(Z.biased, 1)
            chain = Chain(pool, Z.pool_chain)
            for n in range(HEADS):
                if n:
                    pool.wait_ge(Z.strip_ready, n)
                if n >= 2:
                    pool.wait_ge(Z.scores_taken, NT * (n - 1))
                f = R.strip[:, n % 2]
                gf, gb = R.decay[:, n:n + 1], R.neg[:, n:n + 1]
                nc.gpsimd.tensor_scalar(f[:, 0:lo], R.rel[:, 0:lo], gb, None, ALU.mult)
                nc.gpsimd.tensor_scalar(f[:, hi:], R.rel[:, hi:], gf, None, ALU.mult)
                nc.gpsimd.tensor_scalar(f[:, lo:hi], R.rel[:, lo:hi], 0.0, gf, ALU.max, ALU.mult)
                chain(nc.gpsimd.tensor_scalar(R.mid, R.rel[:, lo:hi], 0.0, gb, ALU.min, ALU.mult))
                nc.gpsimd.tensor_tensor(f[:, lo:hi], f[:, lo:hi], R.mid, ALU.add).then_inc(Z.strip_asked, 1)
                pool.wait_ge(Z.exp_ready, n + 2)
                chain(nc.gpsimd.tensor_tensor(R.mid, ident, f[:, lo:hi], ALU.mult))
                nc.gpsimd.tensor_tensor(f[:, lo:hi], f[:, lo:hi], R.mid, ALU.add).then_inc(Z.strip_ready, 1)

        def retain_pe(pe):
            def scores(n, key_tiles):
                r = slice(DH * (n % 2), DH * (n % 2) + DH)
                for kt in key_tiles:
                    if kt >= 2:
                        pe.wait_ge(Z.scores_taken, NT * n + kt - 1)
                    elif n >= 2:
                        pe.wait_ge(Z.scores_taken, NT * (n - 2) + kt + 3)
                    nc.tensor.matmul(ps[:, 2 * (n % 2) + kt % 2, :], L.kT[r, n // 2, kt * P:(kt + 1) * P], L.qT[r, n // 2, :],
                                     start=True, stop=True).then_inc(Z.scores_ready, 1)

            scores(0, range(NT))
            for n in range(HEADS):
                if n + 1 < HEADS:
                    scores(n + 1, (0, 1))
                pe.wait_ge(Z.scores_taken, NT * n + NT)
                if n >= 2:
                    pe.wait_ge(Z.mixed_taken, n - 1)
                for i in range(NT):
                    for kt in range(NT):
                        ins = nc.tensor.matmul(ps[:, 4 + n % 2, i * P:(i + 1) * P], R.w[:, n % 2, kt, i * P:(i + 1) * P],
                                               L.vr[:, kt, n * DV:(n + 1) * DV], start=(kt == 0), stop=(kt == NT - 1))
                ins.then_inc(Z.mixed_ready, 1)
                if n + 1 < HEADS:
                    scores(n + 1, (2, 3))

        def retain_dve(v, link):
            v.wait_ge(Z.rows_loaded, 32)
            w = [small[:, 264 + 16 * j:280 + 16 * j] for j in range(3)]
            log_sigmoid_dve(v, link, R.decay, w, R.decay)
            nc.vector.tensor_scalar(R.neg, R.decay[:, HEADS:], -1.0, None, ALU.mult).then_inc(Z.biased, 1)
            lo = (NT - 1) * P

            def normed(n):
                v.wait_ge(Z.mixed_ready, n + 1)
                stats = small[:, 320:344].rearrange("p (i s) -> p i s", i=NT)
                mv = small[:, 344:352].rearrange("p (i s) -> p i s", i=NT)
                std = small[:, 352:356]
                for i in range(NT):
                    ins = nc.vector.bn_stats(stats[:, i, :], ps[:, 4 + n % 2, i * P:(i + 1) * P])
                link(ins)
                for i in range(NT):
                    ins = nc.vector.bn_aggr(mv[:, i, :], stats[:, i, :])
                ins.then_inc(Z.moments, 1)
                v.wait_ge(Z.deviation, n + 1)
                link(nc.vector.reciprocal(small[:, 356:360], std))
                for i in range(NT):
                    ins = nc.vector.tensor_scalar(xn[:, i, n * DV:(n + 1) * DV], ps[:, 4 + n % 2, i * P:(i + 1) * P],
                                                  mv[:, i, 0:1], small[:, 356 + i:357 + i], ALU.subtract, ALU.mult)
                ins.then_inc(Z.mixed_taken, 1)

            for n in range(HEADS):
                v.wait_ge(Z.strip_ready, n + 1)
                if n >= 2:
                    v.wait_ge(Z.mixed_ready, n - 1)
                for kt in range(NT):
                    v.wait_ge(Z.scores_ready, NT * n + kt + 1)
                    nc.vector.tensor_tensor(R.w[:, n % 2, kt, :], ps[:, 2 * (n % 2) + kt % 2, :],
                                            R.strip[:, n % 2, lo - kt * P:lo - kt * P + S], ALU.mult).then_inc(Z.scores_taken, 1)
                if n:
                    normed(n - 1)
            normed(HEADS - 1)

        def retain_act(a):
            a.dma_start(R.decay[:, 0:HEADS], t["ret_decay_fwd"].partition_broadcast(P)).then_inc(Z.rows_loaded, 16)
            a.dma_start(R.decay[:, HEADS:], t["ret_decay_bwd"].partition_broadcast(P)).then_inc(Z.rows_loaded, 16)
            at, n_rel = TABLES["rel"]
            a.dma_start(R.rel, const[:, at:at + n_rel]).then_inc(Z.more_loaded, 16)
            a.wait_ge(Z.exp_asked, 1)
            nc.scalar.activation(small[:, 264:280], small[:, 264:280], ACT.Exp).then_inc(Z.exp_ready, 1)

            def strip(n):
                a.wait_ge(Z.strip_asked, n + 1)
                nc.scalar.activation(R.strip[:, n % 2], R.strip[:, n % 2], ACT.Exp).then_inc(Z.exp_ready, 1)

            strip(0)
            strip(1)
            for n in range(HEADS):
                if n + 2 < HEADS:
                    strip(n + 2)
                a.wait_ge(Z.moments, n + 1)
                nc.scalar.activation(small[:, 352:356], small[:, 345:352:2], ACT.Sqrt, bias=table("eps")).then_inc(Z.deviation, 1)

        def jobs_pe(pe, jobs):
            for n, (u, pairs, _) in enumerate(jobs):
                first = n == 0 or jobs[n - 1][0] != u
                if n >= 4:
                    who = jobs[n - 4][2]
                    count = sum(j[2] == who for j in jobs[:n - 3])
                    pe.wait_ge(Z.taken_dve if who == "dve" else Z.taken_act, count)
                for c, (left, right) in enumerate(pairs):
                    if first and 4 * c % len(pairs) == 0:
                        wait_halves(pe, u, 4 * c // len(pairs))
                    ins = nc.tensor.matmul(ps[:, n % 4, 0:right.shape[1]], left, right, start=(c == 0), stop=(c == len(pairs) - 1))
                ins.then_inc(Z.proj_ready, 1)
                if n + 1 == len(jobs) or jobs[n + 1][0] != u:
                    release_unit(pe)

        def tiles_jobs(u, src, taker, chunks=KC, parts=(0,), cols=BANK):
            ws = chunks_of_unit(u, cols)
            return [(u, [x for c in range(chunks) for x in passes([y[:, c, i * P:(i + 1) * P] for y in src], [w[:, c, n * BANK:(n + 1) * BANK] for w in ws])], taker)
                    for n in parts for i in range(NT)]

        class M:
            lay = Arena(arena_r)
            yT = (lay(KC, S), lay(KC, S))
            mT = yT
            at = lay.at
            lay = Arena(arena, at)
            part = lay(NT, BANK)
            at = lay.at
            assert at + 4 * S <= 13184
            aT = (Arena(arena_r, at)(4, S), Arena(arena_r, 13184)(4, S))
            gate = Arena(arena, 15232)(2, BANK)
            xT = (xnT_high, h_low)

        def low_of(low):
            return lambda chunks, i: low[:, chunks, i * P:(i + 1) * P]

        def gate_dve(v):
            v.wait_ge(Z.probs_ready, 1)
            nc.vector.tensor_tensor(M.aT[1], C.yT, M.aT[0].bitcast(F32), ALU.subtract)
            for n in range(2 * NT):
                half, i = divmod(n, NT)
                x = xn[:, i, half * BANK:(half + 1) * BANK]
                nc.vector.tensor_tensor(x, x, rows[:, 1, half * BANK:(half + 1) * BANK], ALU.mult).then_inc(Z.weighted, 1)
                v.wait_ge(Z.weighted, n + 1)
                v.wait_ge(Z.taken_act, n + 1)
                ins = nc.vector.tensor_tensor(x, x, M.gate[:, n % 2], ALU.mult)
                ins.then_inc(Z.gated if half == 0 else Z.rows_ready, 1)

        def gate_act(a):
            nc.scalar.activation(M.aT[0], C.yT, ACT.Copy).then_inc(Z.probs_ready, 1)
            high_act(a, U_GATE + 1)
            for n in range(2 * NT):
                a.wait_ge(Z.proj_ready, n + 1)
                if n >= 2:
                    m = n - 1
                    a.wait_ge(Z.gated, min(m, NT))
                    if m > NT:
                        a.wait_ge(Z.rows_ready, m - NT)
                nc.scalar.activation(M.gate[:, n % 2], ps[:, n % 4, :], ACT.Silu).then_inc(Z.taken_act, 1)
                if n == 5:
                    high_act(a, U_GATE + 2)

        U_GATE, U_MERGE, U_MIXED, FIRST_UNITS = 13, 15, 22, 24

        def merge_jobs():
            u = U_MERGE
            jobs = tiles_jobs(u, M.aT, "act", chunks=4, parts=(0, 1), cols=D)
            for n in range(2):
                jobs += tiles_jobs(u + 1 + n, M.xT, "dve")
            for n in range(2):
                jobs += tiles_jobs(u + 3 + 2 * n, M.yT, "act")
                jobs += tiles_jobs(u + 4 + 2 * n, M.xT, "dve")
            return jobs

        def merge_dve(v):
            gates = [n for n, j in enumerate(merge_jobs()) if j[2] == "dve"]
            for k, n in enumerate(gates):
                ret = n >= 16
                half, i = (k // NT) % 2, k % NT
                col = (BANK * half) + (D if ret else 0)
                brow = rows[:, 2:4].rearrange("p a n -> p (a n)")[:, col:col + BANK]
                x = xn[:, i, half * BANK:(half + 1) * BANK]
                v.wait_ge(Z.proj_ready, n + 1)
                nc.vector.tensor_tensor(M.gate[:, k % 2], ps[:, n % 4, :], brow, ALU.add).then_inc(Z.taken_dve, 1)
                v.wait_ge(Z.gated, k + 1)
                if not ret:
                    if k == 0:
                        v.wait_ge(Z.taken_act, 2 * NT)
                    nc.vector.tensor_tensor(x, x, M.gate[:, k % 2], ALU.mult).then_inc(Z.weighted, 1)
                else:
                    if i == 0:
                        v.wait_ge(Z.taken_act, 2 * NT + NT * (half + 1))
                    nc.vector.tensor_tensor(M.gate[:, k % 2], M.gate[:, k % 2], M.part[:, i], ALU.mult).then_inc(Z.rows_ready, 1)
                    v.wait_ge(Z.rows_ready, k - 2 * NT + 1)
                    nc.vector.tensor_tensor(x, x, M.gate[:, k % 2], ALU.add).then_inc(Z.weighted, 1)
                v.wait_ge(Z.weighted, k + 1)

        def merge_act(a):
            k = 0
            copies = 0
            high_act(a, U_MERGE + 1)
            for n, job in enumerate(merge_jobs()):
                if n > 2 * NT and n % NT == 2:
                    high_act(a, job[0] + 1)
                if job[2] == "act":
                    a.wait_ge(Z.proj_ready, n + 1)
                    if n < 2 * NT:
                        half, i = divmod(n, NT)
                        dst = xn[:, i, half * BANK:(half + 1) * BANK]
                    else:
                        i = copies % NT
                        dst = M.part[:, i]
                        if copies >= 3 * NT:
                            a.wait_ge(Z.rows_ready, i + 1)
                    nc.scalar.activation(dst, ps[:, n % 4, :], ACT.Copy).then_inc(Z.taken_act, 1)
                    copies += 1
                else:
                    a.wait_ge(Z.taken_dve, k + 1)
                    nc.scalar.activation(M.gate[:, k % 2], M.gate[:, k % 2], ACT.Sigmoid).then_inc(Z.gated, 1)
                    k += 1

        def add_results_dve(v, dst):
            for n in range(2 * NT):
                half, i = divmod(n, NT)
                x = dst[:, i, half * BANK:(half + 1) * BANK]
                v.wait_ge(Z.proj_ready, n + 1)
                nc.vector.tensor_tensor(x, x, ps[:, n % 4, :], ALU.add).then_inc(Z.taken_dve, 1)

        normed_rows = nc.dram_tensor("normed_rows", (S, D), F32).ap()
        slot_table = nc.dram_tensor("slot_table", (CAP * BLOCKS, 2), I32).ap()
        expert_rows = nc.dram_tensor("expert_rows", (2 * S, D), F32).ap()
        gates = small[:, 400:400 + 2 * NT].rearrange("p (i k) -> p i k", k=2)
        spill_info = small[:, 408:408 + SPILL + 1].bitcast(I32)

        class G:
            lay = Arena(arena)
            w = lay(KC, ROUTES)
            bias = lay(ROUTES)
            logits = lay(NT, ROUTES)
            by_group = lay(NT, EXPERTS)
            group_is = lay(NT, EGROUPS)
            in_group = lay(NT, PER_GROUP)
            best = lay(NT, 8)
            best_at = lay(NT, 8).bitcast(U32)
            group = lay(NT)
            e_at = lay(NT, 2)
            num = lay(NT, EGROUPS)
            one = lay(NT)
            is_expert = [lay(NT, EXPERTS), lay(NT, EXPERTS)]
            either = lay(NT, EXPERTS)
            rank = lay(NT, EXPERTS)
            part = lay(NT, EXPERTS)
            place = lay(NT, EXPERTS)
            count = lay(EXPERTS)
            further = lay(EXPERTS)
            cum = lay(EXPERTS)
            first = lay(EXPERTS)
            tmp = lay(EXPERTS)
            le = lay(SPILL + 1, EXPERTS)
            spill = lay(SPILL + 1)
            slot = lay(NT, 2)
            slot_i = lay(NT, 2).bitcast(I32)
            pair = lay(NT, 2, 2)
            pair_i = lay(NT, 2, 2).bitcast(I32)
            empty = lay(2 * BLOCKS).bitcast(I32)

        def load_routes(a):
            a.dma_start(G.w[:, :, 0:EGROUPS], t["moe_w_group"][0].rearrange("(p c) n -> p c n", c=KC)).then_inc(Z.more_loaded, 16)
            a.dma_start(G.w[:, :, EGROUPS:], t["moe_w_expert"][0].rearrange("(p c) n -> p c n", c=KC)).then_inc(Z.more_loaded, 16)
            a.dma_start(G.bias[:, 0:EGROUPS], t["moe_b_group"].partition_broadcast(P)).then_inc(Z.more_loaded, 16)
            a.dma_start(G.bias[:, EGROUPS:], t["moe_b_expert"].partition_broadcast(P)).then_inc(Z.more_loaded, 16)

        def route_pe(pe):
            for i in range(NT):
                for c in range(KC):
                    ins = nc.tensor.matmul(ps[:, i, 0:ROUTES], xnT[:, c, i * P:(i + 1) * P], G.w[:, c, :], start=(c == 0), stop=(c == KC - 1))
            ins.then_inc(Z.logits_ready, 1)
            pe.wait_ge(Z.chosen, 1)
            for i in range(NT):
                nc.tensor.matmul(ps[:, 4 + i % 2, (i // 2) * EXPERTS:(i // 2 + 1) * EXPERTS], table("before"), G.either[:, i, :], start=True, stop=(i == 0))
                for j in range(i):
                    nc.tensor.matmul(ps[:, 4 + i % 2, (i // 2) * EXPERTS:(i // 2 + 1) * EXPERTS], table("ones"), G.either[:, j, :], start=False, stop=(j == i - 1))
            for j in range(NT):
                ins = nc.tensor.matmul(ps[:, 6, 0:EXPERTS], table("ones"), G.either[:, j, :], start=(j == 0), stop=(j == NT - 1))
            ins.then_inc(Z.ranked, 1)

        def route_act(a):
            a.wait_ge(Z.exp_asked, 1)
            nc.scalar.activation(G.num, G.num, ACT.Exp).then_inc(Z.exp_ready, 1)
            a.wait_ge(Z.exp_asked, 2)
            nc.scalar.activation(G.one, G.one, ACT.Exp).then_inc(Z.exp_ready, 1)
            a.wait_ge(table_out, 16 * (2 * NT + 1))
            a.dma_start(E.table[0:CAP], slot_table.rearrange("(p b) k -> p (b k)", p=CAP)).then_inc(Z.table_in, 16)
            a.wait_ge(Z.table_in, 16)

        def whole_blocks(link, dst, src):
            link(nc.vector.tensor_scalar(dst, src, 1.0 / CAP, 0.5 / CAP - 0.5, ALU.mult, ALU.add))
            link(nc.vector.tensor_scalar(dst, dst, 1.5 * 2 ** 23, None, ALU.add))
            link(nc.vector.tensor_scalar(dst, dst, -1.5 * 2 ** 23, None, ALU.add))

        def route_dve(v, link):
            def over(x, n, w):
                return x.to_broadcast([P, n, w])
            v.wait_ge(Z.logits_ready, 1)
            link(nc.vector.tensor_tensor(G.logits, ps[:, 0:NT, 0:ROUTES], G.bias[:, None, :].to_broadcast([P, NT, ROUTES]), ALU.add))
            lg = G.logits[:, :, 0:EGROUPS]
            for i in range(NT):
                ins = nc.vector.max(G.best[:, i, :], lg[:, i, :])
            link(ins)
            for i in range(NT):
                nc.vector.max_index(G.best_at[:, i, :], G.best[:, i, :], lg[:, i, :])
            ins = nc.vector.tensor_tensor(G.num, lg, G.best[:, :, 0:1].to_broadcast([P, NT, EGROUPS]), ALU.subtract)
            ins.then_inc(Z.exp_asked, 1)
            v.wait_ge(Z.exp_asked, 1)
            link(nc.vector.tensor_copy(G.group[:, :, None], G.best_at[:, :, 0:1]))
            erow = table("expert_row")
            link(nc.vector.tensor_tensor(G.group_is, erow[:, None, 0:EGROUPS].to_broadcast([P, NT, EGROUPS]),
                                         G.group[:, :, None].to_broadcast([P, NT, EGROUPS]), ALU.is_equal))
            for i in range(NT):
                ins = nc.vector.tensor_tensor(G.by_group[:, i, :].rearrange("p (g e) -> p g e", g=EGROUPS),
                                              G.logits[:, i, EGROUPS:].rearrange("p (g e) -> p g e", g=EGROUPS),
                                              G.group_is[:, i, :, None].to_broadcast([P, EGROUPS, PER_GROUP]), ALU.mult)
            link(ins)
            for i in range(NT):
                ins = nc.vector.tensor_reduce(G.in_group[:, i, :], G.by_group[:, i, :].rearrange("p (g e) -> p e g", g=EGROUPS), AX.X, ALU.add)
            link(ins)
            for i in range(NT):
                ins = nc.vector.max(G.best[:, i, :], G.in_group[:, i, :])
            link(ins)
            for i in range(NT):
                ins = nc.vector.max_index(G.best_at[:, i, :], G.best[:, i, :], G.in_group[:, i, :])
            link(ins)
            nc.vector.tensor_tensor(G.one[:, :, None], G.best[:, :, 1:2], G.best[:, :, 0:1], ALU.subtract).then_inc(Z.exp_asked, 1)
            v.wait_ge(Z.exp_ready, 2)
            link(nc.vector.tensor_reduce(gates[:, :, 0], G.num, AX.X, ALU.add))
            link(nc.vector.scalar_tensor_tensor(out=gates[:, :, 0], in0=G.one, scalar=1.0, in1=gates[:, :, 0], op0=ALU.add, op1=ALU.mult))
            link(nc.vector.reciprocal(gates[:, :, 0], gates[:, :, 0]))
            nc.vector.tensor_tensor(gates[:, :, 1], gates[:, :, 0], G.one, ALU.mult)
            link(nc.vector.tensor_copy(G.e_at, G.best_at[:, :, 0:2]))
            link(nc.vector.scalar_tensor_tensor(out=G.e_at, in0=G.group[:, :, None].to_broadcast([P, NT, 2]), scalar=float(PER_GROUP),
                                                in1=G.e_at, op0=ALU.mult, op1=ALU.add))
            for k in range(2):
                ins = nc.vector.tensor_tensor(G.is_expert[k], erow[:, None, :].to_broadcast([P, NT, EXPERTS]),
                                              G.e_at[:, :, k:k + 1].to_broadcast([P, NT, EXPERTS]), ALU.is_equal)
            link(ins)
            nc.vector.tensor_tensor(G.either, G.is_expert[0], G.is_expert[1], ALU.add).then_inc(Z.chosen, 1)
            v.wait_ge(Z.ranked, 1)
            link(nc.vector.tensor_copy(G.count, ps[:, 6, 0:EXPERTS]))
            for i in range(NT):
                ins = nc.vector.tensor_copy(G.rank[:, i, :], ps[:, 4 + i % 2, (i // 2) * EXPERTS:(i // 2 + 1) * EXPERTS])
            link(nc.vector.tensor_scalar(G.further, G.count, -1.0, None, ALU.add))
            whole_blocks(link, G.further, G.further)
            link(nc.vector.tensor_scalar(G.further, G.further, 0.0, None, ALU.max))
            link(nc.vector.memset(G.tmp, 0.0))
            link(nc.vector.tensor_tensor_scan(G.cum, G.further, G.tmp, 0.0, ALU.add, ALU.add))
            link(nc.vector.tensor_tensor(G.first, G.cum, G.further, ALU.subtract))
            m = G.part
            whole_blocks(link, m, G.rank)
            link(nc.vector.scalar_tensor_tensor(out=G.place, in0=m, scalar=-float(CAP), in1=G.rank, op0=ALU.mult, op1=ALU.add))
            link(nc.vector.tensor_scalar(G.place, G.place, float(BLOCKS), None, ALU.mult))
            link(nc.vector.scalar_tensor_tensor(out=G.place, in0=erow[:, None, :].to_broadcast([P, NT, EXPERTS]), scalar=1.0, in1=G.place,
                                                op0=ALU.mult, op1=ALU.add))
            link(nc.vector.scalar_tensor_tensor(out=G.first, in0=G.first, scalar=float(EXPERTS - 1), in1=erow, op0=ALU.add, op1=ALU.subtract))
            link(nc.vector.tensor_tensor(G.by_group, m, G.first[:, None, :].to_broadcast([P, NT, EXPERTS]), ALU.add))
            link(nc.vector.scalar_tensor_tensor(out=G.by_group, in0=m, scalar=0.0, in1=G.by_group, op0=ALU.is_gt, op1=ALU.mult))
            link(nc.vector.tensor_tensor(G.place, G.place, G.by_group, ALU.add))
            for k in range(2):
                link(nc.vector.tensor_tensor(G.is_expert[k], G.is_expert[k], G.place, ALU.mult))
                link(nc.vector.tensor_reduce(G.slot[:, :, k], G.is_expert[k], AX.X, ALU.add))
                tok = table("token")
                link(nc.vector.tensor_copy(G.pair[:, :, k, 0], tok))
                link(nc.vector.tensor_scalar(G.pair[:, :, k, 1], tok, 2.0, float(k), ALU.mult, ALU.add))
            link(nc.vector.tensor_copy(G.pair_i, G.pair))
            nc.vector.tensor_copy(G.slot_i, G.slot).then_inc(Z.placed, 1)
            link(nc.vector.tensor_tensor(G.le, G.cum[:, None, :].to_broadcast([P, SPILL + 1, EXPERTS]),
                                         table("expert_row")[:, 0:SPILL + 1, None].to_broadcast([P, SPILL + 1, EXPERTS]), ALU.is_le))
            link(nc.vector.tensor_reduce(G.spill, G.le, AX.X, ALU.add))
            link(nc.vector.tensor_scalar(G.spill, G.spill, float(EXPERTS - 1), None, ALU.min))
            link(nc.vector.tensor_copy(G.spill[:, SPILL:], G.cum[:, EXPERTS - 1:]))
            link(nc.vector.tensor_copy(spill_info, G.spill))

        def route_pool(pool):
            nc.gpsimd.memset(E.x[0:CAP], 0.0)
            nc.gpsimd.memset(G.empty[0:CAP], NO_ROW).then_inc(Z.cleared, 1)
            pool.wait_ge(Z.cleared, 1)
            pool.dma_start(slot_table.rearrange("(p b) k -> p (b k)", p=CAP), G.empty[0:CAP]).then_inc(table_out, 16)
            pool.wait_ge(normed_stored, 16)
            pool.wait_ge(table_out, 16)
            pool.wait_ge(Z.placed, 1)
            for i in range(NT):
                for k in range(2):
                    nc.gpsimd.indirect_dma_start(out=slot_table, out_offset=bass.IndirectOffsetOnAxis(ap=G.slot_i[:, i, k:k + 1], axis=0),
                                                 in_=G.pair_i[:, i, k, :], in_offset=None).then_inc(table_out, 16)

        U_EXPERTS = 24
        PAR = 4
        assert 3 * PAR % RING == 0 and U_EXPERTS % RING == 0 and EXPERTS % PAR == 0

        class E:
            lay = Arena(arena)
            lay.at = G.lay.at
            table = lay(2 * BLOCKS).bitcast(I32)
            index = lay(4, 2).bitcast(I32)
            fold = lay(CAP)
            x = lay(2, D)
            gate = lay(HID)
            up = lay(HID)
            silu = lay(FC, CAP)
            hT = lay(FC, CAP)
            y = lay(2, D)
            xs = rows_r[:, 0:KC * 2 * CAP].rearrange("p (c k) -> p c k", c=KC)
            high = [xnT_r, xn_r]

        def expert_weights(e):
            w1, w3, w2 = (t[n][0][bass.ds(e, 1)] for n in ("moe_w1", "moe_w3", "moe_w2"))
            return [w1.rearrange("e (p c) n -> p (e c) n", c=KC), w3.rearrange("e (p c) n -> p (e c) n", c=KC),
                    w2.rearrange("e (p c) n -> p (e c) n", c=FC)]

        def wait_past(eng, sem_, value):
            if not isinstance(value, int) or value > 0:
                eng.wait_ge(sem_, value)

        def turns(eng, body):
            for b in range(PAR):
                body(0, b)
            with eng.Fori(1, EXPERTS // PAR) as it:
                for b in range(PAR):
                    body(it, b)

        def experts_sp(sp):
            with sp.Fori(0, EXPERTS // PAR) as it:
                for b in range(PAR):
                    for j, src in enumerate(expert_weights(it * PAR + b)):
                        q = 3 * b + j
                        sp.wait_ge(unit_used, U_EXPERTS + it * (3 * PAR) + (q - RING + 1))
                        sp.dma_start(unit(q, src.shape[2]), src).then_inc(unit_loaded[q % RING], 16)

        def wait_expert_unit(eng, it, q):
            eng.wait_ge(unit_loaded[q % RING], it * (16 * 3 * PAR // RING) + 16 * (FIRST_LOADS[q % RING] + q // RING + 1))

        def gather(into, index):
            return nc.gpsimd.indirect_dma_start(out=E.x[0:CAP, into], out_offset=None, in_=normed_rows,
                                                in_offset=bass.IndirectOffsetOnAxis(ap=index[0:CAP, 0:1], axis=0),
                                                bounds_check=S - 1, oob_is_err=False)

        def scatter(frm, index):
            return nc.gpsimd.indirect_dma_start(out=expert_rows, out_offset=bass.IndirectOffsetOnAxis(ap=index[0:CAP, 1:2], axis=0),
                                                in_=E.y[0:CAP, frm], in_offset=None, bounds_check=2 * S - 1, oob_is_err=False)

        def experts_pool(pool):
            nc.gpsimd.tensor_copy(E.index[0:CAP, 0:2], E.table[0:CAP, 0:4].rearrange("p (e k) -> p e k", k=2)).then_inc(Z.index_copied, 1)
            pool.wait_ge(Z.index_copied, 1)
            for b in range(2):
                gather(b, E.index[:, b]).then_inc(gathered[b], 16)

            def body(it, b):
                e = it * PAR + b
                wait_past(pool, scattered[b % 2], it * 32 + 16 * (b // 2))
                nc.gpsimd.tensor_copy(E.index[0:CAP, (b + 2) % 4], E.table[0:CAP, bass.ds(it * (2 * PAR) + 2 * (b + 2), 2)]).then_inc(Z.index_copied, 1)
                pool.wait_ge(Z.index_copied, e + 2)
                pool.wait_ge(Z.x_turned, e + 1)
                pool.sem_inc(Z.waits_passed, 1)
                gather(b % 2, E.index[:, (b + 2) % 4]).then_inc(gathered[b % 2], 16)
                pool.wait_ge(Z.y_act, e + 1)
                pool.wait_ge(Z.y_dve, e + 1)
                pool.sem_inc(Z.waits_passed, 1)
                scatter(b % 2, E.index[:, b % 4]).then_inc(scattered[b % 2], 16)
            turns(pool, body)
            for s_ in scattered:
                pool.wait_ge(s_, 16 * EXPERTS // 2)
            for s_ in gathered:
                pool.wait_ge(s_, 16 * (EXPERTS // 2 + 1))

        def turn_x(src):
            view = src[0:CAP].rearrange("k (p c) -> k c p", c=KC)
            for c in range(KC):
                ins = nc.tensor.transpose(ps[:, 0, c * CAP:(c + 1) * CAP], view[:, c, :], ident[0:CAP, 0:CAP])
            return ins

        def part_up(u, j, half, bank):
            high = E.high[j].rearrange("p (c n) -> p c n", c=KC)
            low = unit_low(u)
            res = []
            for c in range(4 * half, 4 * half + 4):
                for k, w in enumerate((high, low)):
                    res.append(nc.tensor.matmul(ps[0:2 * CAP, bank, :], E.xs[:, c, :], w[:, c, :],
                                                start=(c == 0 and k == 0), stop=(c == KC - 1 and k == 1)))
            return res

        def fold(src, bank, chunks):
            view = src[0:2 * CAP].rearrange("k (p c) -> k c p", c=FC)
            return [nc.tensor.matmul(ps[:, bank, c * CAP:(c + 1) * CAP], view[:, c, :], E.fold[0:2 * CAP], start=True, stop=True) for c in chunks]

        def down_product(u, chunks):
            res = []
            for half in range(2):
                for c in chunks:
                    ins = nc.tensor.matmul(ps[0:CAP, 5 + half, :], E.hT[:, c, :], unit(u, D)[:, c, half * BANK:(half + 1) * BANK],
                                           start=(c == 0), stop=(c == FC - 1))
                res.append(ins)
            return res

        def quarter(q):
            return slice(q * (UNIT // 4), (q + 1) * (UNIT // 4))

        def split_high(u, j, q):
            nc.scalar.activation(E.high[j][:, quarter(q)], slot(u)[:, quarter(q)], ACT.Copy).then_inc(Z.w_high, 1)

        def split_low(u, j, q):
            nc.vector.tensor_tensor(ring_r[:, u % RING, quarter(q)], slot(u)[:, quarter(q)], E.high[j][:, quarter(q)].bitcast(F32),
                                    ALU.subtract).then_inc(Z.w_low, 1)

        def tokens_high():
            view = ps[:, 0, 0:KC * CAP].rearrange("p (c k) -> p c k", c=KC)
            return nc.scalar.activation(E.xs[:, :, 0:CAP], view, ACT.Copy)

        def tokens_low():
            view = ps[:, 0, 0:KC * CAP].rearrange("p (c k) -> p c k", c=KC)
            return nc.vector.tensor_tensor(E.xs[:, :, CAP:], view, E.xs[:, :, 0:CAP].bitcast(F32), ALU.subtract)

        def turned_bank(bank, half):
            return ps[:, bank, 0:FC * CAP].rearrange("p (c k) -> p c k", c=FC)[:, 2 * half:2 * half + 2, :]

        UP_BANKS = (1, 7)

        def experts_pe(pe):
            pe.wait_ge(gathered[0], 16)
            turn_x(E.x[:, 0]).then_inc(Z.x_turned, 1)
            pe.wait_ge(Z.fold_made, 1)

            def body(it, b):
                e = it * PAR + b
                pe.wait_ge(Z.x_low, e + 1)
                for half in range(2):
                    pe.wait_ge(Z.w_low, e * 8 + 2 * half + 2)
                    gate = part_up(3 * b, 0, half, 2)
                gate[-1].then_inc(Z.gate_ready, 1)
                wait_past(pe, Z.up_kept, e * 2)
                for half in range(2):
                    pe.wait_ge(Z.w_low, e * 8 + 2 * half + 6)
                    up = part_up(3 * b + 1, 1, half, 3)
                    if half == 0:
                        up[0].then_inc(unit_used, 1)
                up[-1].then_inc(Z.up_ready, 1)
                pe.wait_ge(Z.gate_kept, e + 1)
                folded = fold(E.gate, 4, range(FC))
                folded[0].then_inc(unit_used, 1)
                folded[-1].then_inc(Z.gate_turned, 1)
                for half in range(2):
                    if half:
                        pe.wait_ge(gathered[(b + 1) % 2], it * 32 + 16 * ((b + 1) // 2 + 1))
                        pe.sem_inc(Z.pe_passed, 1)
                        turn_x(E.x[:, (b + 1) % 2]).then_inc(Z.x_turned, 1)
                    else:
                        pe.wait_ge(Z.up_kept, e * 2 + 2)
                    fold(E.up, UP_BANKS[half], range(2 * half, 2 * half + 2))[-1].then_inc(Z.up_turned, 1)
                wait_expert_unit(pe, it, 3 * b + 2)
                wait_past(pe, Z.y_act, e)
                wait_past(pe, Z.y_dve, e)
                for half in range(2):
                    pe.wait_ge(Z.hidden_ready, e * 2 + half + 1)
                    down = down_product(3 * b + 2, range(2 * half, 2 * half + 2))
                for ins in down:
                    ins.then_inc(Z.down_ready, 1)
                release_unit(pe)
            turns(pe, body)

        def experts_dve(v):
            nc.vector.tensor_tensor(E.fold[0:2 * CAP], ident[0:2 * CAP, 0:CAP], ident[0:2 * CAP, CAP:2 * CAP], ALU.add).then_inc(Z.fold_made, 1)
            v.wait_ge(Z.x_high, 1)
            tokens_low().then_inc(Z.x_low, 1)

            def keep_y(it, b, e):
                v.wait_ge(Z.down_ready, e * 2)
                s_ = (b + 1) % 2
                wait_past(v, scattered[s_], it * 32 + 16 * ((b - 1) // 2))
                nc.vector.tensor_copy(E.y[0:CAP, s_, BANK:], ps[0:CAP, 6, :]).then_inc(Z.y_dve, 1)

            def body(it, b):
                e = it * PAR + b
                for j in range(2):
                    for q in range(4):
                        v.wait_ge(Z.w_high, e * 8 + 4 * j + q + 1)
                        split_low(3 * b + j, j, q)
                if not (isinstance(it, int) and e == 0):
                    keep_y(it, b, e)
                v.wait_ge(Z.up_ready, e + 1)
                wait_past(v, Z.up_turned, e * 2)
                for half in range(2):
                    cols = slice(half * HID // 2, (half + 1) * HID // 2)
                    nc.vector.tensor_copy(E.up[0:2 * CAP, cols], ps[0:2 * CAP, 3, cols]).then_inc(Z.up_kept, 1)
                wait_past(v, Z.down_ready, e * 2)
                for half in range(2):
                    if half:
                        v.wait_ge(Z.x_high, e + 2)
                        tokens_low().then_inc(Z.x_low, 1)
                    v.wait_ge(Z.up_turned, e * 2 + half + 1)
                    v.wait_ge(Z.silu_ready, e * 2 + half + 1)
                    nc.vector.tensor_tensor(E.hT[:, 2 * half:2 * half + 2, :], E.silu[:, 2 * half:2 * half + 2, :], turned_bank(UP_BANKS[half], half),
                                            ALU.mult).then_inc(Z.hidden_ready, 1)

            turns(v, body)
            keep_y(EXPERTS // PAR, 0, EXPERTS)

        def experts_act(a):
            a.wait_ge(Z.x_turned, 1)
            tokens_high().then_inc(Z.x_high, 1)

            def keep_y(it, b, e):
                a.wait_ge(Z.down_ready, e * 2 - 1)
                s_ = (b + 1) % 2
                wait_past(a, scattered[s_], it * 32 + 16 * ((b - 1) // 2))
                nc.scalar.activation(E.y[0:CAP, s_, 0:BANK], ps[0:CAP, 5, :], ACT.Copy).then_inc(Z.y_act, 1)

            def body(it, b):
                e = it * PAR + b
                for j in range(2):
                    wait_expert_unit(a, it, 3 * b + j)
                    for q in range(4):
                        split_high(3 * b + j, j, q)
                if not (isinstance(it, int) and e == 0):
                    keep_y(it, b, e)
                a.wait_ge(Z.gate_ready, e + 1)
                nc.scalar.activation(E.gate[0:2 * CAP], ps[0:2 * CAP, 2, :], ACT.Copy).then_inc(Z.gate_kept, 1)
                a.wait_ge(Z.gate_turned, e + 1)
                wait_past(a, Z.hidden_ready, e * 2)
                for half in range(2):
                    nc.scalar.activation(E.silu[:, 2 * half:2 * half + 2, :], turned_bank(4, half), ACT.Silu).then_inc(Z.silu_ready, 1)
                a.wait_ge(Z.x_turned, e + 2)
                tokens_high().then_inc(Z.x_high, 1)
            turns(a, body)
            keep_y(EXPERTS // PAR, 0, EXPERTS)

        def spills(eng, body):
            n = eng.value_load(spill_info[0:1, SPILL:SPILL + 1], min_val=0, max_val=SPILL)
            with eng.If(n > 0):
                with eng.Fori(0, SPILL) as j:
                    with eng.If(n > j):
                        body(j)

        def spill_sp(sp):
            sp.wait_ge(stage_open, STAGES_BEFORE_SPILL)

            def body(j):
                e = sp.value_load(spill_info[0:1, bass.ds(j, 1)], min_val=0, max_val=EXPERTS - 1)
                for q, src in enumerate(expert_weights(e)):
                    sp.dma_start(unit(q, src.shape[2]), src).then_inc(spill_loaded, 16)
                sp.wait_ge(spill_used, j + 1)
                sp.sem_inc(spill_next, 1)
            spills(sp, body)
            sp.wait_ge(stage_open, STAGES_BEFORE_SPILL + 1)
            sp.wait_ge(rows_sent, 2)

        def spill_pool(pool):
            def body(j):
                at = pool.snap(j * 2 + 2 * EXPERTS, min_val=2 * EXPERTS, max_val=2 * BLOCKS - 2)
                nc.gpsimd.tensor_copy(E.index[0:CAP, 0], E.table[0:CAP, bass.ds(at, 2)]).then_inc(Z.index_copied, 1)
                pool.wait_ge(Z.index_copied, j + 1)
                pool.sem_inc(Z.waits_passed, 1)
                gather(0, E.index[:, 0]).then_inc(spill_gathered, 16)
                pool.wait_ge(Z.y_act, j * 2 + 2)
                pool.sem_inc(Z.waits_passed, 1)
                scatter(0, E.index[:, 0]).then_inc(spill_scattered, 16)
                pool.wait_ge(spill_scattered, j * 16 + 16)
                pool.sem_inc(Z.waits_passed, 1)
            spills(pool, body)

        def spill_pe(pe):
            def body(j):
                pe.wait_ge(spill_gathered, j * 16 + 16)
                pe.sem_inc(Z.pe_passed, 1)
                turn_x(E.x[:, 0]).then_inc(Z.x_turned, 1)
                pe.wait_ge(Z.x_low, j + 1)
                pe.wait_ge(Z.w_low, j * 8 + 8)
                for half in range(2):
                    gate = part_up(0, 0, half, 2)
                gate[-1].then_inc(Z.gate_ready, 1)
                for half in range(2):
                    up = part_up(1, 1, half, 3)
                up[-1].then_inc(Z.up_ready, 1)
                pe.wait_ge(Z.gate_kept, j + 1)
                fold(E.gate, 4, range(FC))[-1].then_inc(Z.gate_turned, 1)
                pe.wait_ge(Z.up_kept, j + 1)
                fold(E.up, 1, range(FC))[-1].then_inc(Z.up_turned, 1)
                pe.wait_ge(Z.hidden_ready, j + 1)
                pe.wait_ge(spill_loaded, j * 48 + 48)
                for ins in down_product(2, range(FC)):
                    ins.then_inc(Z.down_ready, 1)
                pe.drain().then_inc(spill_used, 1)
            spills(pe, body)

        def spill_dve(v):
            def body(j):
                for k in range(2):
                    for q in range(4):
                        v.wait_ge(Z.w_high, j * 8 + 4 * k + q + 1)
                        split_low(k, k, q)
                v.wait_ge(Z.x_high, j + 1)
                tokens_low().then_inc(Z.x_low, 1)
                v.wait_ge(Z.up_ready, j + 1)
                nc.vector.tensor_copy(E.up[0:2 * CAP], ps[0:2 * CAP, 3, :]).then_inc(Z.up_kept, 1)
                v.wait_ge(Z.up_turned, j + 1)
                v.wait_ge(Z.silu_ready, j + 1)
                nc.vector.tensor_tensor(E.hT, E.silu, ps[:, 1, 0:FC * CAP].rearrange("p (c k) -> p c k", c=FC), ALU.mult).then_inc(Z.hidden_ready, 1)
            spills(v, body)

        def spill_act(a):
            def body(j):
                a.wait_ge(spill_loaded, j * 48 + 48)
                for k in range(2):
                    for q in range(4):
                        split_high(k, k, q)
                a.wait_ge(Z.x_turned, j + 1)
                tokens_high().then_inc(Z.x_high, 1)
                a.wait_ge(Z.gate_ready, j + 1)
                nc.scalar.activation(E.gate[0:2 * CAP], ps[0:2 * CAP, 2, :], ACT.Copy).then_inc(Z.gate_kept, 1)
                a.wait_ge(Z.gate_turned, j + 1)
                nc.scalar.activation(E.silu, ps[:, 4, 0:FC * CAP].rearrange("p (c k) -> p c k", c=FC), ACT.Silu).then_inc(Z.silu_ready, 1)
                for half in range(2):
                    a.wait_ge(Z.down_ready, j * 2 + half + 1)
                    nc.scalar.activation(E.y[0:CAP, 0, half * BANK:(half + 1) * BANK], ps[0:CAP, 5 + half, :], ACT.Copy).then_inc(Z.y_act, 1)
            spills(a, body)

        chosen_rows = Arena(arena)(NT, 2, D)

        def unite_dve(v, link):
            def final(i):
                v.wait_ge(Z.roots_ready, i + 1)
                tile_norm_dve(link, h, rows[:, 1], h, i, 0)

            for i in range(NT):
                v.wait_ge(chosen_loaded[i], 16)
                for k in range(2):
                    ins = nc.vector.scalar_tensor_tensor(out=h[:, i, :], in0=chosen_rows[:, i, k, :], scalar=gates[:, i, k:k + 1], in1=h[:, i, :],
                                                         op0=ALU.mult, op1=ALU.add)
                    if k == 0:
                        link(ins)
                ins.then_inc(Z.tile_added, 1)
                if i:
                    final(i - 1)
            final(NT - 1)

        U_LAYERS = U_EXPERTS + 3 * EXPERTS
        LAYER_UNITS = 24
        UP_PAIRS = 2
        DOWN_BLOCKS = KC
        assert U_LAYERS % RING == 0 and LAYER_UNITS % RING == 0

        class Y:
            lay = Arena(arena)
            qk = lay(4, S)
            mv = lay(NT, MH, DV + 1)
            mo = lay(NT, MH * DV)
            aqT = lay(4, S)
            akT = lay(S)
            av = lay(NT, 2 * DH)
            gates = lay(NT, 2 * MH)
            phase = lay.at
            conv = lay(2, S)
            rot = lay(2, BANK)
            rotk = lay(2, 2 * DH)
            tmp = lay(BANK)
            lay.at = phase
            w = lay(2, NT, S)
            li = lay(S)
            scratch = li.rearrange("p (i k) -> p i k", i=NT)
            lf = lay(S)
            b = lay(S)
            top = lay(S)
            diag = lay(NT, P)
            assert lay.at <= 16340
            lay.at = phase
            masked = lay(2, BANK)
            probs = lay(2, BANK)
            turned = lay(2, BANK)
            res = lay(NT, BANK + 2 * HEADS)
            ff = Arena(arena)
            act = ff(FB, S)
            acc = ff(2, 2, S)
            assert ff.at <= 16340
            squares = Arena(arena, FB * S)(2, D)
            par = Arena(arena, 16340)
            fconv = par(2 * FB, FCONV)
            qconv = par(4, CONV)
            qbias = par(4)
            gbias = par(2 * MH)
            sinks = par(HEADS)
            mnorm = par(MH * DV)

        def layer_row(name, l):
            return t[name][bass.ds(l, 1)]

        def layer_units(l):
            def of(name):
                return t[name][bass.ds(l, 1)]
            w = of("w_in_2").rearrange("l (p c) n -> p (l c) n", c=KC)
            us = [(None, w[:, :, n * BANK:(n + 1) * BANK]) for n in range(3)]
            us += [(None, w[:, :, W_AQ:W_AQ + BANK]), (None, w[:, :, W_AK:W_AK + 4 * DH])]
            wo = of("w_out_2").rearrange("l (p c) n -> p (l c) n", c=KC)
            us += [(None, wo[:, :, n * BANK:(n + 1) * BANK]) for n in range(2)]
            wu = of("w_up_2").rearrange("l (p c) (s n) -> p (l c) s n", c=KC, s=2)
            cols = UP_PAIRS * P
            us += [("up", wu[:, :, :, n * cols:(n + 1) * cols]) for n in range(FB // UP_PAIRS)]
            wd = of("w_down_2").rearrange("l (b p) n -> p (l b) n", p=P)
            us += [(None, wd[:, b0:min(b0 + DOWN_BLOCKS, FB), half * BANK:(half + 1) * BANK])
                   for half in range(2) for b0 in range(0, FB, DOWN_BLOCKS)]
            assert len(us) == LAYER_UNITS
            return us

        Q_QK, Q_MV, Q_MO, Q_AQ, Q_AKV, Q_OUT, Q_UP, Q_DOWN = 0, 1, 2, 3, 4, 5, 7, 18
        SPLIT = Q_DOWN

        def layer_slot(q):
            return q % 2 if q < SPLIT else (q - SPLIT) % RING

        def slot_free(q):
            users = [(k, j) for j in range(q) for k in ({layer_slot(j), layer_slot(j) + 2} if j < SPLIT else {layer_slot(j)})]
            last = [j for k, j in users if k == layer_slot(q)]
            return last[-1] + 1 if last else q - 1

        slot_units = [[q for q in range(LAYER_UNITS) if layer_slot(q) == k] for k in range(RING)]

        def wait_layer_unit(eng, q):
            k = layer_slot(q)
            before = FIRST_LOADS[k] + 3 * EXPERTS // RING
            eng.wait_ge(unit_loaded[k], current["l"] * (16 * len(slot_units[k])) + 16 * (before + slot_units[k].index(q) + 1))

        def lunit(q, cols=BANK):
            return ring[:, layer_slot(q)].rearrange("p (c n) -> p c n", n=cols)

        def rows_of(c, i):
            return xnT_high[:, c, i * P:(i + 1) * P], xn_low[:, i, c, :]

        def all_rows(c):
            return xnT_high[:, c, :], xn_low[:, :, c, :]

        def akv_parts():
            n = KC * 4 * DH
            return ([w[:, 0:n].rearrange("p (c n) -> p c n", c=KC) for w in halves(Q_AKV)],
                    [w[:, n:unit_size(Q_AKV)].rearrange("p (c n) -> p c n", c=KC) for w in halves(Q_AKV)])

        def layers_sp(sp):
            with sp.Fori(0, LAYERS) as l:
                current["l"] = l
                for q, (kind, src) in enumerate(layer_units(l)):
                    if q == 2:
                        sp.wait_ge(rows_sent, l + 3)
                        sp.sem_inc(sp_passed, 1)
                    sp.wait_ge(unit_used, l * LAYER_UNITS + (U_LAYERS + slot_free(q)))
                    if kind == "up":
                        dst = ring[:, layer_slot(q)].rearrange("p (c s n) -> p c s n", c=KC, s=2)
                    else:
                        n = src.shape[1] * src.shape[2]
                        dst = ring[:, layer_slot(q), 0:n].rearrange("p (c n) -> p c n", c=src.shape[1])
                    if q == Q_AKV:
                        w = t["w_in_2"][bass.ds(l, 1)].rearrange("l (p c) n -> p (l c) n", c=KC)
                        gate_w = ring[:, layer_slot(q), n:unit_size(q)].rearrange("p (c n) -> p c n", c=KC)
                        sp.dma_start(gate_w, w[:, :, W_GATES:W_GATES + 2 * MH]).then_inc(gates_loaded, 16)
                    sp.dma_start(dst, src).then_inc(unit_loaded[layer_slot(q)], 16)
            current["l"] = None

        def load_layer(a, l):
            for n, name in enumerate(("g_post_mix_2", "g_pre_ffn_2", "g_post_ffn_2")):
                a.dma_start(rows[:, n + 1], layer_row(name, l).partition_broadcast(P)).then_inc(layer_loaded, 16)
            for dst, name in ((Y.gbias, "gate_bias_2"), (Y.sinks, "attn_sinks_2"), (Y.mnorm, "mh_norm_g_2")):
                a.dma_start(dst, layer_row(name, l).partition_broadcast(P)).then_inc(layer_loaded, 16)
            for dst, name in ((Y.fconv, "ffn_conv_t"), (Y.qconv, "qk_conv_t")):
                a.dma_start(dst, layer_row(name, l).rearrange("l p b k -> (l p) b k")).then_inc(layer_loaded, 16)
            a.dma_start(Y.qbias, layer_row("qk_bias_t", l).rearrange("l p b -> (l p) b")).then_inc(layer_loaded, 16)

        def project_pe(pe):
            def taken(n):
                return (Z.taken_dve, n + 1) if n < 4 else (Z.taken_act, n - 3) if n < 12 else (Z.taken_dve, n - 7)

            def turn(n):
                m = n - 3 * NT
                pe.wait_ge(Z.roped, m + 1)
                if m >= 2:
                    pe.wait_ge(Z.turned_kept, m - 1)
                if n < 4 * NT:
                    for c in range(4):
                        ins = nc.tensor.transpose(ps[:, 4 + m % 2, c * P:(c + 1) * P], Y.rot[:, m % 2, c * P:(c + 1) * P], ident)
                else:
                    ins = nc.tensor.transpose(ps[:, 4 + m % 2, 0:P], Y.rotk[:, m % 2, :], ident)
                ins.then_inc(Z.turned, 1)

            for n in range(5 * NT):
                q, i = divmod(n, NT)
                if n >= 4:
                    pe.wait_ge(*taken(n - 4))
                if q == Q_AKV and i == 0:
                    wait_halves(pe, q, 3)
                for c in range(KC):
                    if q != Q_AKV and i == 0 and c % 2 == 0:
                        wait_halves(pe, q, c // 2)
                    flags = dict(start=(c == 0), stop=(c == KC - 1))
                    if q == Q_AKV:
                        ins = products(ps[:, n % 4, 0:4 * DH], rows_of(c, i), [w[:, c, :] for w in akv_parts()[0]], **flags)
                        continue
                    ws = [w.rearrange("p (c n) -> p c n", c=KC)[:, c, :] for w in halves(q)]
                    if q == Q_QK:
                        ins = products(ps[:, n % 4, :], all_rows(c), [w[:, i * P:(i + 1) * P] for w in ws], weights_left=True, **flags)
                    else:
                        ins = products(ps[:, n % 4, :], rows_of(c, i), ws, **flags)
                if q == Q_AKV:
                    for c in range(KC):
                        ins = products(ps[:, n % 4, 4 * DH:4 * DH + 2 * MH], rows_of(c, i), [w[:, c, :] for w in akv_parts()[1]],
                                       start=(c == 0), stop=(c == KC - 1))
                ins.then_inc(Z.proj_ready, 1)
                if i == NT - 1:
                    release_unit(pe)
                if n - 1 >= 3 * NT:
                    turn(n - 1)
            turn(5 * NT - 1)

        def project_dve(v, link):
            for n in range(4):
                v.wait_ge(Z.weighted, n + 1)
                acc = Y.conv[:, n % 2]
                for back in range(1, CONV):
                    ins = nc.vector.scalar_tensor_tensor(out=acc[:, back:], in0=ps[:, n % 4, 0:S - back], scalar=Y.qconv[:, n, CONV - 1 - back:CONV - back],
                                                         in1=acc[:, back:], op0=ALU.mult, op1=ALU.add)
                    if back < CONV - 1:
                        link(ins)
                    else:
                        ins.then_inc(Z.taken_dve, 1)
            cos = table("cos_nat").rearrange("p (i d) -> p i d", i=NT)
            sin = table("sin_nat").rearrange("p (i d) -> p i d", i=NT)
            for m in range(2 * NT):
                n = 3 * NT + m
                i = m % NT
                v.wait_ge(Z.proj_ready, n + 1)
                if m >= 2:
                    v.wait_ge(Z.turned, m - 1)
                res = ps[:, n % 4, :]
                if m < NT:
                    dst, tmp, src, heads = Y.rot[:, m % 2], Y.tmp, res, HEADS
                else:
                    dst, tmp, src, heads = Y.rotk[:, m % 2], Y.tmp[:, 0:2 * DH], res[:, 0:2 * DH], 2
                    nc.vector.tensor_copy(Y.av[:, i], res[:, 2 * DH:4 * DH])
                    nc.vector.tensor_tensor(Y.gates[:, i], res[:, 4 * DH:4 * DH + 2 * MH], Y.gbias, ALU.add)
                rope(src, tmp, dst, cos[:, i], sin[:, i], heads, paired=True)
                v.wait_ge(Z.taken_dve, m + 5)
                nc.vector.tensor_tensor(dst, dst, tmp, ALU.add).then_inc(Z.roped, 1)
                v.wait_ge(Z.roped, m + 1)

        def project_act(a):
            def newest(n):
                a.wait_ge(Z.proj_ready, n + 1)
                nc.scalar.activation(Y.conv[:, n % 2], ps[:, n % 4, :], ACT.Identity, bias=Y.qbias[:, n:n + 1],
                                     scale=Y.qconv[:, n, CONV - 1:CONV]).then_inc(Z.weighted, 1)

            high_act(a, 1)
            newest(0)
            for n in range(4):
                if n + 1 < 4:
                    if n >= 1:
                        a.wait_ge(Z.gated, n)
                    newest(n + 1)
                a.wait_ge(Z.taken_dve, n + 1)
                nc.scalar.activation(Y.qk[:, n], Y.conv[:, n % 2], ACT.Silu).then_inc(Z.gated, 1)
            for n in range(4, 12):
                i = n % 4
                a.wait_ge(Z.proj_ready, n + 1)
                if n < 8:
                    nc.scalar.activation(Y.mv[:, i, :, 0:DV], ps[:, i, :].rearrange("p (h d) -> p h d", h=MH), ACT.Copy).then_inc(Z.taken_act, 1)
                else:
                    nc.scalar.activation(Y.mo[:, i], ps[:, i, :], ACT.Sigmoid).then_inc(Z.taken_act, 1)
                if i == 1:
                    high_act(a, n // NT + 1)
            for m in range(2 * NT):
                i = m % NT
                a.wait_ge(Z.turned, m + 1)
                bank = ps[:, 4 + m % 2, :]
                if m < NT:
                    nc.scalar.activation(Y.aqT[:, :, i * P:(i + 1) * P], bank.rearrange("p (c k) -> p c k", c=4), ACT.Copy,
                                         scale=DH ** -0.5).then_inc(Z.turned_kept, 1)
                else:
                    nc.scalar.activation(Y.akT[:, i * P:(i + 1) * P], bank[:, 0:P], ACT.Copy).then_inc(Z.turned_kept, 1)
                if i == 1:
                    high_act(a, Q_AQ + m // NT + 1)

        acol = small[:, 64:64 + NT * MH].rearrange("p (i h) -> p i h", i=NT)
        floor = small[:, 80:80 + NT * MH].rearrange("p (i h) -> p i h", i=NT)

        def mlstm_pe(pe):
            pe.wait_ge(Z.biased, 1)
            for x in range(2):
                for i in range(NT):
                    ins = nc.tensor.transpose(ps[0:MH, x, i * P:(i + 1) * P], Y.gates[:, i, x * MH:(x + 1) * MH], ident)
            ins.then_inc(Z.turned, 1)
            pe.wait_ge(Z.ranked, 1)
            for x, src in enumerate((Y.li, Y.lf)):
                for i in range(NT):
                    ins = nc.tensor.transpose(ps[:, 2 + x, i * MH:(i + 1) * MH], src[0:MH, i * P:(i + 1) * P], ident[0:MH, 0:MH])
            ins.then_inc(Z.turned, 1)
            pe.wait_ge(Z.placed, 1)
            pe.wait_ge(Z.exp_ready, 2)
            spread = table("spread").rearrange("p (h k) -> p h k", h=MH)

            def decays(n):
                if n:
                    pe.wait_ge(Z.strip_ready, n)
                nc.tensor.matmul(ps[:, 4, :], spread[0:MH, n, :], Y.top[0:MH, :], start=True, stop=True).then_inc(Z.strip_asked, 1)

            def scores(n, key_tiles):
                r = half_of(n)
                for kt in key_tiles:
                    if kt >= 2:
                        pe.wait_ge(Z.scores_taken, NT * n + kt - 1)
                    elif n >= 2:
                        pe.wait_ge(Z.scores_taken, NT * (n - 2) + kt + 3)
                    nc.tensor.matmul(ps[:, 2 * (n % 2) + kt % 2, kt * P:], Y.qk[r, 2 + n // 2, kt * P:(kt + 1) * P], Y.qk[r, n // 2, kt * P:],
                                     start=True, stop=True).then_inc(Z.scores_ready, 1)

            decays(0)
            scores(0, range(NT))
            for n in range(MH):
                if n + 1 < MH:
                    decays(n + 1)
                    scores(n + 1, (0, 1))
                pe.wait_ge(Z.scores_taken, NT * n + NT)
                if n:
                    pe.wait_ge(Z.mixed_taken, n)
                for i in range(NT):
                    for kt in range(i + 1):
                        ins = nc.tensor.matmul(ps[:, 5 + i // 2, (i % 2) * (DV + 1):(i % 2 + 1) * (DV + 1)], Y.w[:, n % 2, kt, i * P:(i + 1) * P],
                                               Y.mv[:, kt, n, :], start=(kt == 0), stop=(kt == i))
                ins.then_inc(Z.mixed_ready, 1)
                if n + 1 < MH:
                    scores(n + 1, (2, 3))

        def mlstm_dve(v, link):
            work = [small[:, 96 + 16 * j:112 + 16 * j].rearrange("p (i h) -> p i h", i=NT) for j in range(3)]
            nc.vector.memset(Y.mv[:, :, :, DV:DV + 1], 1.0)
            nc.vector.memset(Y.top[0:MH], 0.0)
            lf = Y.gates[:, :, MH:]
            log_sigmoid_dve(v, link, lf, work, lf, done=Z.biased)
            v.wait_ge(Z.turned, 1)
            link(nc.vector.tensor_copy(Y.li[0:MH], ps[0:MH, 0, :]))
            link(nc.vector.tensor_copy(Y.lf[0:MH], ps[0:MH, 1, :]))
            link(nc.vector.tensor_tensor_scan(Y.b[0:MH], Y.lf[0:MH], Y.top[0:MH], 0.0, ALU.add, ALU.add))
            link(nc.vector.tensor_tensor(Y.li[0:MH], Y.li[0:MH], Y.b[0:MH], ALU.subtract))
            link(nc.vector.tensor_tensor_scan(Y.top[0:MH], Y.li[0:MH], Y.li[0:MH], 0.0, ALU.max, ALU.max))
            link(nc.vector.scalar_tensor_tensor(out=Y.lf[0:MH], in0=Y.b[0:MH], scalar=-1.0, in1=Y.top[0:MH], op0=ALU.mult, op1=ALU.subtract))
            nc.vector.tensor_scalar(Y.top[0:MH], Y.top[0:MH], -1.0, None, ALU.mult).then_inc(Z.ranked, 1)
            v.wait_ge(Z.turned, 2)
            nc.vector.tensor_copy(acol, ps[:, 2, 0:NT * MH].rearrange("p (i h) -> p i h", i=NT)).then_inc(Z.placed, 1)

            def mixed(n):
                v.wait_ge(Z.mixed_ready, n + 1)
                both = ps[:, 5:7, 0:2 * (DV + 1)].rearrange("p b (i d) -> p b i d", i=2)
                d = small[:, 144:148].rearrange("p (b i) -> p b i", b=2)
                fl = floor[:, :, n].rearrange("p (b i) -> p b i", b=2)
                den = both[:, :, :, DV]
                link(nc.vector.tensor_scalar(d, den, -1.0, None, ALU.mult))
                link(nc.vector.tensor_tensor(d, d, den, ALU.max))
                link(nc.vector.tensor_tensor(d, d, fl, ALU.max))
                link(nc.vector.reciprocal(d, d))
                y = [xn[:, i, n * DV:(n + 1) * DV] for i in range(NT)]
                for i in range(NT):
                    ins = nc.vector.tensor_scalar(y[i], both[:, i // 2, i % 2, 0:DV], small[:, 144 + i:145 + i], None, ALU.mult)
                ins.then_inc(Z.mixed_taken, 1)
                v.wait_ge(Z.mixed_taken, n + 1)
                for i in range(NT):
                    ins = nc.vector.tensor_tensor_reduce(out=Y.scratch[:, i], in0=y[i], in1=y[i], scale=1.0, scalar=0.0, op0=ALU.mult, op1=ALU.add,
                                                         accum_out=small[:, 148 + i:149 + i])
                ins.then_inc(Z.moments, 1)
                v.wait_ge(Z.deviation, n + 1)
                link(nc.vector.reciprocal(small[:, 156:160], small[:, 152:156]))
                for i in range(NT):
                    ins = nc.vector.scalar_tensor_tensor(out=y[i], in0=y[i], scalar=small[:, 156 + i:157 + i], in1=Y.mnorm[:, n * DV:(n + 1) * DV],
                                                         op0=ALU.mult, op1=ALU.mult)
                link(ins)
                for i in range(NT):
                    ins = nc.vector.tensor_tensor(y[i], y[i], Y.mo[:, i, n * DV:(n + 1) * DV], ALU.mult)
                link(ins)

            def diagonal(n):
                v.wait_ge(Z.strip_asked, n + 1)
                nc.vector.tensor_tensor(Y.diag, ps[:, 4, :].rearrange("p (i k) -> p i k", i=NT),
                                        table("mask_causal_t")[:, None, :].to_broadcast([P, NT, P]), ALU.add).then_inc(Z.weighted, 1)

            diagonal(0)
            for n in range(MH):
                v.wait_ge(Z.strip_ready, n + 1)
                for kt in range(NT):
                    v.wait_ge(Z.scores_ready, NT * n + kt + 1)
                    w = Y.w[:, n % 2, kt, kt * P:]
                    nc.vector.scalar_tensor_tensor(out=w, in0=ps[:, 2 * (n % 2) + kt % 2, kt * P:], scalar=DH ** -0.5, in1=w,
                                                   op0=ALU.mult, op1=ALU.mult).then_inc(Z.scores_taken, 1)
                if n + 1 < MH:
                    diagonal(n + 1)
                if n:
                    mixed(n - 1)
            mixed(MH - 1)

        def mlstm_act(a):
            def deviation(n):
                a.wait_ge(Z.moments, n + 1)
                nc.scalar.activation(small[:, 152:156], small[:, 148:152], ACT.Sqrt, bias=table("eps"), scale=1.0 / DV).then_inc(Z.deviation, 1)

            work = small[:, 96:112]
            a.wait_ge(Z.exp_asked, 1)
            nc.scalar.activation(work, work, ACT.Exp).then_inc(Z.exp_ready, 1)
            a.wait_ge(Z.turned, 2)
            nc.scalar.activation(floor, ps[:, 3, 0:NT * MH].rearrange("p (i h) -> p i h", i=NT), ACT.Exp).then_inc(Z.exp_ready, 1)
            a.wait_ge(Z.placed, 1)
            def exponentials(n):
                a.wait_ge(Z.weighted, n + 1)
                if n >= 2:
                    a.wait_ge(Z.mixed_ready, n - 1)
                for kt in range(NT):
                    bias = acol[:, kt, n:n + 1]
                    ins = nc.scalar.activation(Y.w[:, n % 2, kt, kt * P:(kt + 1) * P], Y.diag[:, kt], ACT.Exp, bias=bias)
                    if kt < NT - 1:
                        ins = nc.scalar.activation(Y.w[:, n % 2, kt, (kt + 1) * P:], ps[:, 4, (kt + 1) * P:], ACT.Exp, bias=bias)
                ins.then_inc(Z.strip_ready, 1)

            exponentials(0)
            for n in range(MH):
                if n + 1 < MH:
                    exponentials(n + 1)
                if n:
                    deviation(n - 1)
            deviation(MH - 1)

        def window_chunks():
            res = []
            for i in range(NT):
                keys = [(slice(j * P, (j + 1) * P), j, P) for j in (i - 1, i) if j >= 0]
                res += [(i, slice(4 * g + j0, 4 * g + j0 + 2), keys, P if i == 0 else 0) for j0 in (0, 2) for g in range(2)]
            return res

        window = Attention(window_chunks(), table("mask_window"), lambda hh: Y.aqT[half_of(hh // 4), hh % 4, :],
                           lambda hh: Y.akT[half_of(hh // 4), :], lambda hh, vt: Y.av[:, vt, (hh // 4) * DH:(hh // 4 + 1) * DH],
                           Y.masked, Y.probs, Y.turned, Y.res, Y.sinks)

        def window_end_dve(v, link):
            m, d = Y.res[:, :, BANK:BANK + HEADS], Y.res[:, :, BANK + HEADS:]
            e = small[:, 64:96].rearrange("p (i h) -> p i h", i=NT)
            nc.vector.tensor_tensor(e, Y.sinks[:, None, :].to_broadcast([P, NT, HEADS]), m, ALU.subtract).then_inc(Z.exp_asked, 1)
            v.wait_ge(Z.exp_ready, 1)
            link(nc.vector.tensor_tensor(d, d, e, ALU.add))
            link(nc.vector.reciprocal(e, d))
            v.wait_ge(Z.mixed_taken, NT)
            for i in range(NT):
                nc.vector.tensor_tensor(xn[:, i, BANK:].rearrange("p (h d) -> p h d", d=DH), Y.res[:, i, 0:BANK].rearrange("p (h d) -> p h d", d=DH),
                                        e[:, i, :, None].to_broadcast([P, HEADS, DH]), ALU.mult)

        def window_end_act(a):
            a.wait_ge(Z.exp_asked, 1)
            nc.scalar.activation(small[:, 64:96], small[:, 64:96], ACT.Exp).then_inc(Z.exp_ready, 1)

        kept_last = xn
        kept_rows = arena[:, NT * D:2 * NT * D].rearrange("p (i n) -> p i n", i=NT)

        def out_jobs():
            jobs = []
            for q in (Q_OUT, Q_OUT + 1):
                ws = [w.rearrange("p (c n) -> p c n", c=KC) for w in halves(q)]
                for i in range(NT):
                    jobs.append((q, [x for c in range(KC) for x in passes(rows_of(c, i), [w[:, c, :] for w in ws])], "act"))
            return jobs

        def up_pe(pe):
            for j in range(FB):
                q = Q_UP + j // UP_PAIRS
                ws = [w.rearrange("p (c s b n) -> p c s b n", c=KC, s=2, b=UP_PAIRS) for w in halves(q)]
                for s_ in range(2):
                    n = 2 * j + s_
                    if n >= 8:
                        pe.wait_ge(Z.taken_dve, n - 7)
                    for c in range(KC):
                        if j % UP_PAIRS == 0 and s_ == 0 and c % 2 == 0:
                            wait_halves(pe, q, c // 2)
                        ins = products(ps[:, n % 8, :], all_rows(c), [w[:, c, s_, j % UP_PAIRS, :] for w in ws], weights_left=True,
                                       start=(c == 0), stop=(c == KC - 1))
                    ins.then_inc(Z.proj_ready, 1)
                if j % UP_PAIRS == UP_PAIRS - 1:
                    release_unit(pe)

        def up_dve(v, link):
            for j in range(FB):
                for s_ in range(2):
                    n = 2 * j + s_
                    acc = Y.acc[:, j % 2, s_]
                    taps = Y.fconv[:, s_ * FB + j]
                    v.wait_ge(Z.weighted, n + 1)
                    link(nc.vector.scalar_tensor_tensor(out=acc[:, 1:], in0=ps[:, n % 8, 0:S - 1], scalar=taps[:, 1:2], in1=acc[:, 1:],
                                                        op0=ALU.mult, op1=ALU.add))
                    nc.vector.scalar_tensor_tensor(out=acc[:, 2:], in0=ps[:, n % 8, 0:S - 2], scalar=taps[:, 0:1], in1=acc[:, 2:],
                                                   op0=ALU.mult, op1=ALU.add).then_inc(Z.taken_dve, 1)
                v.wait_ge(Z.taken_dve, 2 * j + 2)
                v.wait_ge(Z.gated, j + 1)
                nc.vector.tensor_tensor(Y.act[:, j], Y.act[:, j], Y.acc[:, j % 2, 1], ALU.mult).then_inc(Z.rows_ready, 1)

        def up_act(a):
            def newest(n):
                j, s_ = divmod(n, 2)
                a.wait_ge(Z.proj_ready, n + 1)
                if j >= 2:
                    a.wait_ge(Z.rows_ready, j - 1)
                nc.scalar.activation(Y.acc[:, j % 2, s_], ps[:, n % 8, :], ACT.Copy, scale=Y.fconv[:, s_ * FB + j, FCONV - 1:FCONV]).then_inc(Z.weighted, 1)

            for j in range(FB):
                newest(2 * j)
                newest(2 * j + 1)
                a.wait_ge(Z.taken_dve, 2 * j + 1)
                nc.scalar.activation(Y.act[:, j], Y.acc[:, j % 2, 0], ACT.Silu).then_inc(Z.gated, 1)
                q = Q_UP + j // UP_PAIRS
                if j % UP_PAIRS == 0 and Q_UP + 2 <= q + 1 < Q_DOWN:
                    high_act(a, q + 1)

        def down_pe(pe):
            for half in range(2):
                for b0 in range(0, FB, DOWN_BLOCKS):
                    q = Q_DOWN + 3 * half + b0 // DOWN_BLOCKS
                    wait_layer_unit(pe, q)
                    for i in range(NT):
                        for b in range(b0, min(b0 + DOWN_BLOCKS, FB)):
                            ins = nc.tensor.matmul(ps[:, 4 * half + i, :], Y.act[:, b, i * P:(i + 1) * P], lunit(q)[:, b - b0, :],
                                                   start=(b == 0), stop=(b == FB - 1))
                        if b == FB - 1:
                            ins.then_inc(Z.proj_ready, 1)
                    release_unit(pe)

        STAGES_PER_LAYER = 8

        def layer_loop(eng, me, body):
            before = passed[me]
            with eng.Fori(0, LAYERS) as l:
                layer_base[me] = l * STAGES_PER_LAYER
                current["l"] = l
                body(l)
            assert passed[me] == before + STAGES_PER_LAYER
            del layer_base[me]
            current["l"] = None
            passed[me] += (LAYERS - 1) * STAGES_PER_LAYER

        U_ATT, U_REST = 0, 9

        STAGES_BEFORE_SPILL = 15

        def first_units():
            w = t["w_in"][0].rearrange("(p c) n -> p c n", c=KC)

            def w_in(j):
                return w[:, :, j * BANK:(j + 1) * BANK]

            wr = t["w_ret_branch"][0].rearrange("(p c) n -> p c n", c=KC)
            wo = t["w_out"][0].rearrange("(p c) n -> p c n", c=KC)
            us = [w_in(j * GROUPS + g) for g in range(GROUPS) for j in range(3)]
            us += [w_in(j) for j in (9, 10, 11, 12, 13, 14)]
            us += [t["w_attn_branch"][0].rearrange("(p c) n -> p c n", c=4), w_in(15), w_in(16)]
            for n in range(2):
                us += [wr[:, :, n * BANK:(n + 1) * BANK], w_in(17 + n)]
            us += [wo[:, :, n * BANK:(n + 1) * BANK] for n in range(2)]
            return us

        block = ctx.enter_context(nc.Block())

        @block.sync
        def _(sp):
            for i in range(NT):
                sp.dma_start(h[:, i, :], t["x"][0, i * P:(i + 1) * P]).then_inc(x_loaded[i], 16)
            sp.dma_start(rows[:, 0], t["norm_mix_w"].partition_broadcast(P)).then_inc(first_row_loaded, 16)
            sp.dma_start(cst[:, :], const[:, 0:KEPT]).then_inc(consts_loaded, 16)
            for u, src in enumerate(first_units()):
                if u >= 2:
                    sp.wait_ge(unit_used, u - 1)
                sp.dma_start(ring[:, u % 2].rearrange("p (c n) -> p c n", n=src.shape[2]), src).then_inc(unit_loaded[u % 2], 16)
            sp.wait_ge(unit_used, FIRST_UNITS)
            sp.wait_ge(rows_sent, 1)
            experts_sp(sp)
            spill_sp(sp)
            layers_sp(sp)

        @block.tensor
        def _(pe):
            def nxt():
                next_stage(pe, "pe")
            pe.wait_ge(consts_loaded, 16)
            turn_pe(pe, xn, KC, Z.rows_ready, emptied=Z.turned_low)
            nxt()
            for g in range(GROUPS):
                base = U_ATT + 3 * g
                vals = [(base + 2, SHIFTED[i]) for i in range(5)] if g == 0 else [(base + 2, tokens(i, True)) for i in range(NT)]
                heads_pe(pe, [base, base + 1], g > 0, vals)
                nxt()
                attend_pe(pe, dilated(g))
                nxt()
            heads_pe(pe, [9, 10], False, [(11 + n, tokens(i, False)) for n in range(2) for i in range(NT)])
            pe.wait_ge(Z.rows_ready, NT)
            pe.wait_ge(Z.turned_kept, 2 * NT)
            turn_pe(pe, C.o[0][:, :, 0:BANK], 4, bank0=4, before=2 * NT)
            nxt()
            retain_pe(pe)
            nxt()
            jobs_pe(pe, tiles_jobs(U_GATE, M.xT, "act") + tiles_jobs(U_GATE + 1, M.xT, "act"))
            turn_pe(pe, xn, KC, Z.rows_ready, bank0=4, emptied=Z.turned_low)
            nxt()
            jobs_pe(pe, merge_jobs())
            nxt()
            turn_pe(pe, xn, KC, emptied=Z.turned_low)
            pe.wait_ge(Z.turned_low, 2 * NT)
            jobs_pe(pe, tiles_jobs(U_MIXED, M.mT, "dve") + tiles_jobs(U_MIXED + 1, M.mT, "dve"))
            nxt()
            turn_pe(pe, xn, KC, Z.rows_ready)
            nxt()
            route_pe(pe)
            nxt()
            experts_pe(pe)
            nxt()
            spill_pe(pe)
            nxt()
            nxt()

            def layer(l):
                turn_pe(pe, xn, KC, Z.rows_ready, emptied=Z.turned_low)
                nxt()
                project_pe(pe)
                nxt()
                mlstm_pe(pe)
                nxt()
                attend_pe(pe, window)
                nxt()
                turn_pe(pe, xn, KC, emptied=Z.turned_low)
                pe.wait_ge(Z.turned_low, 2 * NT)
                jobs_pe(pe, out_jobs())
                nxt()
                turn_pe(pe, xn, KC, emptied=Z.turned_low)
                nxt()
                up_pe(pe)
                nxt()
                down_pe(pe)
                nxt()
            layer_loop(pe, "pe", layer)

        @block.vector
        def _(v):
            link = Chain(v, Z.dve_chain)

            def nxt():
                next_stage(v, "dve", link)
            norm_dve(v, link, h, rows[:, 0], xn, loaded=x_loaded, row_loaded=first_row_loaded)
            v.wait_ge(Z.rows_ready, NT)
            turn_low_dve(v, xnT_high, h_low_of, in_place=False)
            nxt()
            for g in range(GROUPS):
                heads_dve(v, g > 0)
                nxt()
                attend_dve(v, link, dilated(g))
                nxt()
            heads_dve(v, False)
            combine_dve(v, link)
            nxt()
            retain_dve(v, link)
            nxt()
            v.wait_ge(mixer_rows_loaded, 32)
            gate_dve(v)
            turn_low_dve(v, M.yT[0], low_of(M.yT[1]), bank0=4, in_place=False)
            nxt()
            merge_dve(v)
            nxt()
            turn_low_dve(v, M.mT[0], low_of(M.mT[1]), in_place=False)
            v.wait_ge(Z.more_loaded, 16)
            add_results_dve(v, h)
            nxt()
            v.wait_ge(moe_rows_loaded, 32)
            tile_norms_dve(v, link, h, rows[:, 0], xn)
            nxt()
            route_dve(v, link)
            nxt()
            experts_dve(v)
            nxt()
            spill_dve(v)
            nxt()
            unite_dve(v, link)
            nxt()

            def layer(l):
                tile_norms_dve(v, link, h, rows[:, 0], xn, Z.row0_loaded)
                turn_low_dve(v, xnT_high, xn_low_of)
                nxt()
                project_dve(v, link)
                nxt()
                mlstm_dve(v, link)
                nxt()
                attend_dve(v, link, window)
                window_end_dve(v, link)
                nxt()
                turn_low_dve(v, xnT_high, xn_low_of)
                finish_dve(v, link, kept_rows, rows[:, 1], rows[:, 2], xn)
                nxt()
                turn_low_dve(v, xnT_high, xn_low_of)
                nxt()
                up_dve(v, link)
                nxt()
                finish_dve(v, link, kept_last, rows[:, 3], None, None)
                nxt()
            layer_loop(v, "dve", layer)

        @block.gpsimd
        def _(pool):
            def nxt():
                next_stage(pool, "pool")
            for units in ((), (0, 1, 2), (3,), (4, 5), (6,), (7, 8), (9,), (10, 11, 12)):
                for u in units:
                    low_pool(pool, u)
                nxt()
            retain_pool(pool)
            low_pool(pool, U_GATE)
            nxt()
            for units in ((14, 15), range(16, 23), (23,), ()):
                for u in units:
                    low_pool(pool, u)
                nxt()
            route_pool(pool)
            nxt()
            experts_pool(pool)
            nxt()
            spill_pool(pool)
            nxt()
            nxt()

            def layer(l):
                for units in ((0,), (1, 2, 3, 4), (5,), (6,), (), (7,), range(8, SPLIT), ()):
                    for q in units:
                        low_pool(pool, q)
                    nxt()
            layer_loop(pool, "pool", layer)

        @block.scalar
        def _(a):
            link = Chain(a, Z.act_chain)

            def nxt():
                next_stage(a, "act", link)
            a.wait_ge(consts_loaded, 16)
            norm_act(a)
            a.dma_start(rows[:, 1], t["ret_gn_w"].partition_broadcast(P)).then_inc(mixer_rows_loaded, 16)
            a.dma_start(rows[:, 2:4].rearrange("p a n -> p (a n)"), t["b_branch_gate"].partition_broadcast(P)).then_inc(mixer_rows_loaded, 16)
            turn_act(a, xnT_high, KC)
            nxt()
            for g in range(GROUPS):
                if g == 0:
                    dsts = [L.va[0:SHIFTED[i].stop - SHIFTED[i].start, i, :] for i in range(5)]
                else:
                    dsts = [L.va[:, i, :] for i in range(NT)]
                if g == 0:
                    high_act(a, 0)
                heads_act(a, (DH ** -0.5, 1.0), dsts, {-1: 3 * g + 1, 5: 3 * g + 2})
                high_act(a, 3 * g + 3)
                nxt()
                attend_act(a, dilated(g))
                if g:
                    leave_act(a, g)
                nxt()
            combine_load_act(a)
            heads_act(a, (1.0, DH ** -0.5), [L.vr[:, i, n * BANK:(n + 1) * BANK] for n in range(2) for i in range(NT)],
                      {-1: 10, 5: 11, 8: None, 9: 12})
            turn_act(a, C.yT, 4, bank0=4, before=2 * NT)
            high_act(a, U_GATE)
            nxt()
            retain_act(a)
            nxt()
            gate_act(a)
            turn_act(a, M.yT[0], KC, bank0=4)
            nxt()
            merge_act(a)
            nxt()
            a.dma_start(h[:, :, :], t["x"][0].rearrange("(i p) d -> p i d", p=P)).then_inc(Z.more_loaded, 16)
            a.dma_start(rows[:, 0], t["norm_moe_w"].partition_broadcast(P)).then_inc(moe_rows_loaded, 16)
            a.dma_start(rows[:, 1], t["norm_final_w"].rearrange("(a n) -> a n", a=1).partition_broadcast(P)).then_inc(moe_rows_loaded, 16)
            turn_act(a, M.mT[0], KC)
            high_act(a, U_MIXED + 1)
            nxt()
            load_routes(a)
            a.sem_inc(rows_sent, 1)
            tile_roots_act(a, h, xn)
            a.wait_ge(Z.rows_ready, NT)
            a.dma_start(normed_rows.rearrange("(i p) d -> p i d", p=P), xn[:, :, :]).then_inc(normed_stored, 16)
            turn_act(a, xnT, KC)
            a.wait_ge(Z.more_loaded, 64)
            nxt()
            route_act(a)
            nxt()
            experts_act(a)
            nxt()
            spill_act(a)
            nxt()
            for i in range(NT):
                a.dma_start(chosen_rows[:, i], expert_rows[2 * i * P:2 * (i + 1) * P].rearrange("(p k) d -> p k d", k=2)).then_inc(chosen_loaded[i], 16)
            a.sem_inc(rows_sent, 1)
            tile_roots_act(a, h, xn, ready=Z.tile_added)
            nxt()

            def layer(l):
                a.dma_start(rows[:, 0], layer_row("g_pre_mix_2", l).partition_broadcast(P)).then_inc(Z.row0_loaded, 16)
                high_act(a, 0)
                tile_roots_act(a, h, xn)
                turn_act(a, xnT_high, KC)
                load_layer(a, l)
                a.sem_inc(rows_sent, 1)
                nxt()
                a.wait_ge(layer_loaded, l * 144 + 144)
                project_act(a)
                nxt()
                mlstm_act(a)
                high_act(a, 6)
                nxt()
                attend_act(a, window)
                window_end_act(a)
                nxt()
                turn_act(a, xnT_high, KC)
                finish_act(a, kept_rows, 4, True, then=lambda n: high_act(a, 7) if n == 5 else None)
                nxt()
                turn_act(a, xnT_high, KC)
                nxt()
                high_act(a, 8)
                up_act(a)
                nxt()
                finish_act(a, kept_last, 8, False)
                nxt()
            layer_loop(a, "act", layer)
            a.dma_start(out[0].rearrange("(i p) d -> p i d", p=P), h[:, :, :]).then_inc(out_stored, 16)
            a.wait_ge(out_stored, 16)


def kernel(**inputs):
    import numpy as _np
    import concourse.bacc as _bacc
    from concourse import mybir as _mybir
    from concourse.bass_utils import run_bass_kernel_spmd as _run

    nc, arrays, out = launch_parts(inputs, _bacc, _mybir, _np)
    r = _run(nc, [arrays], core_ids=[0])
    return r.results[0]["out_dram"]


def launch_parts(inputs, _bacc, _mybir, _np):
    nc = _bacc.Bacc("TRN2", target_bir_lowering=False, num_devices=1)
    arrays, t = {}, {}
    for name in INPUTS:
        a = _np.ascontiguousarray(inputs[name])
        arrays[f"in_{name}"] = a
        t[name] = nc.dram_tensor(f"in_{name}", a.shape, _mybir.dt.from_np(a.dtype), kind="ExternalInput").ap()
    for name, frm in (("qk_conv_t", "qk_conv_w_2"), ("ffn_conv_t", "ffn_conv_w_2"), ("qk_bias_t", "qk_conv_b_2")):
        a = _np.asarray(inputs[frm])
        a = a.reshape(a.shape[:-1] + (-1, P))
        a = _np.ascontiguousarray(a.transpose(0, 3, 2, 1) if a.ndim == 4 else a.transpose(0, 2, 1))
        arrays[name] = a
        t[name] = nc.dram_tensor(name, a.shape, _mybir.dt.from_np(a.dtype), kind="ExternalInput").ap()
    arrays["tables"] = tables()
    const = nc.dram_tensor("tables", arrays["tables"].shape, F32, kind="ExternalInput").ap()
    out = nc.dram_tensor("out_dram", (1, S, D), F32, kind="ExternalOutput").ap()
    build(nc, t, const, out)
    return nc, arrays, out
```
